# Optimizing a Trainium2 kernel written in Bass

```python
import jax, jax.numpy as jnp
from jax import lax
import numpy as np

D_MODEL = 1024
BATCH = 1
SEQ = 256
DEPTH = 1

N_META = 16
EPS = 1e-6

SB_HEADS = 8
SB_HEAD_DIM = D_MODEL // 16
SB_WIDTH = SB_HEADS * SB_HEAD_DIM
SB_BLOCK = 128

GLA_HEADS = 4
GLA_DV = D_MODEL // 8
GLA_DK = GLA_DV // 2
GLA_WIDTH = GLA_HEADS * GLA_DV
GLA_KW = GLA_HEADS * GLA_DK
GLA_GATE_RANK = 16
GLA_TAU = 16.0
GLA_CHUNK = 64

MIX_WIDTH = SB_WIDTH + GLA_WIDTH
IN_SPLITS = [SB_WIDTH, SB_WIDTH, SB_WIDTH, GLA_KW, GLA_KW, GLA_WIDTH, GLA_WIDTH, GLA_GATE_RANK]
IN_COLS = sum(IN_SPLITS)

PEER_HEADS = 8
PEER_NKEYS = 128
PEER_TOPK = 16
PEER_QDIM = 128
PEER_HALF = PEER_QDIM // 2
N_EXPERTS = PEER_NKEYS * PEER_NKEYS
PEER_BLOCK = 256


def rmsnorm(x, g):
    xf = x.astype(jnp.float32)
    y = xf * lax.rsqrt(jnp.mean(xf * xf, axis=-1, keepdims=True) + EPS)
    return (y * g.astype(jnp.float32)).astype(x.dtype)

def split_heads(t, n):
    b, l, _ = t.shape
    return t.reshape(b, l, n, -1).transpose(0, 2, 1, 3)

def merge_heads(t):
    b, h, l, d = t.shape
    return t.transpose(0, 2, 1, 3).reshape(b, l, h * d)

def sb_query_block(q_blk, q_pos, k, v):
    L = k.shape[2]
    z = jnp.einsum('bhqd,bhkd->bhqk', q_blk, k).astype(jnp.float32) * (SB_HEAD_DIM ** -0.5)
    mask = jnp.arange(L)[None, :] < q_pos[:, None]
    log_1m = jnp.where(mask, jax.nn.log_sigmoid(-z), 0.0)
    between = lax.cumsum(log_1m, axis=3, reverse=True) - log_1m
    a = jnp.where(mask, jnp.exp(jax.nn.log_sigmoid(z) + between), 0.0)
    return jnp.einsum('bhqk,bhkd->bhqd', a, v.astype(jnp.float32)).astype(v.dtype)

def stick_breaking_attention(q, k, v):
    b, h, L, d = q.shape
    n_real = L - N_META
    o_meta = sb_query_block(q[:, :, :N_META], jnp.arange(N_META), k, v)
    starts = N_META + jnp.arange(n_real // SB_BLOCK) * SB_BLOCK

    def body(start):
        qb = lax.dynamic_slice_in_dim(q, start, SB_BLOCK, axis=2)
        return sb_query_block(qb, start + jnp.arange(SB_BLOCK), k, v)

    o_real = lax.map(body, starts)
    o_real = jnp.moveaxis(o_real, 0, 2).reshape(b, h, n_real, d)
    return jnp.concatenate([o_meta, o_real], axis=2)

def gla_chunk(state, xs):
    q, k, v, lg = xs
    C = q.shape[2]
    bcum = jnp.cumsum(lg, axis=2)
    o_inter = jnp.einsum('bhtd,bhde->bhte', q * jnp.exp(bcum), state)
    causal = (jnp.arange(C)[:, None] >= jnp.arange(C)[None, :])[:, :, None]
    diff = bcum[:, :, :, None, :] - bcum[:, :, None, :, :]
    decay = jnp.where(causal, jnp.exp(jnp.where(causal, diff, 0.0)), 0.0)
    attn = jnp.einsum('bhtd,bhsd,bhtsd->bhts', q, k, decay)
    o = o_inter + jnp.einsum('bhts,bhse->bhte', attn, v)
    b_last = bcum[:, :, -1:, :]
    new_state = jnp.exp(b_last[:, :, 0, :])[..., None] * state + \
        jnp.einsum('bhsd,bhse->bhde', k * jnp.exp(b_last - bcum), v)
    return new_state, o

def gated_linear_attention(q, k, v, lg):
    out_dtype = v.dtype
    q, k, v, lg = (t.astype(jnp.float32) for t in (q, k, v, lg))
    b, h, L, dk = q.shape
    dv = v.shape[-1]
    n_real = L - N_META
    n_chunks = n_real // GLA_CHUNK
    state0 = jnp.zeros((b, h, dk, dv), jnp.float32)
    state, o_meta = gla_chunk(state0, (q[:, :, :N_META], k[:, :, :N_META], v[:, :, :N_META], lg[:, :, :N_META]))

    def to_chunks(t):
        return jnp.moveaxis(t[:, :, N_META:].reshape(b, h, n_chunks, GLA_CHUNK, t.shape[-1]), 2, 0)

    _, o_real = lax.scan(gla_chunk, state, (to_chunks(q), to_chunks(k), to_chunks(v), to_chunks(lg)))
    o_real = jnp.moveaxis(o_real, 0, 2).reshape(b, h, n_real, dv)
    return jnp.concatenate([o_meta, o_real], axis=2).astype(out_dtype)

def hybrid_mixer(hn, w_in, w_gate_up, b_gate_up, sb_norm_g, gla_norm_g, w_out):
    proj = hn @ w_in
    offsets = list(np.cumsum(IN_SPLITS)[:-1])
    sbq, sbk, sbv, gq, gk, gv, gr, glr = jnp.split(proj, offsets, axis=-1)
    sb_o = stick_breaking_attention(split_heads(sbq, SB_HEADS), split_heads(sbk, SB_HEADS),
                                    split_heads(sbv, SB_HEADS))
    sb_o = merge_heads(rmsnorm(sb_o, sb_norm_g.reshape(SB_HEADS, 1, SB_HEAD_DIM)))
    lg = jax.nn.log_sigmoid((glr @ w_gate_up + b_gate_up).astype(jnp.float32)) / GLA_TAU
    gla_o = gated_linear_attention(split_heads(gq, GLA_HEADS) * (GLA_DK ** -0.5),
                                   split_heads(gk, GLA_HEADS), split_heads(gv, GLA_HEADS),
                                   split_heads(lg, GLA_HEADS))
    gla_o = merge_heads(rmsnorm(gla_o, gla_norm_g.reshape(GLA_HEADS, 1, GLA_DV))) * jax.nn.silu(gr)
    return jnp.concatenate([sb_o, gla_o], axis=-1) @ w_out

def peer_ffn(hn, w_peer_q, sub_keys1, sub_keys2, expert_u, expert_v):
    b, L, d = hn.shape
    t = hn.reshape(b * L, d)
    T = t.shape[0]
    q = (t @ w_peer_q).reshape(T, PEER_HEADS, 2, PEER_HALF)
    s1 = jnp.einsum('thd,hkd->thk', q[:, :, 0], sub_keys1).astype(jnp.float32)
    s2 = jnp.einsum('thd,hkd->thk', q[:, :, 1], sub_keys2).astype(jnp.float32)
    v1, i1 = lax.top_k(s1, PEER_TOPK)
    v2, i2 = lax.top_k(s2, PEER_TOPK)
    cand = (v1[..., :, None] + v2[..., None, :]).reshape(T, PEER_HEADS, PEER_TOPK * PEER_TOPK)
    cidx = (i1[..., :, None] * PEER_NKEYS + i2[..., None, :]).reshape(T, PEER_HEADS, PEER_TOPK * PEER_TOPK)
    sc, pos = lax.top_k(cand, PEER_TOPK)
    eidx = jnp.take_along_axis(cidx, pos, axis=-1).reshape(T, PEER_HEADS * PEER_TOPK)
    gates = jax.nn.softmax(sc, axis=-1).reshape(T, PEER_HEADS * PEER_TOPK).astype(hn.dtype)
    n_blocks = -(-T // PEER_BLOCK)
    pad = n_blocks * PEER_BLOCK - T
    tb = jnp.pad(t, ((0, pad), (0, 0))).reshape(n_blocks, PEER_BLOCK, d)
    eb = jnp.pad(eidx, ((0, pad), (0, 0))).reshape(n_blocks, PEER_BLOCK, -1)
    gb = jnp.pad(gates, ((0, pad), (0, 0))).reshape(n_blocks, PEER_BLOCK, -1)

    def block(args):
        xt, e, g = args
        act = jax.nn.gelu(jnp.einsum('nkd,nd->nk', expert_u[e], xt), approximate=False)
        return jnp.einsum('nk,nkd->nd', g * act, expert_v[e])

    y = lax.map(block, (tb, eb, gb)).reshape(n_blocks * PEER_BLOCK, d)[:T]
    return y.reshape(b, L, d)

def first_inputs(seed: int = 0) -> dict:
    key = jax.random.key(seed)
    ks = jax.random.split(key, 20)
    n = jax.random.normal
    f = jnp.float32
    return {
        "x": n(ks[0], (BATCH, SEQ, D_MODEL), f),
        "meta_tokens": n(ks[1], (N_META, D_MODEL), f),
        "norm1_g": 1.0 + 0.02 * n(ks[2], (DEPTH, D_MODEL), f),
        "w_in": n(ks[3], (DEPTH, D_MODEL, IN_COLS), f) * D_MODEL ** -0.5,
        "w_gate_up": n(ks[4], (DEPTH, GLA_GATE_RANK, GLA_KW), f) * GLA_GATE_RANK ** -0.5,
        "b_gate_up": 0.1 * n(ks[5], (DEPTH, GLA_KW), f),
        "sb_norm_g": 1.0 + 0.02 * n(ks[6], (DEPTH, SB_WIDTH), f),
        "gla_norm_g": 1.0 + 0.02 * n(ks[7], (DEPTH, GLA_WIDTH), f),
        "w_out": n(ks[8], (DEPTH, MIX_WIDTH, D_MODEL), f) * MIX_WIDTH ** -0.5,
        "norm2_g": 1.0 + 0.02 * n(ks[9], (DEPTH, D_MODEL), f),
        "w_peer_q": n(ks[10], (DEPTH, D_MODEL, PEER_HEADS * PEER_QDIM), f) * D_MODEL ** -0.5,
        "sub_keys1": n(ks[11], (DEPTH, PEER_HEADS, PEER_NKEYS, PEER_HALF), f) * PEER_HALF ** -0.5,
        "sub_keys2": n(ks[12], (DEPTH, PEER_HEADS, PEER_NKEYS, PEER_HALF), f) * PEER_HALF ** -0.5,
        "expert_u": n(ks[13], (DEPTH, N_EXPERTS, D_MODEL), f) * D_MODEL ** -0.5,
        "expert_v": n(ks[14], (DEPTH, N_EXPERTS, D_MODEL), f) * PEER_HEADS ** -0.5,
        "norm_f_g": 1.0 + 0.02 * n(ks[15], (D_MODEL,), f),
    }

def first_block(x, meta_tokens, norm1_g, w_in, w_gate_up, b_gate_up, sb_norm_g, gla_norm_g, w_out,
              norm2_g, w_peer_q, sub_keys1, sub_keys2, expert_u, expert_v, norm_f_g):
    b = x.shape[0]
    meta = jnp.broadcast_to(meta_tokens.astype(x.dtype)[None], (b, N_META, x.shape[-1]))
    h = jnp.concatenate([meta, x], axis=1)
    for l in range(DEPTH):
        h = h + hybrid_mixer(rmsnorm(h, norm1_g[l]), w_in[l], w_gate_up[l], b_gate_up[l],
                             sb_norm_g[l], gla_norm_g[l], w_out[l])
        h = h + peer_ffn(rmsnorm(h, norm2_g[l]), w_peer_q[l], sub_keys1[l], sub_keys2[l],
                         expert_u[l], expert_v[l])
    return rmsnorm(h, norm_f_g)[:, N_META:]


N_HEADS = 8
HEAD_DIM = 128
ATTN_WIDTH = N_HEADS * HEAD_DIM
N_IDX_HEADS = 8
IDX_DIM = 64
TOPK_MAX = 256
CONV_WIDTH = D_MODEL
CONV_K = 3
D_FF = ((8 * D_MODEL // 3 + 255) // 256) * 256
Q_BLOCK = 128
IDX_SCALE = (N_IDX_HEADS ** -0.5) * (IDX_DIM ** -0.5)

_PROJ_SIZES = [ATTN_WIDTH, ATTN_WIDTH, ATTN_WIDTH,
               N_IDX_HEADS * IDX_DIM, IDX_DIM, N_IDX_HEADS,
               CONV_WIDTH, CONV_WIDTH, CONV_WIDTH,
               D_MODEL, D_MODEL]
PROJ_WIDTH = int(sum(_PROJ_SIZES))
PROJ_SPLITS = [int(s) for s in np.cumsum(_PROJ_SIZES)[:-1]]


def rmsnorm_2(x, g):
    xf = x.astype(jnp.float32)
    y = xf * lax.rsqrt(jnp.mean(xf * xf, axis=-1, keepdims=True) + EPS)
    return (y * g.astype(jnp.float32)).astype(x.dtype)

def dsa_attention(q, k, v, q_idx, k_idx, w_idx):
    b, l = q.shape[0], q.shape[1]
    topk = min(TOPK_MAX, l // 4)
    n_blk = -(-l // Q_BLOCK)
    lp = n_blk * Q_BLOCK

    def pad(a):
        return jnp.pad(a, [(0, 0), (0, lp - l)] + [(0, 0)] * (a.ndim - 2))

    q, k, v, q_idx, k_idx, w_idx = (pad(a) for a in (q, k, v, q_idx, k_idx, w_idx))
    key_pos = jnp.arange(lp)

    def to_blocks(a):
        return jnp.moveaxis(a.reshape((b, n_blk, Q_BLOCK) + a.shape[2:]), 1, 0)

    def one_block(args):
        q_b, qi_b, w_b, start = args
        q_pos = start + jnp.arange(Q_BLOCK)
        visible = key_pos[None, :] <= q_pos[:, None]
        rel = jax.nn.relu(jnp.einsum('bthd,bsd->bths', qi_b, k_idx).astype(jnp.float32))
        score = jnp.einsum('bths,bth->bts', rel, w_b.astype(jnp.float32) * IDX_SCALE)
        score = jnp.where(visible[None], score, -jnp.inf)
        _, sel = lax.top_k(score, topk)
        k_sel = jax.vmap(lambda kb, ib: kb[ib])(k, sel)
        v_sel = jax.vmap(lambda vb, ib: vb[ib])(v, sel)
        valid = sel <= q_pos[None, :, None]
        logits = jnp.einsum('bthd,btkhd->bthk', q_b, k_sel).astype(jnp.float32) * (HEAD_DIM ** -0.5)
        logits = jnp.where(valid[:, :, None, :], logits, -jnp.inf)
        p = jax.nn.softmax(logits, axis=-1).astype(v_sel.dtype)
        return jnp.einsum('bthk,btkhd->bthd', p, v_sel)

    starts = jnp.arange(n_blk) * Q_BLOCK
    out = lax.map(one_block, (to_blocks(q), to_blocks(q_idx), to_blocks(w_idx), starts))
    out = jnp.moveaxis(out, 0, 1).reshape(b, lp, N_HEADS, HEAD_DIM)
    return out[:, :l]

def short_conv(u, w):
    return lax.conv_general_dilated(
        u, w[:, None, :].astype(u.dtype), window_strides=(1,), padding=[(CONV_K - 1, 0)],
        dimension_numbers=('NWC', 'WIO', 'NWC'), feature_group_count=u.shape[-1])

def second_inputs(seed: int = 0) -> dict:
    key = jax.random.key(seed)
    ks = jax.random.split(key, 16)
    f32 = jnp.float32
    nrm = lambda k, shape, scale: (jax.random.normal(k, shape, f32) * scale)
    gain = lambda k: 1.0 + 0.02 * jax.random.normal(k, (DEPTH, D_MODEL), f32)
    return {
        "x": nrm(ks[0], (BATCH, SEQ, D_MODEL), 1.0),
        "meta_tokens": nrm(ks[1], (N_META, D_MODEL), 1.0),
        "norm_mix_g": gain(ks[2]),
        "w_in": nrm(ks[3], (DEPTH, D_MODEL, PROJ_WIDTH), D_MODEL ** -0.5),
        "w_attn_out": nrm(ks[4], (DEPTH, ATTN_WIDTH, D_MODEL), ATTN_WIDTH ** -0.5),
        "conv_w": nrm(ks[5], (DEPTH, CONV_K, CONV_WIDTH), CONV_K ** -0.5),
        "w_conv_out": nrm(ks[6], (DEPTH, CONV_WIDTH, D_MODEL), CONV_WIDTH ** -0.5),
        "w_out": nrm(ks[7], (DEPTH, D_MODEL, D_MODEL), D_MODEL ** -0.5),
        "norm_ffn_g": gain(ks[8]),
        "w_gate": nrm(ks[9], (DEPTH, D_MODEL, D_FF), D_MODEL ** -0.5),
        "w_up": nrm(ks[10], (DEPTH, D_MODEL, D_FF), D_MODEL ** -0.5),
        "w_down": nrm(ks[11], (DEPTH, D_FF, D_MODEL), D_FF ** -0.5),
        "norm_final_g": 1.0 + 0.02 * jax.random.normal(ks[12], (D_MODEL,), f32),
    }

def second_block(x, meta_tokens, norm_mix_g, w_in, w_attn_out, conv_w, w_conv_out, w_out,
              norm_ffn_g, w_gate, w_up, w_down, norm_final_g):
    b = x.shape[0]
    meta = jnp.broadcast_to(meta_tokens[None].astype(x.dtype), (b, N_META, x.shape[-1]))
    h = jnp.concatenate([meta, x], axis=1)
    l = h.shape[1]
    for i in range(DEPTH):
        a = rmsnorm_2(h, norm_mix_g[i])
        proj = a @ w_in[i]
        q, k, v, qi, ki, wi, cu, cb, cc, ga, gb = jnp.split(proj, PROJ_SPLITS, axis=-1)
        y_attn = dsa_attention(q.reshape(b, l, N_HEADS, HEAD_DIM),
                               k.reshape(b, l, N_HEADS, HEAD_DIM),
                               v.reshape(b, l, N_HEADS, HEAD_DIM),
                               qi.reshape(b, l, N_IDX_HEADS, IDX_DIM), ki, wi)
        y_attn = y_attn.reshape(b, l, ATTN_WIDTH) @ w_attn_out[i]
        y_conv = (cb * short_conv(cc * cu, conv_w[i])) @ w_conv_out[i]
        mixed = jax.nn.sigmoid(ga) * y_attn + jax.nn.sigmoid(gb) * y_conv
        h = h + mixed @ w_out[i]
        f = rmsnorm_2(h, norm_ffn_g[i])
        h = h + (jax.nn.silu(f @ w_gate[i]) * (f @ w_up[i])) @ w_down[i]
    out = rmsnorm_2(h, norm_final_g)
    return out[:, N_META:]


def setup_inputs(seed=0):
    out = dict(first_inputs(seed))
    for name, value in second_inputs(seed + 1).items():
        if name != "x":
            out[name + "_2"] = value
    return out


def reference(
    x, meta_tokens, norm1_g, w_in, w_gate_up, b_gate_up, sb_norm_g, gla_norm_g, w_out, norm2_g,
    w_peer_q, sub_keys1, sub_keys2, expert_u, expert_v, norm_f_g, meta_tokens_2, norm_mix_g_2,
    w_in_2, w_attn_out_2, conv_w_2, w_conv_out_2, w_out_2, norm_ffn_g_2, w_gate_2, w_up_2,
    w_down_2, norm_final_g_2,
):
    x = first_block(
        x, meta_tokens, norm1_g, w_in, w_gate_up, b_gate_up, sb_norm_g, gla_norm_g, w_out,
        norm2_g, w_peer_q, sub_keys1, sub_keys2, expert_u, expert_v, norm_f_g,
    )
    return second_block(
        x, meta_tokens_2, norm_mix_g_2, w_in_2, w_attn_out_2, conv_w_2, w_conv_out_2, w_out_2,
        norm_ffn_g_2, w_gate_2, w_up_2, w_down_2, norm_final_g_2,
    )


_drawn_inputs = setup_inputs


def setup_inputs(seed=0):
    import zlib

    import numpy as np

    out = dict(_drawn_inputs(seed))
    spreads = {}
    factors = {'norm_ffn_g_2': 4.068, 'norm_final_g_2': 2.824}
    for name, (base, spread) in spreads.items():
        noise = np.random.default_rng([zlib.crc32(name.encode()), seed]).standard_normal(out[name].shape)
        drawn = base * np.exp(spread * noise) if base else spread * noise
        out[name] = __import__('jax').numpy.asarray(drawn.astype(out[name].dtype))
    for name, factor in factors.items():
        out[name] = (out[name] * factor).astype(out[name].dtype)
    return out
```

```python
from contextlib import ExitStack

import numpy as np

import concourse.bass as bass
from concourse import mybir

F32 = mybir.dt.float32
U32 = mybir.dt.uint32
ALU = mybir.AluOpType
ACT = mybir.ActivationFunctionType
AX = mybir.AxisListType

P = 128
D = 1024
C = D // P
META = 16
REAL = 256
T = META + REAL
EPS = 1e-6

SB_HEADS, SB_DIM = 8, 64
GLA_HEADS, GLA_DK, GLA_DV = 4, 64, 128
GLA_RANK, GLA_TAU = 16, 16.0
SUB = 16
SUBS = REAL // SUB
CLAMP = 40.0

PH, NKEYS, TOPK = 8, 128, 16
SLOTS = PH * TOPK
GROUP = 8
HALF_KEYS = NKEYS // 2

HEADS, HEAD_DIM = 8, 128
IDX_HEADS, IDX_DIM = 8, 64
KEEP = min(256, T // 4)
IDX_SCALE = (IDX_HEADS ** -0.5) * (IDX_DIM ** -0.5)
CONV_K = 3
D_FF = ((8 * D // 3 + 255) // 256) * 256
FF = D_FF // P

NEG = -(2.0 ** 100)
TAKEN = -(2.0 ** 127)

COLS = 256
BLOCK = 2048
RING = 4


def stages():
    counts = [("w_in_features", 8), ("w_in_values", 4), ("w_out", 4), ("w_peer_q", 4),
              ("expert_u", NKEYS // 2), ("expert_v", NKEYS // 2), ("w_in_2_features", 30),
              ("w_in_2_values", 4), ("w_conv_out_2", 4), ("w_attn_out_2", 4), ("w_out_2", 4),
              ("w_gate_up_2", 2 * D_FF // COLS), ("w_down_2", D_FF // COLS)]
    first, at = {}, 0
    for name, n in counts:
        first[name] = at
        at += n
    return first, dict(counts), at


FIRST, COUNT, BLOCKS = stages()

SMALL = {}
_at = 0
for _name, _n in (("glr", C * GLA_RANK), ("kiwi", C * (2 * IDX_DIM + IDX_HEADS)), ("keys", PH * NKEYS),
                  ("meta_2", C * META), ("gate_up", GLA_HEADS * GLA_DK), ("norm1", C), ("norm2", C),
                  ("norm_f", C), ("norm_mix", C), ("norm_ffn", C), ("norm_final", C), ("sb_norm", 4),
                  ("gla_norm", 4), ("b_gate", 2), ("conv", CONV_K * C)):
    SMALL[_name] = (_at, _n)
    _at += _n
SMALL_COLS = _at

TILE0 = {}
_at = 0
for _name, _n in (("w_in_features", 16), ("w_in_values", 12), ("w_out", 8), ("w_peer_q", 8),
                  ("expert_u", NKEYS), ("w_in_2_features", 60), ("w_in_2_values", 12),
                  ("w_conv_out_2", 8), ("w_attn_out_2", 8), ("w_out_2", 8), ("w_gate_up_2", 2 * FF)):
    TILE0[_name] = _at
    _at += _n
BANKS = 4


def build(nc, stream, small_dram, x_dram, out_dram):
    with ExitStack() as ctx:
        def sb(name, shape, dt=F32):
            return ctx.enter_context(nc.sbuf_tensor(name, shape, dt))

        def sem(name):
            return ctx.enter_context(nc.semaphore(name))

        ps = ctx.enter_context(nc.psum_tensor("ps", [P, 8, 512], F32))

        work = sb("work", [P, NKEYS * REAL])
        ring = sb("ring", [P, RING, BLOCK])
        res = sb("res", [P, C, T])
        xn = sb("xn", [P, C * T])
        small = sb("small", [P, SMALL_COLS])
        ones = sb("ones", [P, T])
        zeros = sb("zeros", [P, P])
        ident = sb("ident", [P, P])
        iota = sb("iota", [P, NKEYS])
        onehot1 = sb("onehot1", [P, 2, GROUP, HALF_KEYS])
        onehot2 = sb("onehot2", [P, 2, GROUP, NKEYS])
        slots = sb("slots", [P, 3, REAL])
        var = sb("var", [P, T])
        rstd = sb("rstd", [P, T])

        xn_all = xn[:, :].rearrange("p (c t) -> p c t", c=C)
        xn_real = xn[:, 0:C * REAL].rearrange("p (c t) -> p c t", c=C)

        def view(name, **kw):
            at, n = SMALL[name]
            return small[:, at:at + n]

        glr_w = view("glr").rearrange("p (c n) -> p c n", c=C)
        kiwi_w = view("kiwi").rearrange("p (c n) -> p c n", c=C)
        keys_w = view("keys").rearrange("p (h k) -> p h k", h=PH)
        meta_2 = view("meta_2").rearrange("p (c t) -> p c t", c=C)
        gate_up_w = view("gate_up")
        conv_w = view("conv").rearrange("p (k c) -> p k c", k=CONV_K)

        def carve(sizes):
            at, parts = 0, {}
            for name, n in sizes:
                parts[name] = work[:, at:at + n]
                at += n
            assert at <= NKEYS * REAL, at
            return parts

        W = 3 * P
        one = carve([("feat", 16 * T), ("xm", C * P), ("vtok", 3 * D), ("kbd", 4 * P), ("vbd", 512),
                     ("tri", P), ("bdtri", P), ("win", 2 * P), ("blk64", P), ("hide", W), ("keep", W),
                     ("bdm", 512), ("zm", 9 * W), ("soft", 2 * W), ("sp", 2 * W), ("glrT", T),
                     ("gx", 2 * T), ("gl", 2 * T), ("b", 2 * T), ("nb", 2 * T), ("dq", 2 * REAL),
                     ("qt", 2 * REAL), ("ke", 2 * T), ("kt", 2 * T), ("A", 4 * W), ("A0", 4 * REAL),
                     ("sqh", D), ("rh", D), ("mix", C * REAL), ("sil", 4 * REAL), ("sq", C * T)])
        feat = one["feat"].rearrange("p (n t) -> p n t", n=16)
        xm = one["xm"].rearrange("p (c t) -> p c t", c=C)
        vtok = one["vtok"].rearrange("p (k n) -> p k n", k=3)
        kbd = one["kbd"].rearrange("p (n t) -> p n t", n=4)
        zm = one["zm"].rearrange("p (h n) -> p h n", h=9)
        soft = one["soft"].rearrange("p (h n) -> p h n", h=2)
        sp_ = one["sp"].rearrange("p (h n) -> p h n", h=2)
        gx = one["gx"].rearrange("p (j t) -> p j t", j=2)
        gl = one["gl"].rearrange("p (j t) -> p j t", j=2)
        bcum = one["b"].rearrange("p (j t) -> p j t", j=2)
        nb = one["nb"].rearrange("p (j t) -> p j t", j=2)
        dq = one["dq"].rearrange("p (j t) -> p j t", j=2)
        qt = one["qt"].rearrange("p (j t) -> p j t", j=2)
        ke = one["ke"].rearrange("p (j t) -> p j t", j=2)
        kt = one["kt"].rearrange("p (j t) -> p j t", j=2)
        A = one["A"].rearrange("p (h n) -> p h n", h=4)
        A0 = one["A0"].rearrange("p (h n) -> p h n", h=4)
        mix = one["mix"].rearrange("p (c t) -> p c t", c=C)
        sil = one["sil"].rearrange("p (c t) -> p c t", c=4)
        sq1 = one["sq"]

        act_store = work[:, :].rearrange("p (i t) -> p i t", i=NKEYS)
        base = HALF_KEYS * REAL
        route = {}
        for name, n in (("qp", PH * REAL), ("sc", 16 * 256), ("tv", 256), ("pos", 256), ("ix", 512),
                        ("af", 256), ("bf", 256), ("eq", 2048), ("i1", 256), ("i2", 256), ("gate", 256),
                        ("sum", 16), ("rsum", 16), ("v", 32), ("cand", 256), ("ixf", 512),
                        ("pi", 256)):
            route[name] = work[:, base:base + n]
            base += n
        assert base <= NKEYS * REAL
        qp = route["qp"].rearrange("p (h t) -> p h t", h=PH)
        sc = route["sc"].rearrange("p (c n) -> p c n", c=16)

        two = carve([("feat2", 60 * T), ("v2", 3 * D), ("kidup", T), ("wi", 16), ("score", 2 * T),
                     ("rel", 2 * T), ("selb", 2 * T), ("top8", 16), ("vis", 144), ("lm", 2 * T), ("pr", 2 * T),
                     ("stat", 4 * 16), ("pT", 2 * W), ("ya", C * REAL), ("yc", C * REAL),
                     ("yco", C * REAL), ("tmp", 2 * REAL)])
        feat2 = two["feat2"].rearrange("p (n t) -> p n t", n=60)
        v2 = two["v2"].rearrange("p (k n) -> p k n", k=3)
        score = two["score"].rearrange("p (t n) -> p t n", t=2)
        rel = two["rel"].rearrange("p (t n) -> p t n", t=2)
        selb = two["selb"].rearrange("p (t n) -> p t n", t=2)
        lm = two["lm"].rearrange("p (t n) -> p t n", t=2)
        pr = two["pr"].rearrange("p (t n) -> p t n", t=2)
        pT = two["pT"].rearrange("p (t n) -> p t n", t=2)
        ya = two["ya"].rearrange("p (c t) -> p c t", c=C)
        yc = two["yc"].rearrange("p (c t) -> p c t", c=C)
        yco = two["yco"].rearrange("p (c t) -> p c t", c=C)
        KF, CU, CC, QF, CB, GA, GB, QI = range(0, 64, 8)
        ffa = carve([("ffa", FF * REAL), ("sg", 2 * REAL), ("outT", C * REAL)])
        hidden = ffa["ffa"].rearrange("p (n t) -> p n t", n=FF)
        sg = ffa["sg"].rearrange("p (n t) -> p n t", n=2)
        outT = ffa["outT"].rearrange("p (c t) -> p c t", c=C)
        sq_late = work[:, NKEYS * REAL - C * T:]

        landed = [sem(f"landed{i}") for i in range(RING)]
        block_begun = sem("block_begun")
        x_landed, small_landed, stored = sem("x_landed"), sem("small_landed"), sem("stored")
        zeroed, consts = sem("zeroed"), sem("consts")
        vec_step, act_step, pool_step = sem("vec_step"), sem("act_step"), sem("pool_step")
        tile_ready = sem("tile_ready")
        tile_taken = [sem(f"tile_taken{i}") for i in range(BANKS)]
        squares_ready, sum_ready, var_ready, root_ready, normed = (
            sem(n) for n in ("squares_ready", "sum_ready", "var_ready", "root_ready", "normed"))
        meta_spread, glr_ready, glr_taken, gate_logits_ready, gate_biased, gate_soft, decay_ready = (
            sem(n) for n in ("meta_spread", "glr_ready", "glr_taken", "gate_logits_ready", "gate_biased",
                             "gate_soft", "decay_ready"))
        kbd_ready, z0_ready, z_ready, z_taken, soft_ready, sp_ready, s_ready, d_ready, a_ready = (
            sem(n) for n in ("kbd_ready", "z0_ready", "z_ready", "z_taken", "soft_ready", "sp_ready",
                             "s_ready", "d_ready", "a_ready"))
        vbd_ready, sb_out_ready, sb_mixed, pe_used_sp = (
            sem(n) for n in ("vbd_ready", "sb_out_ready", "sb_mixed", "pe_used_sp"))
        head_sq, head_sum, head_var, head_root = (
            sem(n) for n in ("head_sq", "head_sum", "head_var", "head_root"))
        q_exp_in, q_exp, q_decayed, k_exp_in, k_exp, k_decayed, k_used = (
            sem(n) for n in ("q_exp_in", "q_exp", "q_decayed", "k_exp_in", "k_exp", "k_decayed", "k_used"))
        gla_masked, gla_meta_taken, gla_out_ready, silu_ready, gla_mixed = (
            sem(n) for n in ("gla_masked", "gla_meta_taken", "gla_out_ready", "silu_ready", "gla_mixed"))
        residual = sem("residual")
        key_scores_ready, key_scores_taken, tops_shifted, tops_exp, routed, slots_ready, slots_taken = (
            sem(n) for n in ("key_scores_ready", "key_scores_taken", "tops_shifted", "tops_exp", "routed",
                             "slots_ready", "slots_taken"))
        onehots_ready, gates_ready, gates_applied, y_ready = (
            sem(n) for n in ("onehots_ready", "gates_ready", "gates_applied", "y_ready"))
        kiwi_ready, kiwi_taken, idx_ready, idx_taken, selected = (
            sem(n) for n in ("kiwi_ready", "kiwi_taken", "idx_ready", "idx_taken", "selected"))
        logits_ready, masked_ready, probs_ready, probs_scaled, probs_turned, turned_taken = (
            sem(n) for n in ("logits_ready", "masked_ready", "probs_ready", "probs_scaled",
                             "probs_turned", "turned_taken"))
        attn_ready, attn_taken, conv_ready, sigmoid_ready, conv_gated, mixed_ready = (
            sem(n) for n in ("attn_ready", "attn_taken", "conv_ready", "sigmoid_ready", "conv_gated",
                             "mixed_ready"))
        vis_ready = sem("vis_ready")

        def block_landed(eng, b, slot, turn=0):
            eng.wait_ge(landed[slot], turn * 16 + 16 * (b // RING + 1))

        def bank_is_free(eng, g, turn=None):
            if turn is not None:
                eng.wait_ge(tile_taken[g % BANKS], turn + g // BANKS)
            elif g >= BANKS:
                eng.wait_ge(tile_taken[g % BANKS], g // BANKS)

        def tiles_are_taken(eng, g):
            for bank in range(BANKS):
                eng.wait_ge(tile_taken[bank], (g - bank + BANKS - 1) // BANKS)

        def bank_of(g):
            return ps[:, g % BANKS, :]

        def ring_cols(slot):
            return ring[:, slot, :].rearrange("p (c n) -> p c n", c=C)

        def ring_rows(slot):
            return ring[:, slot, :].rearrange("p (c n) -> p c n", c=2)

        block = ctx.enter_context(nc.Block())

        @block.sync
        def _(sp):
            sp.dma_start(res[:, :, :].rearrange("p c t -> p (c t)"), x_dram).then_inc(x_landed, 16)
            sp.dma_start(small[:, :], small_dram).then_inc(small_landed, 16)
            for b in range(RING):
                sp.dma_start(ring[:, b, :], stream[b]).then_inc(landed[b], 16)
            with sp.Fori(1, BLOCKS // RING) as i:
                for k in range(RING):
                    sp.wait_ge(block_begun, i * RING + (k + 2 - RING))
                    sp.dma_start(ring[:, k, :], stream[i * RING + k]).then_inc(landed[k], 16)
            for b in range(BLOCKS // RING * RING, BLOCKS):
                sp.wait_ge(block_begun, b + 2 - RING)
                sp.dma_start(ring[:, b % RING, :], stream[b]).then_inc(landed[b % RING], 16)
            sp.wait_ge(normed, 6)
            sp.dma_start(out_dram, outT.rearrange("p c t -> p (c t)")).then_inc(stored, 16)
            sp.wait_ge(stored, 16)

        @block.gpsimd
        def _(pool):
            g = nc.gpsimd
            for tile, value in ((ones[:, :], 1.0), (zeros[:, :], 0.0), (ident[:, :], 0.0),
                                (one["tri"], 1.0), (one["bdtri"], 1.0), (one["win"], 0.0),
                                (one["blk64"], 1.0), (one["hide"], 0.0), (one["keep"], 1.0),
                                (one["bdm"], 1.0), (one["kbd"], 0.0)):
                g.memset(tile, value).then_inc(zeroed, 1)
            pool.wait_ge(zeroed, 11)
            g.iota(iota[:, :], [[1, NKEYS]], base=0, channel_multiplier=0,
                   allow_small_or_imprecise_dtypes=True).then_inc(consts, 1)
            g.affine_select(out=ident[:, :], in_=ident[:, :], compare_op=ALU.not_equal, fill=1.0, base=0,
                            pattern=[[-1, P]], channel_multiplier=1).then_inc(consts, 1)
            g.affine_select(out=one["tri"], in_=one["tri"], compare_op=ALU.is_ge, fill=0.0, base=0,
                            pattern=[[-1, P]], channel_multiplier=1).then_inc(consts, 1)
            g.memset(one["win"][:, P - META:P], 1.0).then_inc(consts, 1)
            for name, fill, off in (("keep", 0.0, 0), ("hide", NEG, -1)):
                for at, n in ((0, 2 * P), (2 * P, P)):
                    v = one[name][:, at:at + n]
                    g.affine_select(out=v, in_=v, compare_op=ALU.is_ge, fill=fill, base=off,
                                    pattern=[[1, n]], channel_multiplier=-1).then_inc(consts, 1)
            for n, (name, groups, size, inner) in enumerate((("bdtri", 8, META, META), ("blk64", 2, 64, 64),
                                                             ("bdm", 8, META, 64))):
                v = one[name].rearrange("p (g n) -> p g n", g=groups)
                g.affine_select(out=v, in_=v, compare_op=ALU.is_ge, fill=0.0, base=size - 1,
                                pattern=[[size, groups], [0, inner]],
                                channel_multiplier=-1).then_inc(pool_step, 1)
                pool.wait_ge(pool_step, n + 1)
                g.affine_select(out=v, in_=v, compare_op=ALU.is_ge, fill=0.0, base=0,
                                pattern=[[-size, groups], [-1 if name == "bdtri" else 0, inner]],
                                channel_multiplier=1).then_inc(consts, 1)
            pool.wait_ge(y_ready, 1)
            g.memset(two["vis"], 0.0).then_inc(pool_step, 1)
            pool.wait_ge(pool_step, 4)
            g.affine_select(out=two["vis"], in_=two["vis"], compare_op=ALU.is_ge, fill=NEG, base=META,
                            pattern=[[-1, META + P]], channel_multiplier=1).then_inc(vis_ready, 1)
            pool.wait_ge(sigmoid_ready, 1)
            tiles_are_taken(pool, TILE0["w_conv_out_2"] + 8)
            g.tensor_tensor(yco, yco, feat2[:, GB:GB + 8, META:], ALU.mult).then_inc(conv_gated, 1)

        CONSTS = 11

        @block.tensor
        def _(pe):
            mm = nc.tensor.matmul

            def norm(k, sq, tokens):
                pe.wait_ge(squares_ready, k + 1)
                for c in range(C):
                    last = mm(ps[:, 7, 0:tokens], ones[:, 0:P], sq[:, c, :], start=c == 0, stop=c == C - 1)
                last.then_inc(sum_ready, 1)

            def column_block(b, g, slot, rhs, tokens, turn=0, tile_turn=None):
                block_landed(pe, b, slot, turn)
                w = ring_cols(slot)
                for j in range(2):
                    bank_is_free(pe, g + j, tile_turn)
                    for c in range(C):
                        last = mm(bank_of(g + j)[:, 0:tokens], w[:, c, j * P:(j + 1) * P], rhs[:, c, :],
                                  start=c == 0, stop=c == C - 1)
                        if j == c == 0:
                            last.then_inc(block_begun, 1)
                    last.then_inc(tile_ready, 1)

            def columns(name, rhs, tokens, n=None):
                b0, g0 = FIRST[name], TILE0[name]
                n = COUNT[name] if n is None else n
                looped = n // RING if n > 2 * RING else 0
                if looped:
                    with pe.Fori(0, looped) as i:
                        for k in range(RING):
                            column_block(b0 + k, g0 + 2 * k, (b0 + k) % RING, rhs, tokens, i, i * 2)
                for k in range(looped * RING, n):
                    column_block(b0 + k, g0 + 2 * k, (b0 + k) % RING, rhs, tokens)

            def value_blocks(name, meta, meta_rows):
                for k in range(COUNT[name]):
                    b, g = FIRST[name] + k, TILE0[name] + 3 * k
                    block_landed(pe, b, b % RING)
                    w = ring_cols(b % RING)
                    for j in range(3):
                        rows = meta_rows if j == 0 else P
                        lhs = meta if j == 0 else xn_all[:, :, META + (j - 1) * P:META + j * P]
                        bank_is_free(pe, g + j)
                        for c in range(C):
                            last = mm(bank_of(g + j)[0:rows, 0:COLS], lhs[:, c, :], w[:, c, :],
                                      start=c == 0, stop=c == C - 1)
                            if j == c == 0:
                                last.then_inc(block_begun, 1)
                        last.then_inc(tile_ready, 1)

            pe.wait_ge(zeroed, 11)
            pe.wait_ge(consts, CONSTS)
            norm(0, sq1.rearrange("p (c t) -> p c t", c=C), T)
            pe.wait_ge(normed, 1)
            pe.wait_ge(small_landed, 16)
            for c in range(C):
                last = mm(ps[0:GLA_RANK, 6, 0:T], glr_w[:, c, :], xn_all[:, c, :], start=c == 0,
                          stop=c == C - 1)
            last.then_inc(glr_ready, 1)
            columns("w_in_features", xn_all, T)
            pe.wait_ge(glr_taken, 1)
            for j in range(2):
                last = mm(ps[:, 4 + j, 0:T], gate_up_w[0:GLA_RANK, j * P:(j + 1) * P],
                          one["glrT"][0:GLA_RANK, :], start=True, stop=True)
            last.then_inc(gate_logits_ready, 1)
            pe.wait_ge(meta_spread, 1)
            value_blocks("w_in_values", xm, P)
            tiles_are_taken(pe, TILE0["w_out"])

            pe.wait_ge(kbd_ready, 1)
            pe.wait_ge(gate_biased, 2)
            for p in range(4):
                last = mm(ps[:, 4, 0:REAL], kbd[:, p, :], feat[:, p, META:], start=p == 0, stop=p == 3)
            last.then_inc(z0_ready, 1)

            def head_scores(h):
                rows = slice(64 * (h % 2), 64 * (h % 2) + 64)
                q, k = feat[rows, h // 2, :], feat[rows, 4 + h // 2, :]
                if h >= 2:
                    pe.wait_ge(z_taken, h - 1)
                z = ps[:, 5 + h % 2, :]
                mm(z[:, 0:2 * P], k[:, META:META + P], q[:, META:], start=True, stop=True)
                mm(z[:, 2 * P:W], k[:, META + P:], q[:, META + P:], start=True,
                   stop=True).then_inc(z_ready, 1)

            def suffix_sums(h):
                pe.wait_ge(sp_ready, h + 1)
                if h < 8:
                    if h >= 2:
                        pe.wait_ge(d_ready, h - 1)
                    bank = ps[:, 7 if h % 2 else 0, :]
                    s = sp_[:, h % 2, :]
                    mm(bank[:, 0:W], one["tri"], s, start=True, stop=True)
                    mm(bank[:, P:2 * P], ones[:, 0:P], s[:, 2 * P:W], start=False, stop=True,
                       skip_group_check=True).then_inc(s_ready, 1)
                    at = P - META - META * h
                    mm(ps[:, 1, 0:2 * P], one["win"][:, at:at + P], s[:, 0:2 * P], start=h == 0, stop=False)
                    mm(ps[:, 1, P:2 * P], one["win"][:, at:at + P], s[:, 2 * P:W], start=False,
                       stop=False).then_inc(pe_used_sp, 1)
                else:
                    mm(ps[:, 1, 0:2 * P], one["bdtri"], sp_[:, 0, 0:2 * P], start=False,
                       stop=True).then_inc(s_ready, 1)

            head_scores(0)
            for h in range(8):
                if h < 7:
                    head_scores(h + 1)
                suffix_sums(h)
            suffix_sums(8)
            pe.wait_ge(a_ready, 9)
            pe.wait_ge(vbd_ready, 1)
            for h in range(8):
                o = ps[64 * (h % 2):64 * (h % 2) + 64, 2 + h // 4, 256 * (h // 2 % 2):256 * (h // 2 % 2) + 256]
                cols = slice(64 * h, 64 * h + 64)
                mm(o, vtok[:, 1, cols], zm[:, h, 0:2 * P], start=True, stop=False)
                mm(o[:, P:2 * P], vtok[:, 2, cols], zm[:, h, 2 * P:W], start=False, stop=False)
                last = mm(o, one["vbd"][:, cols], zm[:, 8, 0:2 * P], start=False, stop=True)
            last.then_inc(sb_out_ready, 1)
            pe.wait_ge(head_sq, 1)
            for j in range(2):
                last = mm(ps[:, 4 + j, :], one["blk64"], one["sqh"][:, 512 * j:512 * j + 512],
                          start=True, stop=True)
            last.then_inc(head_sum, 1)

            pe.wait_ge(q_decayed, 1)
            pe.wait_ge(sb_mixed, 1)
            for i in range(SUBS):
                for j in range(2):
                    n = 2 * i + j
                    pe.wait_ge(k_decayed, n + 1)
                    for e in range(2):
                        h = 2 * j + e
                        rows = slice(64 * e, 64 * e + 64)
                        q = qt[rows, j, SUB * i:SUB * i + SUB]
                        at = 256 * j + SUB * i
                        mm(ps[:, 4 + h, SUB * i:SUB * i + SUB], kt[rows, j, META:META + P], q,
                           start=True, stop=True)
                        last = mm(ps[0:META, e, at:at + SUB], kt[rows, j, 0:META], q, start=True, stop=True)
                        if i >= SUBS // 2:
                            last = mm(ps[:, 4 + h, P + SUB * i:P + SUB * i + SUB], kt[rows, j, META + P:], q,
                                      start=True, stop=True)
                    last.then_inc(k_used, 1)
            pe.wait_ge(gla_masked, 4)
            pe.wait_ge(gla_meta_taken, 1)
            for h in range(GLA_HEADS):
                o = ps[:, 2 + h // 2, 256 * (h % 2):256 * (h % 2) + 256]
                cols = slice(512 + GLA_DV * h, 512 + GLA_DV * h + GLA_DV)
                mm(o, vtok[:, 1, cols], A[:, h, 0:2 * P], start=True, stop=False)
                mm(o[:, P:2 * P], vtok[:, 2, cols], A[:, h, 2 * P:W], start=False, stop=False)
                last = mm(o, vtok[0:META, 0, cols], A0[0:META, h, :], start=False, stop=True)
            last.then_inc(gla_out_ready, 1)
            pe.wait_ge(head_sq, 2)
            for j in range(2):
                last = mm(ps[:, 4 + j, :], ones[:, 0:P], one["sqh"][:, 512 * j:512 * j + 512],
                          start=True, stop=True)
            last.then_inc(head_sum, 1)

            pe.wait_ge(gla_mixed, 1)
            columns("w_out", mix, REAL)
            norm(1, sq1[:, 0:C * REAL].rearrange("p (c t) -> p c t", c=C), REAL)
            pe.wait_ge(normed, 2)
            columns("w_peer_q", xn_real, REAL)
            tiles_are_taken(pe, TILE0["expert_u"])
            for h in range(PH):
                if h >= 2:
                    pe.wait_ge(key_scores_taken, 2 * (h - 1))
                for half in range(2):
                    rows = slice(64 * half, 64 * half + 64)
                    for t in range(2):
                        last = mm(ps[:, 4 + 2 * (h % 2) + half, t * P:t * P + P], qp[rows, h, t * P:t * P + P],
                                  keys_w[rows, h, :], start=True, stop=True)
                    last.then_inc(key_scores_ready, 1)

            b0, g0 = FIRST["expert_u"], TILE0["expert_u"]
            def experts_in(first, turns, gates=None):
                with pe.Fori(first, first + turns) as i:
                    for k in range(RING):
                        column_block(b0 + k, g0 + 2 * k, (b0 + k) % RING, xn_real, REAL, i, i * 2)
                        if gates is not None:
                            gate_tables(i * 4 - (4 * gates - k), k, 4)

            def gate_tables(n, k, bank0):
                pe.wait_ge(onehots_ready, n + 1)
                for j in range(GROUP):
                    last = mm(ps[:, bank0 + k % 2, HALF_KEYS * j:HALF_KEYS * (j + 1)], onehot2[:, k % 2, j, :],
                              onehot1[:, k % 2, j, :], start=True, stop=True)
                last.then_inc(gates_ready, 1)

            experts_in(0, 8)
            pe.wait_ge(routed, 1)
            for t in range(2):
                for j, name in enumerate(("gate", "i1", "i2")):
                    last = nc.tensor.transpose(ps[:, 4 + t, P * j:P * j + P],
                                               route[name][:, t * P:(t + 1) * P], ident[:, :])
            last.then_inc(slots_ready, 1)
            pe.wait_ge(slots_taken, 1)
            experts_in(8, 8, gates=8)

            tiles_are_taken(pe, TILE0["w_in_2_features"])
            pe.wait_ge(gates_applied, 32)
            def open_sums():
                for n in range(4):
                    mm(ps[:, 4 + n, :], zeros[:, :], xn[:, 0:512], start=True, stop=True)

            def row_block(b, slot, rows0, rows1, turn=0):
                block_landed(pe, b, slot, turn)
                w = ring_rows(slot)
                for c, rhs in enumerate((rows0, rows1)):
                    for n in range(C):
                        i = mm(ps[:, 4 + n // 2, 256 * (n % 2):256 * (n % 2) + 256], w[:, c, n * P:(n + 1) * P],
                               rhs, start=False, stop=True, skip_group_check=True)
                        if c == n == 0:
                            i.then_inc(block_begun, 1)

            def close_sums():
                mm(ps[:, 7, 0:1], zeros[:, :], xn[:, 0:1], start=False, stop=True,
                   skip_group_check=True).then_inc(y_ready, 1)

            open_sums()
            b0 = FIRST["expert_v"]
            with pe.Fori(0, 8) as i:
                for k in range(RING):
                    row_block(b0 + k, (b0 + k) % RING, act_store[:, i * 8 + 2 * k, :],
                              act_store[:, i * 8 + (2 * k + 1), :], i)
                    gate_tables(i * 4 + (32 + k), k, 0)
            pe.wait_ge(gates_applied, 64)
            with pe.Fori(8, 16) as i:
                for k in range(RING):
                    row_block(b0 + k, (b0 + k) % RING, act_store[:, i * 8 + 2 * k, :],
                              act_store[:, i * 8 + (2 * k + 1), :], i)
            close_sums()

            sq = sq_late.rearrange("p (c t) -> p c t", c=C)
            sq_r = sq_late[:, 0:C * REAL].rearrange("p (c t) -> p c t", c=C)
            norm(2, sq_r, REAL)
            norm(3, sq, T)
            pe.wait_ge(normed, 4)
            columns("w_in_2_features", xn_all, T)
            for c in range(C):
                mm(ps[:, 4, 0:T], kiwi_w[:, c, 0:P], xn_all[:, c, :], start=c == 0, stop=c == C - 1)
            for t in range(2):
                for c in range(C):
                    last = mm(ps[:, 5, 8 * t:8 * t + 8], xn_all[:, c, META + P * t:META + P * t + P],
                              kiwi_w[:, c, P:P + IDX_HEADS], start=c == 0, stop=c == C - 1)
            last.then_inc(kiwi_ready, 1)
            value_blocks("w_in_2_values", xn_all[:, :, 0:META], META)
            pe.wait_ge(kiwi_taken, 2)
            tiles_are_taken(pe, TILE0["w_in_2_values"])
            for t in range(2):
                seen = META + P * (t + 1)
                for h in range(IDX_HEADS):
                    n = 8 * t + h
                    rows = slice(64 * (h % 2), 64 * (h % 2) + 64)
                    if n >= 2:
                        pe.wait_ge(idx_taken, n - 1)
                    mm(ps[:, 4 + n % 2, 0:seen], feat2[rows, QI + h // 2, META + P * t:META + P * t + P],
                       two["kidup"][rows, 0:seen], start=True, stop=True).then_inc(idx_ready, 1)
            pe.wait_ge(conv_ready, 1)
            columns("w_conv_out_2", yc, REAL)
            tiles_are_taken(pe, TILE0["w_attn_out_2"])
            pe.wait_ge(idx_taken, 16)

            def attention_scores(n):
                t, h = n // 8, n % 8
                seen = META + P * (t + 1)
                if n >= 2:
                    pe.wait_ge(masked_ready, n - 1)
                mm(ps[:, n % 2, 0:seen], feat2[:, QF + h, META + P * t:META + P * t + P],
                   feat2[:, KF + h, 0:seen], start=True, stop=True).then_inc(logits_ready, 1)

            def attention_values(n):
                t, h = n // 8, n % 8
                pe.wait_ge(probs_scaled, n + 1)
                if n >= 2:
                    pe.wait_ge(turned_taken, n - 1)
                turned = ps[:, 2 + n % 2, :]
                p = pr[:, n % 2, :]
                last = nc.tensor.transpose(turned[0:META, 0:P], p[:, 0:META], ident[:, :])
                for c in range(t + 1):
                    last = nc.tensor.transpose(turned[:, P * (c + 1):P * (c + 2)],
                                               p[:, META + P * c:META + P * (c + 1)], ident[:, :])
                last.then_inc(probs_turned, 1)
                pe.wait_ge(turned_taken, n + 1)
                o = ps[:, 4 + 2 * t + h // 4, P * (h % 4):P * (h % 4) + P]
                cols = slice(P * h, P * h + P)
                mm(o, v2[0:META, 0, cols], pT[0:META, n % 2, 0:P], start=True, stop=False)
                for c in range(t + 1):
                    last = mm(o, v2[:, 1 + c, cols], pT[:, n % 2, P * (c + 1):P * (c + 2)], start=False,
                              stop=c == t)
                last.then_inc(attn_ready, 1)

            attention_scores(0)
            for n in range(16):
                if n < 15:
                    attention_scores(n + 1)
                attention_values(n)
            pe.wait_ge(attn_taken, 4)
            columns("w_attn_out_2", ya, REAL)
            pe.wait_ge(mixed_ready, 1)
            columns("w_out_2", ya, REAL)
            norm(4, sq_r, REAL)
            pe.wait_ge(normed, 5)
            b0, g0 = FIRST["w_gate_up_2"], TILE0["w_gate_up_2"]
            columns("w_gate_up_2", xn_real, REAL)
            open_sums()
            tiles_are_taken(pe, TILE0["w_gate_up_2"] + 2 * FF)
            b0, turns = FIRST["w_down_2"], COUNT["w_down_2"] // RING
            with pe.Fori(0, turns) as i:
                for k in range(RING):
                    row_block(b0 + k, (b0 + k) % RING, hidden[:, i * 8 + 2 * k, :],
                              hidden[:, i * 8 + (2 * k + 1), :], i)
            for k in range(turns * RING, COUNT["w_down_2"]):
                row_block(b0 + k, (b0 + k) % RING, hidden[:, 2 * k, :], hidden[:, 2 * k + 1, :])
            close_sums()
            norm(5, sq_r, REAL)

        @block.scalar
        def _(act):
            a = nc.scalar.activation
            steps = [0]

            def link(ins):
                steps[0] += 1
                ins.then_inc(act_step, 1)
                act.wait_ge(act_step, steps[0])


            def norm(k, src, sq):
                a(sq, src, ACT.Square).then_inc(squares_ready, 1)
                act.wait_ge(var_ready, k + 1)
                n = T if k in (0, 3) else REAL
                a(rstd[:, 0:n], var[:, 0:n], ACT.Sqrt).then_inc(root_ready, 1)

            def take(g, out, tokens, turn=0, rows=P):
                act.wait_ge(tile_ready, turn + g + 1)
                a(out, bank_of(g)[0:rows, 0:tokens], ACT.Copy).then_inc(tile_taken[g % BANKS], 1)

            act.wait_ge(x_landed, 16)
            norm(0, res[:, :, :], sq1.rearrange("p (c t) -> p c t", c=C))
            act.wait_ge(glr_ready, 1)
            a(one["glrT"][0:GLA_RANK, :], ps[0:GLA_RANK, 6, 0:T], ACT.Copy).then_inc(glr_taken, 1)
            with act.Fori(0, 2) as i:
                for j in range(0, 8, 2):
                    take(j, feat[:, i * 8 + j, :], T, i * 8)

            for n in range(0, 12, 2):
                take(16 + n, vtok[:, n % 3, COLS * (n // 3):COLS * (n // 3) + COLS], COLS)
            act.wait_ge(gate_biased, 2)
            link(a(gl, gx, ACT.Abs))
            link(a(gl, gl, ACT.Exp, scale=-1.0))
            a(gl, gl, ACT.Ln, bias=1.0).then_inc(gate_soft, 1)

            def softness(n, cols):
                act.wait_ge(z_taken, n + 1)
                if n >= 2:
                    act.wait_ge(sp_ready, n - 1)
                s = soft[:, n % 2, 0:cols]
                link(a(s, zm[:, n, 0:cols], ACT.Abs))
                link(a(s, s, ACT.Exp, scale=-1.0))
                a(s, s, ACT.Ln, bias=1.0).then_inc(soft_ready, 1)

            def weights(n, cols):
                act.wait_ge(d_ready, n + 1)
                a(zm[:, n, 0:cols], zm[:, n, 0:cols], ACT.Exp).then_inc(a_ready, 1)

            softness(0, W)
            for n in range(1, 9):
                softness(n, W if n < 8 else REAL)
                weights(n - 1, W)
            weights(8, REAL)

            def head_norm(k, ready):
                act.wait_ge(ready, 1)
                a(one["sqh"].rearrange("p (b n) -> p b n", b=2), ps[:, 2:4, :], ACT.Square).then_inc(head_sq, 1)
                act.wait_ge(head_var, k + 1)
                a(one["rh"], one["rh"], ACT.Sqrt).then_inc(head_root, 1)

            head_norm(0, sb_out_ready)
            act.wait_ge(q_exp_in, 1)
            a(dq, dq, ACT.Exp).then_inc(q_exp, 1)
            for n in range(2 * SUBS):
                seen = META + P * (1 + (n >= SUBS))
                act.wait_ge(k_exp_in, n + 1)
                a(ke[:, n % 2, 0:seen], ke[:, n % 2, 0:seen], ACT.Exp).then_inc(k_exp, 1)
            act.wait_ge(k_used, 2 * SUBS)
            a(A0[0:META, :, :].rearrange("p (j e) t -> p e j t", e=2),
              ps[0:META, 0:2, :].rearrange("p e (j t) -> p e j t", j=2), ACT.Copy).then_inc(gla_meta_taken, 1)
            a(sil, feat[:, 12:16, META:], ACT.Silu).then_inc(silu_ready, 1)
            head_norm(1, gla_out_ready)

            tiles_are_taken(act, TILE0["w_out"] + 8)
            norm(1, res[:, :, META:], sq1[:, 0:C * REAL].rearrange("p (c t) -> p c t", c=C))
            for h in range(PH):
                take(TILE0["w_peer_q"] + h, qp[:, h, :], REAL)
            for n in range(2 * PH):
                h, half = n // 2, n % 2
                act.wait_ge(key_scores_ready, n + 1)
                a(sc[:, h:h + 9:8, half * P:half * P + P],
                  ps[:, 4 + 2 * (h % 2) + half, 0:2 * P].rearrange("p (t k) -> p t k", t=2),
                  ACT.Copy).then_inc(key_scores_taken, 1)

            g0 = TILE0["expert_u"]
            def experts(first, turns):
                with act.Fori(first, first + turns) as i:
                    for j in range(8):
                        act.wait_ge(tile_ready, i * 8 + (g0 + j + 1))
                        a(act_store[:, i * 8 + j, :], bank_of(g0 + j)[:, 0:REAL],
                          ACT.Gelu).then_inc(tile_taken[(g0 + j) % BANKS], 1)

            experts(0, 6)
            act.wait_ge(tops_shifted, 1)
            a(route["gate"], route["gate"], ACT.Exp).then_inc(tops_exp, 1)
            experts(6, 2)
            act.wait_ge(slots_ready, 1)
            a(slots[:, :, :].rearrange("p j (t n) -> p t j n", t=2),
              ps[:, 4:6, 0:3 * P].rearrange("p t (j n) -> p t j n", j=3), ACT.Copy).then_inc(slots_taken, 1)
            experts(8, 8)

            sq = sq_late.rearrange("p (c t) -> p c t", c=C)
            sq_r = sq_late[:, 0:C * REAL].rearrange("p (c t) -> p c t", c=C)
            act.wait_ge(residual, 4)
            norm(2, res[:, :, META:], sq_r)
            act.wait_ge(normed, 3)
            norm(3, res[:, :, :], sq)
            g0 = TILE0["w_in_2_features"]
            with act.Fori(0, 7) as i:
                for j in range(0, 8, 2):
                    take(g0 + j, feat2[:, i * 8 + j, :], T, i * 8)
            for j in range(56, 60, 2):
                take(g0 + j, feat2[:, j, :], T)
            act.wait_ge(kiwi_ready, 1)
            a(two["kidup"], ps[:, 4, 0:T], ACT.Copy).then_inc(kiwi_taken, 1)
            a(two["wi"], ps[:, 5, 0:16], ACT.Copy, scale=IDX_SCALE).then_inc(kiwi_taken, 1)
            g0 = TILE0["w_in_2_values"]
            for n in range(0, 12, 2):
                rows = META if n % 3 == 0 else P
                take(g0 + n, v2[0:rows, n % 3, COLS * (n // 3):COLS * (n // 3) + COLS], COLS, rows=rows)
            tiles_are_taken(act, g0)
            a(feat2[:, GA:GA + 16, :], feat2[:, GA:GA + 16, :], ACT.Sigmoid).then_inc(sigmoid_ready, 1)
            for n in range(8):
                take(TILE0["w_conv_out_2"] + n, yco[:, n, :], REAL)

            stat = two["stat"]
            def probs(n):
                seen = META + P * (n // 8 + 1)
                act.wait_ge(masked_ready, n + 1)
                if n >= 2:
                    act.wait_ge(probs_turned, n - 1)
                a(pr[:, n % 2, 0:seen], lm[:, n % 2, 0:seen], ACT.Exp, bias=stat[:, 16 + n:17 + n],
                  accum_out=stat[:, 32 + n:33 + n]).then_inc(probs_ready, 1)

            def turned(n):
                t = n // 8
                act.wait_ge(probs_turned, n + 1)
                if n >= 2:
                    act.wait_ge(attn_ready, n - 1)
                link(a(pT[0:META, n % 2, 0:P], ps[0:META, 2 + n % 2, 0:P], ACT.Copy))
                end = P * (t + 2)
                a(pT[:, n % 2, P:end], ps[:, 2 + n % 2, P:end], ACT.Copy).then_inc(turned_taken, 1)

            def outputs(n):
                t, q = n // 2, n % 2
                act.wait_ge(attn_ready, 4 * (n + 1))
                a(ya[:, 4 * q:4 * q + 4, P * t:P * t + P],
                  ps[:, 4 + n, :].rearrange("p (h m) -> p h m", h=4), ACT.Copy).then_inc(attn_taken, 1)

            probs(0)
            for n in range(16):
                if n < 15:
                    probs(n + 1)
                turned(n)
                if n % 4 == 0 and n:
                    outputs(n // 4 - 1)
            outputs(3)

            tiles_are_taken(act, TILE0["w_out_2"] + 8)
            norm(4, res[:, :, META:], sq_r)
            g0 = TILE0["w_gate_up_2"]

            def gate_tiles(n, turn=None):
                for j in range(2):
                    g = g0 + 4 * n + j
                    act.wait_ge(tile_ready, (0 if turn is None else turn * 8) + g + 1)
                    if n or turn is not None:
                        act.wait_ge(tile_taken[(g + 2) % BANKS], (0 if turn is None else turn * 2) + (g - 2) // BANKS + 1)
                    a(sg[:, j, :], bank_of(g)[:, 0:REAL], ACT.Silu).then_inc(tile_taken[g % BANKS], 1)

            gate_tiles(0)
            gate_tiles(1)
            with act.Fori(1, FF // 4) as i:
                gate_tiles(0, i)
                gate_tiles(1, i)
            gate_tiles(FF // 2 - 1)
            act.wait_ge(residual, 8)
            norm(5, res[:, :, META:], sq_r)

        @block.vector
        def _(dve):
            v = nc.vector
            steps = [0]

            def link(ins):
                steps[0] += 1
                ins.then_inc(vec_step, 1)
                dve.wait_ge(vec_step, steps[0])

            tt, ts, stt = v.tensor_tensor, v.tensor_scalar, v.scalar_tensor_tensor

            def norm(k, src, gain, dst):
                n = T if k in (0, 3) else REAL
                at = SMALL[gain][0]
                dve.wait_ge(sum_ready, k + 1)
                ts(var[:, 0:n], ps[:, 7, 0:n], 1.0 / D, EPS, ALU.mult, ALU.add).then_inc(var_ready, 1)
                dve.wait_ge(root_ready, k + 1)
                link(v.reciprocal(rstd[:, 0:n], rstd[:, 0:n]))
                for c in range(C):
                    i = stt(dst[:, c, :], src[:, c, :], small[:, at + c:at + c + 1], rstd[:, 0:n], ALU.mult, ALU.mult)
                    if c < C - 1:
                        link(i)
                i.then_inc(normed, 1)
                dve.wait_ge(normed, k + 1)

            def take(g, out, tokens, turn=0, rows=P):
                dve.wait_ge(tile_ready, turn + g + 1)
                v.tensor_copy(out, bank_of(g)[0:rows, 0:tokens]).then_inc(tile_taken[g % BANKS], 1)

            dve.wait_ge(x_landed, 16)
            dve.wait_ge(small_landed, 16)
            norm(0, res, "norm1", xn_all)
            xm4 = one["xm"].rearrange("p (c r t) -> p c r t", c=C, r=P // META)
            v.tensor_copy(xm4, xn_all[:, :, 0:META].unsqueeze(2).broadcast_to([P, C, P // META, META])
                          ).then_inc(meta_spread, 1)
            with dve.Fori(0, 2) as i:
                for j in range(1, 8, 2):
                    take(j, feat[:, i * 8 + j, :], T, i * 8)
            dve.wait_ge(gate_logits_ready, 1)
            bg = SMALL["b_gate"][0]
            for j in range(2):
                ts(gx[:, j, :], ps[:, 4 + j, 0:T], small[:, bg + j:bg + j + 1], None, ALU.add).then_inc(gate_biased, 1)
            tiles_are_taken(dve, 16)
            for h in range(8):
                rows = slice(64 * (h % 2), 64 * (h % 2) + 64)
                i = v.tensor_copy(kbd[rows, h // 2, META * h:META * h + META], feat[rows, 4 + h // 2, 0:META])
                link(i) if h < 7 else i.then_inc(kbd_ready, 1)
            for n in range(1, 12, 2):
                take(16 + n, vtok[:, n % 3, COLS * (n // 3):COLS * (n // 3) + COLS], COLS)
            tiles_are_taken(dve, 28)
            tt(one["vbd"], vtok[:, 0, 0:512], one["bdm"], ALU.mult).then_inc(vbd_ready, 1)

            def scaled(n):
                if n < 8:
                    dve.wait_ge(z_ready, n + 1)
                    stt(zm[:, n, :], ps[:, 5 + n % 2, 0:W], SB_DIM ** -0.5, one["hide"], ALU.mult,
                        ALU.add).then_inc(z_taken, 1)
                else:
                    dve.wait_ge(z0_ready, 1)
                    ts(zm[:, n, 0:REAL], ps[:, 4, 0:REAL], SB_DIM ** -0.5, None, ALU.mult).then_inc(z_taken, 1)

            def softplus(n, cols):
                dve.wait_ge(soft_ready, n + 1)
                if n >= 2:
                    dve.wait_ge(pe_used_sp, n - 1)
                stt(sp_[:, n % 2, 0:cols], zm[:, n, 0:cols], 0.0, soft[:, n % 2, 0:cols], ALU.max,
                    ALU.add).then_inc(sp_ready, 1)

            def log_weight(n, cols):
                dve.wait_ge(s_ready, n + 1)
                bank = 1 if n == 8 else 7 if n % 2 else 0
                tt(zm[:, n, 0:cols], zm[:, n, 0:cols], ps[:, bank, 0:cols], ALU.subtract).then_inc(d_ready, 1)

            scaled(0)
            for n in range(9):
                if n < 8:
                    scaled(n + 1)
                softplus(n, W if n < 8 else REAL)
                if n:
                    log_weight(n - 1, W)
            log_weight(8, REAL)

            def head_norm(k, width):
                dve.wait_ge(head_sum, k + 1)
                ts(one["rh"].rearrange("p (b n) -> p b n", b=2), ps[:, 4:6, :], 1.0 / width, EPS, ALU.mult,
                   ALU.add).then_inc(head_var, 1)
                dve.wait_ge(head_root, k + 1)
                link(v.reciprocal(one["rh"], one["rh"]))

            dve.wait_ge(gate_soft, 1)
            link(stt(gx, gx, 0.0, gl, ALU.min, ALU.subtract))
            for j in range(2):
                link(v.tensor_tensor_scan(gl[:, j, :], ones[:, 0:T], gx[:, j, :], 0.0, ALU.mult, ALU.add))
            link(ts(bcum, gl, 1.0 / GLA_TAU, None, ALU.mult))
            link(ts(nb, gl, -1.0 / GLA_TAU, None, ALU.mult))
            for j in range(2):
                grp = bcum[:, j, META:].rearrange("p (i s) -> p i s", s=SUB)
                link(tt(dq[:, j, :].rearrange("p (i s) -> p i s", s=SUB), grp,
                             grp[:, :, SUB // 2 - 1:SUB // 2].broadcast_to([P, SUBS, SUB]), ALU.subtract))
            ts(dq, dq, -CLAMP, CLAMP, ALU.max, ALU.min).then_inc(q_exp_in, 1)

            head_norm(0, SB_DIM)
            at = SMALL["sb_norm"][0]
            for p in range(4):
                i = stt(mix[:, p, :], ps[:, 2 + p // 2, 256 * (p % 2):256 * (p % 2) + 256],
                        small[:, at + p:at + p + 1], one["rh"][:, 256 * p:256 * p + 256], ALU.mult, ALU.mult)
                link(i) if p < 3 else i.then_inc(sb_mixed, 1)
            dve.wait_ge(q_exp, 1)
            stt(qt, feat[:, 8:10, META:], GLA_DK ** -0.5, dq, ALU.mult, ALU.mult).then_inc(q_decayed, 1)

            def key_exponent(n):
                i, j = n // 2, n % 2
                seen = META + P * (1 + (i >= SUBS // 2))
                mid = META + SUB * i + SUB // 2 - 1
                if n >= 2:
                    dve.wait_ge(k_decayed, n - 1)
                ts(ke[:, j, 0:seen], nb[:, j, 0:seen], bcum[:, j, mid:mid + 1], CLAMP, ALU.add,
                   ALU.min).then_inc(k_exp_in, 1)

            def key_decay(n):
                i, j = n // 2, n % 2
                seen = META + P * (1 + (i >= SUBS // 2))
                dve.wait_ge(k_exp, n + 1)
                if n >= 2:
                    dve.wait_ge(k_used, n - 1)
                tt(kt[:, j, 0:seen], ke[:, j, 0:seen], feat[:, 10 + j, 0:seen], ALU.mult).then_inc(k_decayed, 1)

            key_exponent(0)
            for n in range(2 * SUBS):
                if n < 2 * SUBS - 1:
                    key_exponent(n + 1)
                key_decay(n)
            dve.wait_ge(k_used, 2 * SUBS)
            for h in range(GLA_HEADS):
                tt(A[:, h, :], ps[:, 4 + h, 0:W], one["keep"], ALU.mult).then_inc(gla_masked, 1)
            head_norm(1, GLA_DV)
            at = SMALL["gla_norm"][0]
            for h in range(4):
                link(stt(mix[:, 4 + h, :], ps[:, 2 + h // 2, 256 * (h % 2):256 * (h % 2) + 256],
                              small[:, at + h:at + h + 1], one["rh"][:, 256 * h:256 * h + 256], ALU.mult, ALU.mult))
            dve.wait_ge(silu_ready, 1)
            tt(mix[:, 4:8, :], mix[:, 4:8, :], sil, ALU.mult).then_inc(gla_mixed, 1)

            def add_tiles(name):
                for n in range(8):
                    g = TILE0[name] + n
                    dve.wait_ge(tile_ready, g + 1)
                    tt(res[:, n, META:], res[:, n, META:], bank_of(g)[:, 0:REAL], ALU.add).then_inc(
                        tile_taken[g % BANKS], 1)

            add_tiles("w_out")
            norm(1, res[:, :, META:], "norm2", xn_real)

            R = route
            dve.wait_ge(key_scores_taken, 16)

            def best16(values, out, index):
                link(v.max(out[:, 0:8], values))
                link(v.max_index(index[:, 0:8], out[:, 0:8], values))
                link(v.match_replace(out=values, in_to_replace=out[:, 0:8], in_values=values, imm_value=TAKEN))
                link(v.max(out[:, 8:16], values))
                link(v.max_index(index[:, 8:16], out[:, 8:16], values))

            rows = {k: R[k].rearrange("p (c k) -> p c k", c=16) for k in ("tv", "pos", "ix")}
            cand = R["cand"].rearrange("p (a b) -> p a b", a=TOPK)
            for c in range(16):
                index = rows["ix"][:, c, :].bitcast(U32)
                for half in range(2):
                    best16(sc[:, c, P * half:P * half + P], R["v"][:, TOPK * half:TOPK * half + TOPK],
                           index[:, TOPK * half:TOPK * half + TOPK])
                link(tt(cand, R["v"][:, 0:TOPK].unsqueeze(2).broadcast_to([P, TOPK, TOPK]),
                             R["v"][:, TOPK:].unsqueeze(1).broadcast_to([P, TOPK, TOPK]), ALU.add))
                best16(R["cand"], rows["tv"][:, c, :], rows["pos"][:, c, :].bitcast(U32))
            link(v.tensor_copy(R["ixf"], R["ix"].bitcast(U32)))

            tv = R["tv"].rearrange("p (c k) -> p c k", c=16)
            gate = R["gate"].rearrange("p (c k) -> p c k", c=16)
            tt(gate, tv, tv[:, :, 0:1].broadcast_to([P, 16, TOPK]), ALU.subtract).then_inc(tops_shifted, 1)
            pos, pi = R["pos"].bitcast(U32), R["pi"].bitcast(U32)
            link(ts(pi, pos, 4, None, ALU.logical_shift_right))
            link(v.tensor_copy(R["af"], pi))
            link(ts(pi, pos, TOPK - 1, None, ALU.bitwise_and))
            link(v.tensor_copy(R["bf"], pi))
            ix = R["ixf"].rearrange("p (c h k) -> p c h k", c=16, h=2)
            for t in range(2):
                for half, (digit, out) in enumerate(((R["af"], R["i1"]), (R["bf"], R["i2"]))):
                    part = slice(SLOTS * t, SLOTS * t + SLOTS)
                    eq = R["eq"].rearrange("p (s a) -> p s a", a=TOPK)
                    link(tt(eq, digit[:, part].unsqueeze(2).broadcast_to([P, SLOTS, TOPK]),
                                 iota[:, 0:TOPK].unsqueeze(1).broadcast_to([P, SLOTS, TOPK]), ALU.is_equal))
                    eq4 = R["eq"].rearrange("p (c k a) -> p c k a", c=PH, a=TOPK)
                    link(tt(eq4, eq4, ix[:, PH * t:PH * t + PH, half, :].unsqueeze(2).broadcast_to(
                        [P, PH, TOPK, TOPK]), ALU.mult))
                    link(v.tensor_reduce(out[:, part], eq, AX.X, ALU.add))
            dve.wait_ge(tops_exp, 1)
            link(v.tensor_reduce(R["sum"], gate, AX.X, ALU.add))
            link(v.reciprocal(R["rsum"], R["sum"]))
            tt(gate, gate, R["rsum"].unsqueeze(2).broadcast_to([P, 16, TOPK]), ALU.mult).then_inc(routed, 1)

            def onehots(n, k, token, half):
                for j in range(GROUP):
                    ts(onehot2[:, k % 2, j, :], iota[:, :], slots[:, 2, token(j)], None, ALU.is_equal)
                    i = ts(onehot1[:, k % 2, j, :], iota[:, HALF_KEYS * half:HALF_KEYS * (half + 1)],
                           slots[:, 1, token(j)], slots[:, 0, token(j)], ALU.is_equal, ALU.mult)
                i.then_inc(onehots_ready, 1)

            def apply_gates(n, k, span, half, bank0):
                dve.wait_ge(gates_ready, n + 1)
                h = act_store[:, HALF_KEYS * half:HALF_KEYS * (half + 1), span]
                g = ps[:, bank0 + k % 2, :].rearrange("p (t i) -> p i t", t=GROUP)
                tt(h, h, g, ALU.mult).then_inc(gates_applied, 1)

            dve.wait_ge(slots_taken, 1)
            for half in range(2):
                n0, bank0 = 32 * half, 4 - 4 * half
                if half == 0:
                    tiles_are_taken(dve, TILE0["expert_u"] + HALF_KEYS)
                else:
                    tiles_are_taken(dve, TILE0["w_in_2_features"])
                for k in range(4):
                    onehots(n0 + k, k, lambda j: slice(GROUP * k + j, GROUP * k + j + 1), half)
                    if k:
                        apply_gates(n0 + k - 1, k - 1, slice(GROUP * (k - 1), GROUP * k), half, bank0)
                with dve.Fori(1, 8) as i:
                    for k in range(4):
                        at = i * (4 * GROUP) + GROUP * k
                        onehots(0, k, lambda j: bass.ds(i * (4 * GROUP) + (GROUP * k + j), 1), half)
                        apply_gates(i * 4 + (n0 + k - 1), k - 1,
                                    bass.ds(i * (4 * GROUP) + GROUP * (k - 1), GROUP), half, bank0)
                apply_gates(n0 + 31, 3, slice(REAL - GROUP, REAL), half, bank0)

            def add_sums(n):
                dve.wait_ge(y_ready, n)
                for m in range(4):
                    r = res[:, 2 * m:2 * m + 2, META:]
                    tt(r, r, ps[:, 4 + m, :].rearrange("p (c t) -> p c t", c=2), ALU.add).then_inc(residual, 1)

            add_sums(1)
            link(v.tensor_copy(res[:, :, 0:META], meta_2))
            dve.wait_ge(residual, 4)
            norm(2, res[:, :, META:], "norm_f", res[:, :, META:])
            norm(3, res, "norm_mix", xn_all)
            g0 = TILE0["w_in_2_features"]
            with dve.Fori(0, 7) as i:
                for j in range(1, 8, 2):
                    take(g0 + j, feat2[:, i * 8 + j, :], T, i * 8)
            for j in range(57, 60, 2):
                take(g0 + j, feat2[:, j, :], T)
            g0 = TILE0["w_in_2_values"]
            tiles_are_taken(dve, g0)
            for n in range(1, 12, 2):
                rows = META if n % 3 == 0 else P
                take(g0 + n, v2[0:rows, n % 3, COLS * (n // 3):COLS * (n // 3) + COLS], COLS, rows=rows)
            dve.wait_ge(kiwi_taken, 2)
            dve.wait_ge(vis_ready, 1)
            for t in range(2):
                seen = META + P * (t + 1)
                for h in range(IDX_HEADS):
                    n = 8 * t + h
                    dve.wait_ge(idx_ready, n + 1)
                    out = score[:, t, 0:seen] if h == 0 else rel[:, n % 2, 0:seen]
                    ts(out, ps[:, 4 + n % 2, 0:seen], 0.0, two["wi"][:, n:n + 1], ALU.max,
                       ALU.mult).then_inc(idx_taken, 1)
                    dve.wait_ge(idx_taken, n + 1)
                    if h:
                        link(tt(score[:, t, 0:seen], score[:, t, 0:seen], out, ALU.add))
                part = score[:, t, P * t:seen]
                link(tt(part, part, two["vis"], ALU.add))
            u = feat2[:, CU:CU + 8, :]
            link(tt(u, u, feat2[:, CC:CC + 8, :], ALU.mult))
            at = SMALL["conv"][0]
            for c in range(C):
                w = [small[:, at + C * k + c:at + C * k + c + 1] for k in range(CONV_K)]
                link(ts(yc[:, c, :], u[:, c, META:], w[2], None, ALU.mult))
                for k in (1, 0):
                    off = META - (CONV_K - 1) + k
                    link(stt(yc[:, c, :], u[:, c, off:off + REAL], w[k], yc[:, c, :], ALU.mult, ALU.add))
            tt(yc, yc, feat2[:, CB:CB + 8, META:], ALU.mult).then_inc(conv_ready, 1)
            top8 = two["top8"]
            for t in range(2):
                seen = META + P * (t + 1)
                s = score[:, t, 0:seen]
                for r in range(-(-KEEP // 8)):
                    link(v.max(top8[:, 0:8], s))
                    if 8 * (r + 1) > KEEP:
                        link(v.memset(top8[:, KEEP - 8 * r:8], TAKEN))
                    link(v.match_replace(out=s, in_to_replace=top8[:, 0:8], in_values=s, imm_value=TAKEN))
                link(ts(selb[:, t, 0:seen], s, TAKEN, NEG, ALU.not_equal, ALU.mult))
                part = selb[:, t, P * t:seen]
                link(tt(part, part, two["vis"], ALU.add))

            stat = two["stat"]
            def mask_logits(n):
                t = n // 8
                seen = META + P * (t + 1)
                dve.wait_ge(logits_ready, n + 1)
                if n >= 2:
                    dve.wait_ge(probs_ready, n - 1)
                m = lm[:, n % 2, 0:seen]
                link(stt(m, ps[:, n % 2, 0:seen], HEAD_DIM ** -0.5, selb[:, t, 0:seen], ALU.mult, ALU.add))
                link(v.tensor_reduce(stat[:, n:n + 1], m, AX.X, ALU.max))
                ts(stat[:, 16 + n:17 + n], stat[:, n:n + 1], -1.0, None, ALU.mult).then_inc(masked_ready, 1)

            def scale_probs(n):
                seen = META + P * (n // 8 + 1)
                dve.wait_ge(probs_ready, n + 1)
                link(v.reciprocal(stat[:, 48 + n:49 + n], stat[:, 32 + n:33 + n]))
                m = pr[:, n % 2, 0:seen]
                ts(m, m, stat[:, 48 + n:49 + n], None, ALU.mult).then_inc(probs_scaled, 1)

            mask_logits(0)
            for n in range(16):
                if n < 15:
                    mask_logits(n + 1)
                scale_probs(n)

            dve.wait_ge(sigmoid_ready, 1)
            dve.wait_ge(conv_gated, 1)
            for n in range(8):
                g = TILE0["w_attn_out_2"] + n
                dve.wait_ge(tile_ready, g + 1)
                tt(yc[:, n, :], bank_of(g)[:, 0:REAL], feat2[:, GA + n, META:], ALU.mult).then_inc(
                    tile_taken[g % BANKS], 1)
            tiles_are_taken(dve, TILE0["w_out_2"])
            tt(ya, yc, yco, ALU.add).then_inc(mixed_ready, 1)
            add_tiles("w_out_2")
            norm(4, res[:, :, META:], "norm_ffn", xn_real)

            g0 = TILE0["w_gate_up_2"]

            def up_tiles(n, turn=0):
                for j in range(2):
                    g = g0 + 4 * n + 2 + j
                    dve.wait_ge(tile_taken[(g - 2) % BANKS], turn * 2 + (g - 2) // BANKS + 1)
                    dve.wait_ge(tile_ready, turn * 8 + g + 1)
                    tt(hidden[:, turn * 4 + (2 * n + j), :], bank_of(g)[:, 0:REAL], sg[:, j, :],
                       ALU.mult).then_inc(tile_taken[g % BANKS], 1)

            with dve.Fori(0, FF // 4) as i:
                up_tiles(0, i)
                up_tiles(1, i)
            up_tiles(FF // 2 - 1)
            add_sums(2)
            dve.wait_ge(residual, 8)
            norm(5, res[:, :, META:], "norm_final", outT)


def columns_to_blocks(w):
    n = w.shape[1]
    return w.reshape(C, P, n // COLS, COLS).transpose(2, 1, 0, 3).reshape(n // COLS, P, BLOCK)


def rows_to_blocks(w):
    n = w.shape[0]
    return w.reshape(n // COLS, 2, P, D).transpose(0, 2, 1, 3).reshape(n // COLS, P, BLOCK)


def kernel(**inputs):
    import concourse.bacc as bacc
    from concourse.bass_utils import run_bass_kernel_spmd

    a = {k: np.asarray(v) for k, v in inputs.items()}
    w1, w2 = a["w_in"][0], a["w_in_2"][0]
    o1 = np.cumsum([0, 512, 512, 512, 256, 256, 512, 512, 16])
    o2 = np.cumsum([0, 1024, 1024, 1024, 512, 64, 8, 1024, 1024, 1024, 1024, 1024])

    def cut(w, o, *ids):
        return np.concatenate([w[:, o[i]:o[i + 1]] for i in ids], axis=1)

    gate = a["w_gate_2"][0].reshape(D, D_FF // COLS, 1, COLS)
    up = a["w_up_2"][0].reshape(D, D_FF // COLS, 1, COLS)
    gate_up = np.concatenate([gate, up], axis=2).reshape(D, 2 * D_FF)
    stream = np.concatenate([
        columns_to_blocks(cut(w1, o1, 0, 1, 3, 4, 6)),
        columns_to_blocks(cut(w1, o1, 2, 5)),
        columns_to_blocks(a["w_out"][0]),
        columns_to_blocks(a["w_peer_q"][0]),
        columns_to_blocks(a["expert_u"][0].T),
        rows_to_blocks(a["expert_v"][0]),
        columns_to_blocks(cut(w2, o2, 1, 6, 8, 0, 7, 9, 10, 3)),
        columns_to_blocks(cut(w2, o2, 2)),
        columns_to_blocks(a["w_conv_out_2"][0]),
        columns_to_blocks(a["w_attn_out_2"][0]),
        columns_to_blocks(a["w_out_2"][0]),
        columns_to_blocks(gate_up),
        rows_to_blocks(a["w_down_2"][0]),
    ], axis=0)
    assert stream.shape == (BLOCKS, P, BLOCK)

    def features(w):
        return w.reshape(C, P, -1).transpose(1, 0, 2).reshape(P, -1)

    ki, wi = cut(w2, o2, 4), cut(w2, o2, 5)
    keys = np.concatenate([a["sub_keys1"][0].transpose(2, 0, 1), a["sub_keys2"][0].transpose(2, 0, 1)])
    parts = {
        "glr": features(cut(w1, o1, 7)), "kiwi": features(np.concatenate([ki, ki, wi], axis=1)),
        "keys": keys.reshape(P, -1), "meta_2": features(a["meta_tokens_2"].T),
        "gate_up": np.concatenate([a["w_gate_up"][0]] * (P // GLA_RANK)),
        "norm1": features(a["norm1_g"][0]), "norm2": features(a["norm2_g"][0]),
        "norm_f": features(a["norm_f_g"]), "norm_mix": features(a["norm_mix_g_2"][0]),
        "norm_ffn": features(a["norm_ffn_g_2"][0]), "norm_final": features(a["norm_final_g_2"]),
        "sb_norm": a["sb_norm_g"][0].reshape(4, P).T, "gla_norm": a["gla_norm_g"][0].reshape(4, P).T,
        "b_gate": a["b_gate_up"][0].reshape(2, P).T,
        "conv": a["conv_w_2"][0].reshape(CONV_K * C, P).T,
    }
    small = np.concatenate([parts[k].reshape(P, n) for k, (_, n) in SMALL.items()], axis=1)
    tokens = np.concatenate([a["meta_tokens"], a["x"][0]])
    arrays = {"stream": stream, "small": np.ascontiguousarray(small),
              "tokens": np.ascontiguousarray(features(tokens.T))}

    nc = bacc.Bacc("TRN2", target_bir_lowering=False, num_devices=1)
    dram = {k: nc.dram_tensor(f"in_{k}", v.shape, F32, kind="ExternalInput").ap() for k, v in arrays.items()}
    out = nc.dram_tensor("out_dram", (P, C * REAL), F32, kind="ExternalOutput").ap()
    build(nc, dram["stream"], dram["small"], dram["tokens"], out)
    r = run_bass_kernel_spmd(nc, [{f"in_{k}": v for k, v in arrays.items()}], core_ids=[0])
    got = r.results[0]["out_dram"]
    return np.ascontiguousarray(got.reshape(P, C, REAL).transpose(2, 1, 0)).reshape(1, REAL, D)
```

```python
from contextlib import ExitStack

import numpy as np

import concourse.bass as bass
from concourse import mybir

F32 = mybir.dt.float32
F32R = mybir.dt.float32r
BF16 = mybir.dt.bfloat16
U32 = mybir.dt.uint32
ALU = mybir.AluOpType
ACT = mybir.ActivationFunctionType
AX = mybir.AxisListType

P = 128
D = 1024
C = D // P
META = 16
REAL = 256
T = META + REAL
EPS = 1e-6

SB_HEADS, SB_DIM = 8, 64
GLA_HEADS, GLA_DK, GLA_DV = 4, 64, 128
GLA_RANK, GLA_TAU = 16, 16.0
SUB = 16
SUBS = REAL // SUB
CLAMP = 40.0

PH, NKEYS, TOPK = 8, 128, 16
SLOTS = PH * TOPK
GROUP = 8
HALF_KEYS = NKEYS // 2

HEADS, HEAD_DIM = 8, 128
IDX_HEADS, IDX_DIM = 8, 64
KEEP = min(256, T // 4)
IDX_SCALE = (IDX_HEADS ** -0.5) * (IDX_DIM ** -0.5)
CONV_K = 3
D_FF = ((8 * D // 3 + 255) // 256) * 256
FF = D_FF // P

NEG = -(2.0 ** 100)
TAKEN = -(2.0 ** 127)

COLS = 128
BLOCK = 1024
RING = 4
LEAD = 2


def stages():
    counts = [("w_in_features", 16), ("w_in_values", 8), ("w_out", 8), ("w_peer_q", 8),
              ("expert_u", NKEYS), ("expert_v", NKEYS), ("w_in_2_features", 60),
              ("w_in_2_values", 8), ("w_conv_out_2", 8), ("w_attn_out_2", 8), ("w_out_2", 8),
              ("w_gate_up_2", 2 * D_FF // COLS), ("w_down_2", D_FF // COLS)]
    first, at = {}, 0
    for name, n in counts:
        first[name] = at
        at += n
    return first, dict(counts), at


FIRST, COUNT, BLOCKS = stages()

SMALL = {}
_at = 0
for _name, _n in (("glr", C * GLA_RANK), ("meta_2", C * META), ("gate_up", GLA_HEADS * GLA_DK), ("norm1", C), ("norm2", C),
                  ("norm_f", C), ("norm_mix", C), ("norm_ffn", C), ("norm_final", C), ("sb_norm", 4),
                  ("gla_norm", 4), ("b_gate", 2), ("conv", CONV_K * C)):
    SMALL[_name] = (_at, _n)
    _at += _n
SMALL_COLS = _at
KEYS_COLS = PH * NKEYS
KIWI_COLS = C * (2 * IDX_DIM + IDX_HEADS)

TILE0 = {}
_at = 0
for _name, _n in (("w_in_features", 16), ("w_in_values", 12), ("w_out", 8), ("w_peer_q", 8),
                  ("expert_u", NKEYS), ("w_in_2_features", 60), ("w_in_2_values", 12),
                  ("w_conv_out_2", 8), ("w_attn_out_2", 8), ("w_out_2", 8), ("w_gate_up_2", 2 * FF)):
    TILE0[_name] = _at
    _at += _n
BANKS = 4


def build(nc, stream, small_dram, keys_dram, kiwi_dram, x_dram, out_dram):
    with ExitStack() as ctx:
        def sb(name, shape, dt=F32):
            return ctx.enter_context(nc.sbuf_tensor(name, shape, dt))

        def sem(name):
            return ctx.enter_context(nc.semaphore(name))

        ps = ctx.enter_context(nc.psum_tensor("ps", [P, 8, 512], F32))

        work = sb("work", [P, NKEYS * REAL])
        ring = sb("ring", [P, RING, BLOCK])
        res = sb("res", [P, C, T])
        w_hi = sb("w_hi", [P, RING, BLOCK], F32R)
        w_lo = sb("w_lo", [P, RING, BLOCK], F32R)
        x_hi = sb("x_hi", [P, C * T], F32R)
        x_lo = sb("x_lo", [P, C * T], F32R)
        small = sb("small", [P, SMALL_COLS])
        ones = sb("ones", [P, P])
        zeros = sb("zeros", [P, P])
        ident = sb("ident", [P, P])
        iota = sb("iota", [P, NKEYS])
        onehot1 = sb("onehot1", [P, 2, 3, HALF_KEYS, GROUP], BF16)
        onehot2 = sb("onehot2", [P, 2, NKEYS, GROUP], BF16)
        iota_rows = sb("iota_rows", [P, NKEYS, GROUP], BF16)
        slots = sb("slots", [P, 5, REAL], BF16)
        spare = sb("spare", [P, 2 * T])
        var, rstd = spare[:, 0:T], spare[:, T:2 * T]
        gate_rest, gate_f = spare[:, 0:REAL], spare[:, REAL:2 * REAL]

        def tokens_of(x, n):
            return x[:, 0:C * n].rearrange("p (c t) -> p c t", c=C)

        x_parts = {n: (tokens_of(x_hi, n), tokens_of(x_lo, n)) for n in (T, REAL)}

        def view(name):
            at, n = SMALL[name]
            return small[:, at:at + n]

        glr_w = view("glr").rearrange("p (c n) -> p c n", c=C)
        meta_2 = view("meta_2").rearrange("p (c t) -> p c t", c=C)
        gate_up_w = view("gate_up")
        conv_w = view("conv").rearrange("p (k c) -> p k c", k=CONV_K)

        def carve(sizes):
            at, parts = 0, {}
            for name, n in sizes:
                parts[name] = work[:, at:at + n]
                at += n
            assert at <= NKEYS * REAL, at
            return parts

        W = 3 * P
        one = carve([("feat", 16 * T), ("ones_t", T), ("vtok", 3 * D), ("kbd", 4 * P), ("vbd", 512),
                     ("tri", P), ("bdtri", P), ("rep", P), ("win", 2 * P), ("blk64", P), ("hide", W), ("keep", W),
                     ("bdm", 512), ("zm", 9 * W), ("soft", 2 * W), ("sp", 2 * W), ("glrT", T),
                     ("gx", 2 * T), ("gl", 2 * T), ("b", 2 * T), ("nb", 2 * T), ("dq", 2 * REAL),
                     ("qt", 2 * REAL), ("ke", 2 * T), ("kt", 2 * T), ("A", 4 * W), ("A0", 4 * REAL),
                     ("sqh", D), ("rh", D), ("mix", C * REAL), ("sil", 4 * REAL), ("keys", KEYS_COLS), ("sq", C * T)])
        feat = one["feat"].rearrange("p (n t) -> p n t", n=16)
        vtok = one["vtok"].rearrange("p (k n) -> p k n", k=3)
        kbd = one["kbd"].rearrange("p (n t) -> p n t", n=4)
        zm = one["zm"].rearrange("p (h n) -> p h n", h=9)
        soft = one["soft"].rearrange("p (h n) -> p h n", h=2)
        sp_ = one["sp"].rearrange("p (h n) -> p h n", h=2)
        gx = one["gx"].rearrange("p (j t) -> p j t", j=2)
        gl = one["gl"].rearrange("p (j t) -> p j t", j=2)
        bcum = one["b"].rearrange("p (j t) -> p j t", j=2)
        nb = one["nb"].rearrange("p (j t) -> p j t", j=2)
        dq = one["dq"].rearrange("p (j t) -> p j t", j=2)
        qt = one["qt"].rearrange("p (j t) -> p j t", j=2)
        ke = one["ke"].rearrange("p (j t) -> p j t", j=2)
        kt = one["kt"].rearrange("p (j t) -> p j t", j=2)
        A = one["A"].rearrange("p (h n) -> p h n", h=4)
        A0 = one["A0"].rearrange("p (h n) -> p h n", h=4)
        mix = one["mix"].rearrange("p (c t) -> p c t", c=C)
        sil = one["sil"].rearrange("p (c t) -> p c t", c=4)
        keys_w = one["keys"].rearrange("p (h k) -> p h k", h=PH)
        sq1 = one["sq"]

        act_store = work[:, :].rearrange("p (i t) -> p i t", i=NKEYS)
        base = HALF_KEYS * REAL
        route = {}
        for name, n in (("qp", PH * REAL), ("sc", 16 * 256), ("tv", 256), ("pos", 256), ("ix", 512),
                        ("af", 256), ("bf", 256), ("eq", 2048), ("i1", 256), ("i2", 256), ("gate", 256),
                        ("sum", 16), ("rsum", 16), ("v", 32), ("cand", 256), ("ixf", 512),
                        ("pi", 256)):
            route[name] = work[:, base:base + n]
            base += n
        assert base <= NKEYS * REAL
        qp = route["qp"].rearrange("p (h t) -> p h t", h=PH)
        sc = route["sc"].rearrange("p (c n) -> p c n", c=16)

        two = carve([("feat2", 60 * T), ("v2", 3 * D), ("kidup", T), ("wi", 16), ("score", 2 * T),
                     ("rel", 2 * T), ("selb", 2 * T), ("top8", 16), ("vis", 144), ("lm", 2 * T), ("pr", 2 * T),
                     ("stat", 4 * 16), ("pT", 2 * W), ("ya", C * REAL), ("yc", C * REAL),
                     ("yco", C * REAL)])
        kiwi_w = two["ya"][:, 0:KIWI_COLS].rearrange("p (c n) -> p c n", c=C)
        feat2 = two["feat2"].rearrange("p (n t) -> p n t", n=60)
        v2 = two["v2"].rearrange("p (k n) -> p k n", k=3)
        score = two["score"].rearrange("p (t n) -> p t n", t=2)
        rel = two["rel"].rearrange("p (t n) -> p t n", t=2)
        selb = two["selb"].rearrange("p (t n) -> p t n", t=2)
        lm = two["lm"].rearrange("p (t n) -> p t n", t=2)
        pr = two["pr"].rearrange("p (t n) -> p t n", t=2)
        pT = two["pT"].rearrange("p (t n) -> p t n", t=2)
        ya = two["ya"].rearrange("p (c t) -> p c t", c=C)
        yc = two["yc"].rearrange("p (c t) -> p c t", c=C)
        yco = two["yco"].rearrange("p (c t) -> p c t", c=C)
        KF, CU, CC, QF, CB, GA, GB, QI = range(0, 64, 8)
        ffa = carve([("ffa", FF * REAL), ("sg", 2 * REAL), ("outT", C * REAL)])
        hidden = ffa["ffa"].rearrange("p (n t) -> p n t", n=FF)
        sg = ffa["sg"].rearrange("p (n t) -> p n t", n=2)
        outT = ffa["outT"].rearrange("p (c t) -> p c t", c=C)
        sq_late = work[:, NKEYS * REAL - C * T:]

        landed = [sem(f"landed{i}") for i in range(RING)]
        block_begun, w_hi_ready, w_lo_ready = sem("block_begun"), sem("w_hi_ready"), sem("w_lo_ready")
        x_hi_ready, x_lo_ready = sem("x_hi_ready"), sem("x_lo_ready")
        keys_landed, kiwi_landed = sem("keys_landed"), sem("kiwi_landed")
        x_landed, small_landed, stored = sem("x_landed"), sem("small_landed"), sem("stored")
        zeroed, consts = sem("zeroed"), sem("consts")
        vec_step, act_step, pool_step = sem("vec_step"), sem("act_step"), sem("pool_step")
        tile_ready = sem("tile_ready")
        tile_taken = [sem(f"tile_taken{i}") for i in range(BANKS)]
        squares_ready, sum_ready, var_ready, root_ready, normed = (
            sem(n) for n in ("squares_ready", "sum_ready", "var_ready", "root_ready", "normed"))
        glr_ready, glr_taken, gate_logits_ready, gate_biased, gate_soft, decay_ready = (
            sem(n) for n in ("glr_ready", "glr_taken", "gate_logits_ready", "gate_biased",
                             "gate_soft", "decay_ready"))
        kbd_ready, z0_ready, z_ready, z_taken, soft_ready, sp_ready, s_ready, d_ready, a_ready = (
            sem(n) for n in ("kbd_ready", "z0_ready", "z_ready", "z_taken", "soft_ready", "sp_ready",
                             "s_ready", "d_ready", "a_ready"))
        vbd_ready, sb_out_ready, sb_mixed, pe_used_sp = (
            sem(n) for n in ("vbd_ready", "sb_out_ready", "sb_mixed", "pe_used_sp"))
        head_sq, head_sum, head_var, head_root = (
            sem(n) for n in ("head_sq", "head_sum", "head_var", "head_root"))
        q_exp_in, q_exp, q_decayed, k_exp_in, k_exp, k_decayed, k_used = (
            sem(n) for n in ("q_exp_in", "q_exp", "q_decayed", "k_exp_in", "k_exp", "k_decayed", "k_used"))
        gla_masked, gla_meta_taken, gla_out_ready, silu_ready, gla_mixed = (
            sem(n) for n in ("gla_masked", "gla_meta_taken", "gla_out_ready", "silu_ready", "gla_mixed"))
        residual, meta_values_ready = sem("residual"), sem("meta_values_ready")
        key_scores_ready, key_scores_taken, tops_shifted, tops_exp, routed, slots_ready, slots_taken = (
            sem(n) for n in ("key_scores_ready", "key_scores_taken", "tops_shifted", "tops_exp", "routed",
                             "slots_ready", "slots_taken"))
        keys_matched, onehots_ready, gates_ready, gates_applied, y_ready = (
            sem(n) for n in ("keys_matched", "onehots_ready", "gates_ready", "gates_applied", "y_ready"))
        kiwi_ready, kiwi_taken, idx_ready, idx_taken, selected = (
            sem(n) for n in ("kiwi_ready", "kiwi_taken", "idx_ready", "idx_taken", "selected"))
        logits_ready, masked_ready, probs_ready, probs_scaled, probs_turned, turned_taken = (
            sem(n) for n in ("logits_ready", "masked_ready", "probs_ready", "probs_scaled",
                             "probs_turned", "turned_taken"))
        attn_ready, attn_taken, conv_ready, sigmoid_ready, conv_gated, mixed_ready = (
            sem(n) for n in ("attn_ready", "attn_taken", "conv_ready", "sigmoid_ready", "conv_gated",
                             "mixed_ready"))
        vis_ready = sem("vis_ready")

        ACTS0 = 2 * 3
        X_MIX = (ACTS0 + NKEYS) // 2
        X_CONV, X_ATTN, X_MIXED, X_FFN = X_MIX + 1, X_MIX + 2, X_MIX + 3, X_MIX + 4
        HIDDEN0 = 2 * (X_FFN + 1)

        def split_hi(act, b, turn=None):
            if b >= BLOCKS:
                return
            t, k = (0, b % RING) if turn is None else (turn, b % RING)
            act.wait_ge(landed[k], t * 16 + 16 * (b // RING + 1))
            if turn is not None or b >= RING:
                act.wait_ge(block_begun, t * RING + (b - RING + 2))
            nc.scalar.activation(w_hi[:, k, :], ring[:, k, :], ACT.Copy).then_inc(w_hi_ready, 1)

        def split_lo(dve, b, turn=None):
            if b >= BLOCKS:
                return
            t, k = (0, b % RING) if turn is None else (turn, b % RING)
            dve.wait_ge(w_hi_ready, t * RING + (b + 1))
            nc.vector.tensor_tensor(w_lo[:, k, :], ring[:, k, :], w_hi[:, k, :].bitcast(F32),
                                    ALU.subtract).then_inc(w_lo_ready, 1)

        def operand_hi(act, n, src, ready, value):
            tokens = src.shape[2]
            for half in range(2):
                if ready is not None:
                    act.wait_ge(ready, value + half)
                c = slice(4 * half, 4 * half + 4)
                nc.scalar.activation(x_parts[tokens][0][:, c, :], src[:, c, :], ACT.Copy).then_inc(x_hi_ready, 1)

        def operand_lo(dve, n, src):
            tokens = src.shape[2]
            for half in range(2):
                dve.wait_ge(x_hi_ready, 2 * n + half + 1)
                c = slice(4 * half, 4 * half + 4)
                nc.vector.tensor_tensor(x_parts[tokens][1][:, c, :], src[:, c, :],
                                        x_parts[tokens][0][:, c, :].bitcast(F32),
                                        ALU.subtract).then_inc(x_lo_ready, 1)

        def bank_is_free(eng, g, turn=None):
            if turn is not None:
                eng.wait_ge(tile_taken[g % BANKS], turn + g // BANKS)
            elif g >= BANKS:
                eng.wait_ge(tile_taken[g % BANKS], g // BANKS)

        def tiles_are_taken(eng, g):
            for bank in range(BANKS):
                eng.wait_ge(tile_taken[bank], (g - bank + BANKS - 1) // BANKS)

        def bank_of(g):
            return ps[:, g % BANKS, :]

        block = ctx.enter_context(nc.Block())

        @block.sync
        def _(sp):
            sp.dma_start(res[:, :, :].rearrange("p c t -> p (c t)"), x_dram).then_inc(x_landed, 16)
            sp.dma_start(small[:, :], small_dram).then_inc(small_landed, 16)
            for b in range(RING):
                sp.dma_start(ring[:, b, :], stream[b]).then_inc(landed[b], 16)
            sp.dma_start(one["keys"], keys_dram).then_inc(keys_landed, 16)
            with sp.Fori(1, BLOCKS // RING) as i:
                for k in range(RING):
                    sp.wait_ge(w_lo_ready, i * RING + (k + 1 - RING))
                    sp.dma_start(ring[:, k, :], stream[i * RING + k]).then_inc(landed[k], 16)
            for b in range(BLOCKS // RING * RING, BLOCKS):
                sp.wait_ge(w_lo_ready, b + 1 - RING)
                sp.dma_start(ring[:, b % RING, :], stream[b]).then_inc(landed[b % RING], 16)
            for half in range(2):
                sp.wait_ge(normed, 11 + half)
                part = slice(half * 4 * REAL, (half + 1) * 4 * REAL)
                sp.dma_start(out_dram[:, part], outT.rearrange("p c t -> p (c t)")[:, part]).then_inc(stored, 16)
            sp.wait_ge(stored, 32)

        @block.gpsimd
        def _(pool):
            g = nc.gpsimd
            for tile, value in ((ones[:, :], 1.0), (one["ones_t"], 1.0), (zeros[:, :], 0.0), (ident[:, :], 0.0),
                                (one["tri"], 1.0), (one["rep"], 0.0), (one["bdtri"], 1.0), (one["win"], 0.0),
                                (one["blk64"], 1.0), (one["hide"], 0.0), (one["keep"], 1.0),
                                (one["bdm"], 1.0), (one["kbd"], 0.0)):
                g.memset(tile, value).then_inc(zeroed, 1)
            pool.wait_ge(zeroed, 13)
            g.iota(iota[:, :], [[1, NKEYS]], base=0, channel_multiplier=0,
                   allow_small_or_imprecise_dtypes=True).then_inc(consts, 1)
            g.affine_select(out=ident[:, :], in_=ident[:, :], compare_op=ALU.not_equal, fill=1.0, base=0,
                            pattern=[[-1, P]], channel_multiplier=1).then_inc(consts, 1)
            g.affine_select(out=one["tri"], in_=one["tri"], compare_op=ALU.is_ge, fill=0.0, base=0,
                            pattern=[[-1, P]], channel_multiplier=1).then_inc(consts, 1)
            v = one["rep"][0:META, :].rearrange("p (h m) -> p h m", m=META)
            g.affine_select(out=v, in_=v, compare_op=ALU.not_equal, fill=1.0, base=0,
                            pattern=[[0, P // META], [-1, META]], channel_multiplier=1).then_inc(consts, 1)
            g.memset(one["win"][:, P - META:P], 1.0).then_inc(consts, 1)
            for name, fill, off in (("keep", 0.0, 0), ("hide", NEG, -1)):
                for at, n in ((0, 2 * P), (2 * P, P)):
                    v = one[name][:, at:at + n]
                    g.affine_select(out=v, in_=v, compare_op=ALU.is_ge, fill=fill, base=off,
                                    pattern=[[1, n]], channel_multiplier=-1).then_inc(consts, 1)
            for n, (name, groups, size, inner) in enumerate((("bdtri", 8, META, META), ("blk64", 2, 64, 64),
                                                             ("bdm", 8, META, 64))):
                v = one[name].rearrange("p (g n) -> p g n", g=groups)
                g.affine_select(out=v, in_=v, compare_op=ALU.is_ge, fill=0.0, base=size - 1,
                                pattern=[[size, groups], [0, inner]],
                                channel_multiplier=-1).then_inc(pool_step, 1)
                pool.wait_ge(pool_step, n + 1)
                g.affine_select(out=v, in_=v, compare_op=ALU.is_ge, fill=0.0, base=0,
                                pattern=[[-size, groups], [-1 if name == "bdtri" else 0, inner]],
                                channel_multiplier=1).then_inc(consts, 1)
            pool.wait_ge(y_ready, 1)
            g.memset(two["vis"], 0.0).then_inc(pool_step, 1)
            pool.wait_ge(pool_step, 4)
            g.affine_select(out=two["vis"], in_=two["vis"], compare_op=ALU.is_ge, fill=NEG, base=META,
                            pattern=[[-1, META + P]], channel_multiplier=1).then_inc(vis_ready, 1)
            pool.wait_ge(sigmoid_ready, 1)
            tiles_are_taken(pool, TILE0["w_conv_out_2"] + 8)
            g.tensor_tensor(yco, yco, feat2[:, GB:GB + 8, META:], ALU.mult).then_inc(conv_gated, 1)

        CONSTS = 12

        @block.tensor
        def _(pe):
            mm = nc.tensor.matmul

            def norm(k, sq, tokens):
                pe.wait_ge(squares_ready, k + 1)
                for c in range(C):
                    last = mm(ps[:, 7, 0:tokens], ones[:, 0:P], sq[:, c, :], start=c == 0, stop=c == C - 1)
                last.then_inc(sum_ready, 1)

            def parts_ready(b, turn=0):
                pe.wait_ge(w_lo_ready, turn * RING + (b + 1))

            def operand_ready(n):
                pe.wait_ge(x_lo_ready, 2 * n + 2)

            def column_block(b, g, tokens, turn=0, tile_turn=None, owed=False):
                parts_ready(b, turn)
                bank_is_free(pe, g, tile_turn)
                k, (xh, xl), out = b % RING, x_parts[tokens], bank_of(g)[:, 0:tokens]
                for c in range(C):
                    w = w_hi[:, k, c * P:(c + 1) * P]
                    i = mm(out, w, xh[:, c, :], start=c == 0, stop=False)
                    if c == 0:
                        i.then_inc(block_begun, 1)
                    i = mm(out, w, xl[:, c, :], start=False, stop=False)
                    if c == 0 and owed:
                        i.then_inc(block_begun, 1)
                for c in range(C):
                    last = mm(out, w_lo[:, k, c * P:(c + 1) * P], xh[:, c, :], start=False, stop=c == C - 1)
                last.then_inc(tile_ready, 1)

            def columns(name, tokens, owed=False):
                b0, g0, n = FIRST[name], TILE0[name], COUNT[name]
                looped = n // RING if n > 4 * RING else 0
                if looped:
                    with pe.Fori(0, looped) as i:
                        for k in range(RING):
                            column_block(b0 + k, g0 + k, tokens, i, i)
                for k in range(looped * RING, n):
                    column_block(b0 + k, g0 + k, tokens, owed=owed and k == 0)

            def value_blocks(name):
                xh, xl = x_parts[T]
                for n in range(COUNT[name] // 2):
                    b, g = FIRST[name] + 2 * n, TILE0[name] + 3 * n
                    k = b % RING
                    parts_ready(b + 1)
                    for j in range(3):
                        bank_is_free(pe, g + j)
                        out = bank_of(g + j)[:, 0:2 * COLS].rearrange("p (k n) -> p k n", k=2)
                        at = META + (j - 1) * P if j else 0
                        for c in range(C):
                            hi = w_hi[:, k:k + 2, c * P:(c + 1) * P]
                            lo = w_lo[:, k:k + 2, c * P:(c + 1) * P]
                            i = mm(out, xh[:, c, at:at + P], hi, start=c == 0, stop=False)
                            if c == j == 0:
                                i.then_inc(block_begun, 1)
                            i = mm(out, xh[:, c, at:at + P], lo, start=False, stop=False)
                            if c == j == 0 and n:
                                i.then_inc(block_begun, 1)
                            last = mm(out, xl[:, c, at:at + P], hi, start=False, stop=c == C - 1)
                        last.then_inc(tile_ready, 1)

            pe.wait_ge(zeroed, 13)
            pe.wait_ge(consts, CONSTS)
            norm(0, sq1.rearrange("p (c t) -> p c t", c=C), T)
            pe.wait_ge(normed, 2)
            pe.wait_ge(small_landed, 16)
            xn = tokens_of(sq1, T)
            for c in range(C):
                last = mm(ps[0:GLA_RANK, 6, 0:T], glr_w[:, c, :], xn[:, c, :], start=c == 0,
                          stop=c == C - 1)
            last.then_inc(glr_ready, 1)
            operand_ready(0)
            columns("w_in_features", T)
            pe.wait_ge(glr_taken, 1)
            for j in range(2):
                last = mm(ps[:, 4 + j, 0:T], gate_up_w[0:GLA_RANK, j * P:(j + 1) * P],
                          one["glrT"][0:GLA_RANK, :], start=True, stop=True)
            last.then_inc(gate_logits_ready, 1)
            value_blocks("w_in_values")
            tiles_are_taken(pe, TILE0["w_out"])

            pe.wait_ge(kbd_ready, 1)
            pe.wait_ge(gate_biased, 2)
            for p in range(4):
                last = mm(ps[:, 4, 0:REAL], kbd[:, p, :], feat[:, p, META:], start=p == 0, stop=p == 3)
            last.then_inc(z0_ready, 1)

            mm(ps[:, 2, :], one["rep"][0:META, :], vtok[0:META, 0, 0:512], start=True,
               stop=True).then_inc(meta_values_ready, 1)

            def head_scores(h):
                rows = slice(64 * (h % 2), 64 * (h % 2) + 64)
                q, k = feat[rows, h // 2, :], feat[rows, 4 + h // 2, :]
                if h >= 2:
                    pe.wait_ge(z_taken, h - 1)
                z = ps[:, 5 + h % 2, :]
                mm(z[:, 0:2 * P], k[:, META:META + P], q[:, META:], start=True, stop=True)
                mm(z[:, 2 * P:W], k[:, META + P:], q[:, META + P:], start=True,
                   stop=True).then_inc(z_ready, 1)

            def suffix_sums(h):
                pe.wait_ge(sp_ready, h + 1)
                if h < 8:
                    if h >= 2:
                        pe.wait_ge(d_ready, h - 1)
                    bank = ps[:, 7 if h % 2 else 0, :]
                    s = sp_[:, h % 2, :]
                    mm(bank[:, 0:W], one["tri"], s, start=True, stop=True)
                    mm(bank[:, P:2 * P], ones[:, 0:P], s[:, 2 * P:W], start=False, stop=True,
                       skip_group_check=True).then_inc(s_ready, 1)
                    at = P - META - META * h
                    mm(ps[:, 1, 0:2 * P], one["win"][:, at:at + P], s[:, 0:2 * P], start=h == 0, stop=False)
                    mm(ps[:, 1, P:2 * P], one["win"][:, at:at + P], s[:, 2 * P:W], start=False,
                       stop=False).then_inc(pe_used_sp, 1)
                else:
                    mm(ps[:, 1, 0:2 * P], one["bdtri"], sp_[:, 0, 0:2 * P], start=False,
                       stop=True).then_inc(s_ready, 1)

            head_scores(0)
            for h in range(8):
                if h < 7:
                    head_scores(h + 1)
                suffix_sums(h)
            suffix_sums(8)
            pe.wait_ge(a_ready, 9)
            pe.wait_ge(vbd_ready, 1)
            for h in range(8):
                o = ps[64 * (h % 2):64 * (h % 2) + 64, 2 + h // 4, 256 * (h // 2 % 2):256 * (h // 2 % 2) + 256]
                cols = slice(64 * h, 64 * h + 64)
                mm(o, vtok[:, 1, cols], zm[:, h, 0:2 * P], start=True, stop=False)
                mm(o[:, P:2 * P], vtok[:, 2, cols], zm[:, h, 2 * P:W], start=False, stop=False)
                last = mm(o, one["vbd"][:, cols], zm[:, 8, 0:2 * P], start=False, stop=True)
            last.then_inc(sb_out_ready, 1)
            pe.wait_ge(head_sq, 1)
            for j in range(2):
                last = mm(ps[:, 4 + j, :], one["blk64"], one["sqh"][:, 512 * j:512 * j + 512],
                          start=True, stop=True)
            last.then_inc(head_sum, 1)

            pe.wait_ge(q_decayed, 1)
            pe.wait_ge(sb_mixed, 1)
            for i in range(SUBS):
                for j in range(2):
                    n = 2 * i + j
                    pe.wait_ge(k_decayed, n + 1)
                    for e in range(2):
                        h = 2 * j + e
                        rows = slice(64 * e, 64 * e + 64)
                        q = qt[rows, j, SUB * i:SUB * i + SUB]
                        at = 256 * j + SUB * i
                        mm(ps[:, 4 + h, SUB * i:SUB * i + SUB], kt[rows, j, META:META + P], q,
                           start=True, stop=True)
                        last = mm(ps[0:META, e, at:at + SUB], kt[rows, j, 0:META], q, start=True, stop=True)
                        if i >= SUBS // 2:
                            last = mm(ps[:, 4 + h, P + SUB * i:P + SUB * i + SUB], kt[rows, j, META + P:], q,
                                      start=True, stop=True)
                    last.then_inc(k_used, 1)
            pe.wait_ge(gla_masked, 4)
            pe.wait_ge(gla_meta_taken, 1)
            for h in range(GLA_HEADS):
                o = ps[:, 2 + h // 2, 256 * (h % 2):256 * (h % 2) + 256]
                cols = slice(512 + GLA_DV * h, 512 + GLA_DV * h + GLA_DV)
                mm(o, vtok[:, 1, cols], A[:, h, 0:2 * P], start=True, stop=False)
                mm(o[:, P:2 * P], vtok[:, 2, cols], A[:, h, 2 * P:W], start=False, stop=False)
                last = mm(o, vtok[0:META, 0, cols], A0[0:META, h, :], start=False, stop=True)
            last.then_inc(gla_out_ready, 1)
            pe.wait_ge(head_sq, 2)
            for j in range(2):
                last = mm(ps[:, 4 + j, :], ones[:, 0:P], one["sqh"][:, 512 * j:512 * j + 512],
                          start=True, stop=True)
            last.then_inc(head_sum, 1)

            operand_ready(1)
            columns("w_out", REAL, owed=True)
            norm(1, sq1[:, 0:C * REAL].rearrange("p (c t) -> p c t", c=C), REAL)
            operand_ready(2)
            columns("w_peer_q", REAL)
            pe.wait_ge(keys_landed, 16)
            tiles_are_taken(pe, TILE0["expert_u"])
            for h in range(PH):
                if h >= 2:
                    pe.wait_ge(key_scores_taken, 2 * (h - 1))
                for half in range(2):
                    rows = slice(64 * half, 64 * half + 64)
                    for t in range(2):
                        last = mm(ps[:, 4 + 2 * (h % 2) + half, t * P:t * P + P], qp[rows, h, t * P:t * P + P],
                                  keys_w[rows, h, :], start=True, stop=True)
                    last.then_inc(key_scores_ready, 1)

            b0, g0 = FIRST["expert_u"], TILE0["expert_u"]

            def gate_tables(n, k, bank0):
                pe.wait_ge(onehots_ready, n + 1)
                for j in range(GROUP):
                    for part in range(3):
                        last = mm(ps[:, bank0 + k, HALF_KEYS * j:HALF_KEYS * (j + 1)], onehot2[:, k, :, j],
                                  onehot1[:, k, part, :, j], start=part == 0, stop=part == 2)
                last.then_inc(gates_ready, 1)

            with pe.Fori(0, 16) as i:
                for k in range(RING):
                    column_block(b0 + k, g0 + k, REAL, i, i)
            pe.wait_ge(routed, 1)
            for t in range(2):
                for j, name in enumerate(("gate", "i1", "i2")):
                    last = nc.tensor.transpose(ps[:, 4 + t, P * j:P * j + P],
                                               route[name][:, t * P:(t + 1) * P], ident[:, :])
            last.then_inc(slots_ready, 1)
            pe.wait_ge(slots_taken, 2)
            with pe.Fori(16, 32) as i:
                for k in range(RING):
                    column_block(b0 + k, g0 + k, REAL, i, i)
                    if k % 2:
                        gate_tables(i * 2 + (k // 2 - 32), k // 2, 4)

            tiles_are_taken(pe, TILE0["w_in_2_features"])
            pe.wait_ge(gates_applied, 32)

            def open_sums():
                for n in range(4):
                    mm(ps[:, 4 + n, :], zeros[:, :], res[:, 0:2, 0:REAL], start=True, stop=True)

            xh4, xl4 = x_hi[:, 0:RING * REAL], x_lo[:, 0:RING * REAL]

            def row_block(b, turn=0, n=0):
                parts_ready(b, turn)
                pe.wait_ge(x_lo_ready, turn * RING + (n + 1))
                k = b % RING
                xh, xl = xh4[:, k * REAL:(k + 1) * REAL], xl4[:, k * REAL:(k + 1) * REAL]
                for n, (w, x) in enumerate([(w_hi, xh), (w_hi, xl), (w_lo, xh)]):
                    for m in range(C):
                        i = mm(ps[:, 4 + m // 2, 256 * (m % 2):256 * (m % 2) + 256], w[:, k, m * P:(m + 1) * P],
                               x, start=False, stop=True, skip_group_check=True)
                        if n == m == 0:
                            i.then_inc(block_begun, 1)

            def close_sums():
                mm(ps[:, 7, 0:1], zeros[:, :], ones[:, 0:1], start=False, stop=True,
                   skip_group_check=True).then_inc(y_ready, 1)

            open_sums()
            b0 = FIRST["expert_v"]
            with pe.Fori(0, 16) as i:
                for k in range(RING):
                    row_block(b0 + k, i, ACTS0 + k)
                    if k % 2:
                        gate_tables(i * 2 + (32 + k // 2), k // 2, 0)
            with pe.Fori(16, 32) as i:
                for k in range(RING):
                    row_block(b0 + k, i, ACTS0 + k)
            close_sums()

            sq = sq_late.rearrange("p (c t) -> p c t", c=C)
            sq_r = sq_late[:, 0:C * REAL].rearrange("p (c t) -> p c t", c=C)
            norm(2, sq_r, REAL)
            norm(3, sq, T)
            operand_ready(X_MIX)
            columns("w_in_2_features", T)
            xn = tokens_of(sq_late, T)
            pe.wait_ge(kiwi_landed, 16)
            for c in range(C):
                mm(ps[:, 4, 0:T], kiwi_w[:, c, 0:P], xn[:, c, :], start=c == 0, stop=c == C - 1)
            for t in range(2):
                for c in range(C):
                    last = mm(ps[:, 5, 8 * t:8 * t + 8], xn[:, c, META + P * t:META + P * t + P],
                              kiwi_w[:, c, P:P + IDX_HEADS], start=c == 0, stop=c == C - 1)
            last.then_inc(kiwi_ready, 1)
            value_blocks("w_in_2_values")
            pe.wait_ge(kiwi_taken, 2)
            tiles_are_taken(pe, TILE0["w_in_2_values"])
            for t in range(2):
                seen = META + P * (t + 1)
                for h in range(IDX_HEADS):
                    n = 8 * t + h
                    rows = slice(64 * (h % 2), 64 * (h % 2) + 64)
                    if n >= 2:
                        pe.wait_ge(idx_taken, n - 1)
                    mm(ps[:, 4 + n % 2, 0:seen], feat2[rows, QI + h // 2, META + P * t:META + P * t + P],
                       two["kidup"][rows, 0:seen], start=True, stop=True).then_inc(idx_ready, 1)
            operand_ready(X_CONV)
            columns("w_conv_out_2", REAL, owed=True)
            tiles_are_taken(pe, TILE0["w_attn_out_2"])
            pe.wait_ge(idx_taken, 16)

            def attention_scores(n):
                t, h = n // 8, n % 8
                seen = META + P * (t + 1)
                if n >= 2:
                    pe.wait_ge(masked_ready, n - 1)
                mm(ps[:, n % 2, 0:seen], feat2[:, QF + h, META + P * t:META + P * t + P],
                   feat2[:, KF + h, 0:seen], start=True, stop=True).then_inc(logits_ready, 1)

            def attention_values(n):
                t, h = n // 8, n % 8
                pe.wait_ge(probs_scaled, n + 1)
                if n >= 2:
                    pe.wait_ge(turned_taken, n - 1)
                turned = ps[:, 2 + n % 2, :]
                p = pr[:, n % 2, :]
                last = nc.tensor.transpose(turned[0:META, 0:P], p[:, 0:META], ident[:, :])
                for c in range(t + 1):
                    last = nc.tensor.transpose(turned[:, P * (c + 1):P * (c + 2)],
                                               p[:, META + P * c:META + P * (c + 1)], ident[:, :])
                last.then_inc(probs_turned, 1)
                pe.wait_ge(turned_taken, n + 1)
                o = ps[:, 4 + 2 * t + h // 4, P * (h % 4):P * (h % 4) + P]
                cols = slice(P * h, P * h + P)
                mm(o, v2[0:META, 0, cols], pT[0:META, n % 2, 0:P], start=True, stop=False)
                for c in range(t + 1):
                    last = mm(o, v2[:, 1 + c, cols], pT[:, n % 2, P * (c + 1):P * (c + 2)], start=False,
                              stop=c == t)
                last.then_inc(attn_ready, 1)

            attention_scores(0)
            for n in range(16):
                if n < 15:
                    attention_scores(n + 1)
                attention_values(n)
            operand_ready(X_ATTN)
            columns("w_attn_out_2", REAL)
            operand_ready(X_MIXED)
            columns("w_out_2", REAL)
            norm(4, sq_r, REAL)
            operand_ready(X_FFN)
            columns("w_gate_up_2", REAL)
            open_sums()
            b0, turns = FIRST["w_down_2"], FF // RING
            with pe.Fori(0, turns) as i:
                for k in range(RING):
                    row_block(b0 + k, i, HIDDEN0 + k)
            for k in range(turns * RING, FF):
                row_block(b0 + k, 0, HIDDEN0 + k)
            close_sums()
            norm(5, sq_r, REAL)

        @block.scalar
        def _(act):
            a = nc.scalar.activation
            steps = [0]

            def link(ins):
                steps[0] += 1
                ins.then_inc(act_step, 1)
                act.wait_ge(act_step, steps[0])


            def norm(k, src, sq):
                a(sq, src, ACT.Square).then_inc(squares_ready, 1)
                act.wait_ge(var_ready, k + 1)
                n = T if k in (0, 3) else REAL
                a(rstd[:, 0:n], var[:, 0:n], ACT.Sqrt).then_inc(root_ready, 1)

            def take(g, out, tokens, turn=0, rows=P):
                act.wait_ge(tile_ready, turn + g + 1)
                a(out, bank_of(g)[0:rows, 0:tokens], ACT.Copy).then_inc(tile_taken[g % BANKS], 1)

            def ahead(b, turn=None):
                split_hi(act, b + LEAD, turn)

            def value_tiles(name, out):
                for n in range(COUNT[name] // 2):
                    ahead(FIRST[name] + 2 * n)
                    ahead(FIRST[name] + 2 * n + 1)
                    for j in range(n % 2, 3, 2):
                        take(TILE0[name] + 3 * n + j, out[:, j, 2 * COLS * n:2 * COLS * (n + 1)], 2 * COLS)

            act.wait_ge(x_landed, 16)
            norm(0, res[:, :, :], tokens_of(sq1, T))
            ahead(-2)
            ahead(-1)
            operand_hi(act, 0, tokens_of(sq1, T), normed, 1)
            act.wait_ge(glr_ready, 1)
            a(one["glrT"][0:GLA_RANK, :], ps[0:GLA_RANK, 6, 0:T], ACT.Copy).then_inc(glr_taken, 1)
            for n in range(16):
                ahead(n)
                if n % 2 == 0:
                    take(n, feat[:, n, :], T)
            value_tiles("w_in_values", vtok)
            act.wait_ge(gate_biased, 2)
            link(a(gl, gx, ACT.Abs))
            link(a(gl, gl, ACT.Exp, scale=-1.0))
            a(gl, gl, ACT.Ln, bias=1.0).then_inc(gate_soft, 1)

            def softness(n, cols):
                act.wait_ge(z_taken, n + 1)
                if n >= 2:
                    act.wait_ge(sp_ready, n - 1)
                s = soft[:, n % 2, 0:cols]
                link(a(s, zm[:, n, 0:cols], ACT.Abs))
                link(a(s, s, ACT.Exp, scale=-1.0))
                a(s, s, ACT.Ln, bias=1.0).then_inc(soft_ready, 1)

            def weights(n, cols):
                act.wait_ge(d_ready, n + 1)
                a(zm[:, n, 0:cols], zm[:, n, 0:cols], ACT.Exp).then_inc(a_ready, 1)

            softness(0, W)
            for n in range(1, 9):
                softness(n, W if n < 8 else REAL)
                weights(n - 1, W)
            weights(8, REAL)

            def head_norm(k, ready):
                act.wait_ge(ready, 1)
                a(one["sqh"].rearrange("p (b n) -> p b n", b=2), ps[:, 2:4, :], ACT.Square).then_inc(head_sq, 1)
                act.wait_ge(head_var, k + 1)
                a(one["rh"], one["rh"], ACT.Sqrt).then_inc(head_root, 1)

            head_norm(0, sb_out_ready)
            act.wait_ge(q_exp_in, 1)
            a(dq, dq, ACT.Exp).then_inc(q_exp, 1)
            for n in range(2 * SUBS):
                seen = META + P * (1 + (n >= SUBS))
                act.wait_ge(k_exp_in, n + 1)
                a(ke[:, n % 2, 0:seen], ke[:, n % 2, 0:seen], ACT.Exp).then_inc(k_exp, 1)
            act.wait_ge(k_used, 2 * SUBS)
            a(A0[0:META, :, :].rearrange("p (j e) t -> p e j t", e=2),
              ps[0:META, 0:2, :].rearrange("p e (j t) -> p e j t", j=2), ACT.Copy).then_inc(gla_meta_taken, 1)
            a(sil, feat[:, 12:16, META:], ACT.Silu).then_inc(silu_ready, 1)
            head_norm(1, gla_out_ready)

            act.wait_ge(gla_mixed, 1)
            operand_hi(act, 1, mix, None, 0)
            for n in range(8):
                ahead(FIRST["w_out"] + n)
            tiles_are_taken(act, TILE0["w_out"] + 8)
            norm(1, res[:, :, META:], tokens_of(sq1, REAL))
            operand_hi(act, 2, tokens_of(sq1, REAL), normed, 3)
            for h in range(PH):
                ahead(FIRST["w_peer_q"] + h)
                take(TILE0["w_peer_q"] + h, qp[:, h, :], REAL)
            for n in range(2 * PH):
                h, half = n // 2, n % 2
                act.wait_ge(key_scores_ready, n + 1)
                a(sc[:, h:h + 9:8, half * P:half * P + P],
                  ps[:, 4 + 2 * (h % 2) + half, 0:2 * P].rearrange("p (t k) -> p t k", t=2),
                  ACT.Copy).then_inc(key_scores_taken, 1)

            b0, g0 = FIRST["expert_u"], TILE0["expert_u"]

            def experts(first, last):
                with act.Fori(first, last) as i:
                    for k in range(RING):
                        ahead(b0 + k, i)
                        act.wait_ge(tile_ready, i * RING + (g0 + k + 1))
                        a(act_store[:, i * RING + k, :], bank_of(g0 + k)[:, 0:REAL],
                          ACT.Gelu).then_inc(tile_taken[(g0 + k) % BANKS], 1)

            experts(0, 13)
            act.wait_ge(tops_shifted, 1)
            a(route["gate"], route["gate"], ACT.Exp).then_inc(tops_exp, 1)
            experts(13, 16)
            act.wait_ge(slots_ready, 1)
            a(gate_f.rearrange("p (t n) -> p t n", t=2), ps[:, 4:6, 0:P], ACT.Copy).then_inc(slots_taken, 1)
            a(slots[:, 3:5, :].rearrange("p j (t n) -> p t j n", t=2),
              ps[:, 4:6, P:3 * P].rearrange("p t (j n) -> p t j n", j=2), ACT.Copy).then_inc(slots_taken, 1)
            experts(16, 32)

            def row_operand(src, b, turn=None):
                ahead(b, turn)
                k = b % RING
                a(x_hi[:, k * REAL:(k + 1) * REAL], src, ACT.Copy).then_inc(x_hi_ready, 1)

            b0 = FIRST["expert_v"]
            for half in range(2):
                act.wait_ge(gates_applied, 32 * (half + 1))
                with act.Fori(16 * half, 16 * half + 16) as i:
                    for k in range(RING):
                        row_operand(act_store[:, i * RING + k, :], b0 + k, i)

            sq = tokens_of(sq_late, T)
            sq_r = tokens_of(sq_late, REAL)
            act.wait_ge(residual, 4)
            act.dma_start(two["ya"][:, 0:KIWI_COLS], kiwi_dram).then_inc(kiwi_landed, 16)
            norm(2, res[:, :, META:], sq_r)
            act.wait_ge(normed, 6)
            norm(3, res[:, :, :], sq)
            operand_hi(act, X_MIX, sq, normed, 7)
            b0, g0 = FIRST["w_in_2_features"], TILE0["w_in_2_features"]
            with act.Fori(0, 15) as i:
                for k in range(RING):
                    ahead(b0 + k, i)
                    if k % 2 == 0:
                        take(g0 + k, feat2[:, i * RING + k, :], T, i * RING)
            act.wait_ge(kiwi_ready, 1)
            a(two["kidup"], ps[:, 4, 0:T], ACT.Copy).then_inc(kiwi_taken, 1)
            a(two["wi"], ps[:, 5, 0:16], ACT.Copy, scale=IDX_SCALE).then_inc(kiwi_taken, 1)
            value_tiles("w_in_2_values", v2)
            tiles_are_taken(act, TILE0["w_in_2_values"])
            a(feat2[:, GA:GA + 16, :], feat2[:, GA:GA + 16, :], ACT.Sigmoid).then_inc(sigmoid_ready, 1)
            act.wait_ge(conv_ready, 1)
            operand_hi(act, X_CONV, yc, None, 0)
            for n in range(8):
                ahead(FIRST["w_conv_out_2"] + n)
                take(TILE0["w_conv_out_2"] + n, yco[:, n, :], REAL)

            stat = two["stat"]
            def probs(n):
                seen = META + P * (n // 8 + 1)
                act.wait_ge(masked_ready, n + 1)
                if n >= 2:
                    act.wait_ge(probs_turned, n - 1)
                a(pr[:, n % 2, 0:seen], lm[:, n % 2, 0:seen], ACT.Exp, bias=stat[:, 16 + n:17 + n],
                  accum_out=stat[:, 32 + n:33 + n]).then_inc(probs_ready, 1)

            def turned(n):
                t = n // 8
                act.wait_ge(probs_turned, n + 1)
                if n >= 2:
                    act.wait_ge(attn_ready, n - 1)
                link(a(pT[0:META, n % 2, 0:P], ps[0:META, 2 + n % 2, 0:P], ACT.Copy))
                end = P * (t + 2)
                a(pT[:, n % 2, P:end], ps[:, 2 + n % 2, P:end], ACT.Copy).then_inc(turned_taken, 1)

            def outputs(n):
                t, q = n // 2, n % 2
                act.wait_ge(attn_ready, 4 * (n + 1))
                a(ya[:, 4 * q:4 * q + 4, P * t:P * t + P],
                  ps[:, 4 + n, :].rearrange("p (h m) -> p h m", h=4), ACT.Copy).then_inc(attn_taken, 1)

            probs(0)
            for n in range(16):
                if n < 15:
                    probs(n + 1)
                turned(n)
                if n % 4 == 0 and n:
                    outputs(n // 4 - 1)
            outputs(3)

            act.wait_ge(attn_taken, 4)
            operand_hi(act, X_ATTN, ya, None, 0)
            for n in range(8):
                ahead(FIRST["w_attn_out_2"] + n)
            operand_hi(act, X_MIXED, ya, mixed_ready, 1)
            for n in range(8):
                ahead(FIRST["w_out_2"] + n)
            tiles_are_taken(act, TILE0["w_out_2"] + 8)
            norm(4, res[:, :, META:], sq_r)
            operand_hi(act, X_FFN, tokens_of(sq_late, REAL), normed, 9)
            b0, g0 = FIRST["w_gate_up_2"], TILE0["w_gate_up_2"]

            def gate_tiles(turn=None):
                t = 0 if turn is None else turn
                for k in range(RING):
                    ahead(b0 + k, t)
                    if k < 2:
                        g = g0 + k
                        act.wait_ge(tile_ready, t * RING + (g + 1))
                        if turn is not None:
                            act.wait_ge(tile_taken[(g + 2) % BANKS], t + (g + 2) // BANKS)
                        a(sg[:, k, :], bank_of(g)[:, 0:REAL], ACT.Silu).then_inc(tile_taken[g % BANKS], 1)

            gate_tiles()
            with act.Fori(1, FF // 2) as i:
                gate_tiles(i)
            tiles_are_taken(act, g0 + 2 * FF)
            b0 = FIRST["w_down_2"]
            with act.Fori(0, FF // RING) as i:
                for k in range(RING):
                    row_operand(hidden[:, i * RING + k, :], b0 + k, i)
            for n in range(FF // RING * RING, FF):
                row_operand(hidden[:, n, :], b0 + n)
            act.wait_ge(residual, 8)
            norm(5, res[:, :, META:], sq_r)

        @block.vector
        def _(dve):
            v = nc.vector
            steps = [0]

            def link(ins):
                steps[0] += 1
                ins.then_inc(vec_step, 1)
                dve.wait_ge(vec_step, steps[0])

            tt, ts, stt = v.tensor_tensor, v.tensor_scalar, v.scalar_tensor_tensor

            def norm(k, src, gain, dst):
                n = T if k in (0, 3) else REAL
                at = SMALL[gain][0]
                dve.wait_ge(sum_ready, k + 1)
                ts(var[:, 0:n], ps[:, 7, 0:n], 1.0 / D, EPS, ALU.mult, ALU.add).then_inc(var_ready, 1)
                dve.wait_ge(root_ready, k + 1)
                link(v.reciprocal(rstd[:, 0:n], rstd[:, 0:n]))
                for c in range(C):
                    i = stt(dst[:, c, :], src[:, c, :], small[:, at + c:at + c + 1], rstd[:, 0:n], ALU.mult, ALU.mult)
                    if c % 4 == 3:
                        i.then_inc(normed, 1)

            def take(g, out, tokens, turn=0, rows=P):
                dve.wait_ge(tile_ready, turn + g + 1)
                v.tensor_copy(out, bank_of(g)[0:rows, 0:tokens]).then_inc(tile_taken[g % BANKS], 1)

            dve.wait_ge(x_landed, 16)
            dve.wait_ge(small_landed, 16)
            def ahead(b, turn=None):
                split_lo(dve, b + LEAD, turn)

            def value_tiles(name, out):
                for n in range(COUNT[name] // 2):
                    ahead(FIRST[name] + 2 * n)
                    ahead(FIRST[name] + 2 * n + 1)
                    for j in range(1 - n % 2, 3, 2):
                        take(TILE0[name] + 3 * n + j, out[:, j, 2 * COLS * n:2 * COLS * (n + 1)], 2 * COLS)

            norm(0, res, "norm1", tokens_of(sq1, T))
            operand_lo(dve, 0, tokens_of(sq1, T))
            ahead(-2)
            ahead(-1)
            for n in range(16):
                ahead(n)
                if n % 2:
                    take(n, feat[:, n, :], T)
            dve.wait_ge(gate_logits_ready, 1)
            bg = SMALL["b_gate"][0]
            for j in range(2):
                ts(gx[:, j, :], ps[:, 4 + j, 0:T], small[:, bg + j:bg + j + 1], None, ALU.add).then_inc(gate_biased, 1)
            tiles_are_taken(dve, 16)
            for h in range(8):
                rows = slice(64 * (h % 2), 64 * (h % 2) + 64)
                i = v.tensor_copy(kbd[rows, h // 2, META * h:META * h + META], feat[rows, 4 + h // 2, 0:META])
                link(i) if h < 7 else i.then_inc(kbd_ready, 1)
            value_tiles("w_in_values", vtok)
            tiles_are_taken(dve, TILE0["w_out"])
            dve.wait_ge(meta_values_ready, 1)
            tt(one["vbd"], ps[:, 2, :], one["bdm"], ALU.mult).then_inc(vbd_ready, 1)

            def scaled(n):
                if n < 8:
                    dve.wait_ge(z_ready, n + 1)
                    stt(zm[:, n, :], ps[:, 5 + n % 2, 0:W], SB_DIM ** -0.5, one["hide"], ALU.mult,
                        ALU.add).then_inc(z_taken, 1)
                else:
                    dve.wait_ge(z0_ready, 1)
                    ts(zm[:, n, 0:REAL], ps[:, 4, 0:REAL], SB_DIM ** -0.5, None, ALU.mult).then_inc(z_taken, 1)

            def softplus(n, cols):
                dve.wait_ge(soft_ready, n + 1)
                if n >= 2:
                    dve.wait_ge(pe_used_sp, n - 1)
                stt(sp_[:, n % 2, 0:cols], zm[:, n, 0:cols], 0.0, soft[:, n % 2, 0:cols], ALU.max,
                    ALU.add).then_inc(sp_ready, 1)

            def log_weight(n, cols):
                dve.wait_ge(s_ready, n + 1)
                bank = 1 if n == 8 else 7 if n % 2 else 0
                tt(zm[:, n, 0:cols], zm[:, n, 0:cols], ps[:, bank, 0:cols], ALU.subtract).then_inc(d_ready, 1)

            scaled(0)
            for n in range(9):
                if n < 8:
                    scaled(n + 1)
                softplus(n, W if n < 8 else REAL)
                if n:
                    log_weight(n - 1, W)
            log_weight(8, REAL)

            def head_norm(k, width):
                dve.wait_ge(head_sum, k + 1)
                ts(one["rh"].rearrange("p (b n) -> p b n", b=2), ps[:, 4:6, :], 1.0 / width, EPS, ALU.mult,
                   ALU.add).then_inc(head_var, 1)
                dve.wait_ge(head_root, k + 1)
                link(v.reciprocal(one["rh"], one["rh"]))

            dve.wait_ge(gate_soft, 1)
            link(stt(gx, gx, 0.0, gl, ALU.min, ALU.subtract))
            for j in range(2):
                link(v.tensor_tensor_scan(gl[:, j, :], one["ones_t"], gx[:, j, :], 0.0, ALU.mult, ALU.add))
            link(ts(bcum, gl, 1.0 / GLA_TAU, None, ALU.mult))
            link(ts(nb, gl, -1.0 / GLA_TAU, None, ALU.mult))
            for j in range(2):
                grp = bcum[:, j, META:].rearrange("p (i s) -> p i s", s=SUB)
                link(tt(dq[:, j, :].rearrange("p (i s) -> p i s", s=SUB), grp,
                             grp[:, :, SUB // 2 - 1:SUB // 2].broadcast_to([P, SUBS, SUB]), ALU.subtract))
            ts(dq, dq, -CLAMP, CLAMP, ALU.max, ALU.min).then_inc(q_exp_in, 1)

            head_norm(0, SB_DIM)
            at = SMALL["sb_norm"][0]
            for p in range(4):
                i = stt(mix[:, p, :], ps[:, 2 + p // 2, 256 * (p % 2):256 * (p % 2) + 256],
                        small[:, at + p:at + p + 1], one["rh"][:, 256 * p:256 * p + 256], ALU.mult, ALU.mult)
                link(i) if p < 3 else i.then_inc(sb_mixed, 1)
            dve.wait_ge(q_exp, 1)
            stt(qt, feat[:, 8:10, META:], GLA_DK ** -0.5, dq, ALU.mult, ALU.mult).then_inc(q_decayed, 1)

            def key_exponent(n):
                i, j = n // 2, n % 2
                seen = META + P * (1 + (i >= SUBS // 2))
                mid = META + SUB * i + SUB // 2 - 1
                if n >= 2:
                    dve.wait_ge(k_decayed, n - 1)
                ts(ke[:, j, 0:seen], nb[:, j, 0:seen], bcum[:, j, mid:mid + 1], CLAMP, ALU.add,
                   ALU.min).then_inc(k_exp_in, 1)

            def key_decay(n):
                i, j = n // 2, n % 2
                seen = META + P * (1 + (i >= SUBS // 2))
                dve.wait_ge(k_exp, n + 1)
                if n >= 2:
                    dve.wait_ge(k_used, n - 1)
                tt(kt[:, j, 0:seen], ke[:, j, 0:seen], feat[:, 10 + j, 0:seen], ALU.mult).then_inc(k_decayed, 1)

            key_exponent(0)
            for n in range(2 * SUBS):
                if n < 2 * SUBS - 1:
                    key_exponent(n + 1)
                key_decay(n)
            dve.wait_ge(k_used, 2 * SUBS)
            for h in range(GLA_HEADS):
                tt(A[:, h, :], ps[:, 4 + h, 0:W], one["keep"], ALU.mult).then_inc(gla_masked, 1)
            head_norm(1, GLA_DV)
            at = SMALL["gla_norm"][0]
            for h in range(4):
                link(stt(mix[:, 4 + h, :], ps[:, 2 + h // 2, 256 * (h % 2):256 * (h % 2) + 256],
                              small[:, at + h:at + h + 1], one["rh"][:, 256 * h:256 * h + 256], ALU.mult, ALU.mult))
            dve.wait_ge(silu_ready, 1)
            tt(mix[:, 4:8, :], mix[:, 4:8, :], sil, ALU.mult).then_inc(gla_mixed, 1)
            operand_lo(dve, 1, mix)

            def add_tiles(name):
                for n in range(8):
                    ahead(FIRST[name] + n)
                    g = TILE0[name] + n
                    dve.wait_ge(tile_ready, g + 1)
                    tt(res[:, n, META:], res[:, n, META:], bank_of(g)[:, 0:REAL], ALU.add).then_inc(
                        tile_taken[g % BANKS], 1)

            add_tiles("w_out")
            norm(1, res[:, :, META:], "norm2", tokens_of(sq1, REAL))
            operand_lo(dve, 2, tokens_of(sq1, REAL))
            for n in range(8):
                ahead(FIRST["w_peer_q"] + n)

            R = route
            dve.wait_ge(key_scores_taken, 16)

            def best16(values, out, index):
                link(v.max(out[:, 0:8], values))
                link(v.max_index(index[:, 0:8], out[:, 0:8], values))
                link(v.match_replace(out=values, in_to_replace=out[:, 0:8], in_values=values, imm_value=TAKEN))
                link(v.max(out[:, 8:16], values))
                link(v.max_index(index[:, 8:16], out[:, 8:16], values))

            rows = {k: R[k].rearrange("p (c k) -> p c k", c=16) for k in ("tv", "pos", "ix")}
            cand = R["cand"].rearrange("p (a b) -> p a b", a=TOPK)
            b0 = FIRST["expert_u"]
            for c in range(16):
                index = rows["ix"][:, c, :].bitcast(U32)
                for half in range(2):
                    ahead(b0 + 3 * c + half)
                    best16(sc[:, c, P * half:P * half + P], R["v"][:, TOPK * half:TOPK * half + TOPK],
                           index[:, TOPK * half:TOPK * half + TOPK])
                link(tt(cand, R["v"][:, 0:TOPK].unsqueeze(2).broadcast_to([P, TOPK, TOPK]),
                             R["v"][:, TOPK:].unsqueeze(1).broadcast_to([P, TOPK, TOPK]), ALU.add))
                ahead(b0 + 3 * c + 2)
                best16(R["cand"], rows["tv"][:, c, :], rows["pos"][:, c, :].bitcast(U32))
            link(v.tensor_copy(R["ixf"], R["ix"].bitcast(U32)))

            tv = R["tv"].rearrange("p (c k) -> p c k", c=16)
            gate = R["gate"].rearrange("p (c k) -> p c k", c=16)
            tt(gate, tv, tv[:, :, 0:1].broadcast_to([P, 16, TOPK]), ALU.subtract).then_inc(tops_shifted, 1)
            pos, pi = R["pos"].bitcast(U32), R["pi"].bitcast(U32)
            ahead(b0 + 48)
            link(ts(pi, pos, 4, None, ALU.logical_shift_right))
            link(v.tensor_copy(R["af"], pi))
            link(ts(pi, pos, TOPK - 1, None, ALU.bitwise_and))
            link(v.tensor_copy(R["bf"], pi))
            ix = R["ixf"].rearrange("p (c h k) -> p c h k", c=16, h=2)
            for t in range(2):
                for half, (digit, out) in enumerate(((R["af"], R["i1"]), (R["bf"], R["i2"]))):
                    part = slice(SLOTS * t, SLOTS * t + SLOTS)
                    ahead(b0 + 49 + 3 * (2 * t + half))
                    eq = R["eq"].rearrange("p (s a) -> p s a", a=TOPK)
                    link(tt(eq, digit[:, part].unsqueeze(2).broadcast_to([P, SLOTS, TOPK]),
                                 iota[:, 0:TOPK].unsqueeze(1).broadcast_to([P, SLOTS, TOPK]), ALU.is_equal))
                    ahead(b0 + 50 + 3 * (2 * t + half))
                    eq4 = R["eq"].rearrange("p (c k a) -> p c k a", c=PH, a=TOPK)
                    link(tt(eq4, eq4, ix[:, PH * t:PH * t + PH, half, :].unsqueeze(2).broadcast_to(
                        [P, PH, TOPK, TOPK]), ALU.mult))
                    ahead(b0 + 51 + 3 * (2 * t + half))
                    link(v.tensor_reduce(out[:, part], eq, AX.X, ALU.add))
            for n in range(61, HALF_KEYS):
                ahead(b0 + n)
            dve.wait_ge(tops_exp, 1)
            link(v.tensor_reduce(R["sum"], gate, AX.X, ALU.add))
            link(v.reciprocal(R["rsum"], R["sum"]))
            tt(gate, gate, R["rsum"].unsqueeze(2).broadcast_to([P, 16, TOPK]), ALU.mult).then_inc(routed, 1)

            def onehots(n, k, tokens, half):
                first = iota_rows[:, HALF_KEYS * half:HALF_KEYS * (half + 1), :]

                def spread(row, width):
                    return slots[:, row, tokens].unsqueeze(1).broadcast_to([P, width, GROUP])

                matched = onehot1[:, k, 2, :, :]
                tt(matched, first, spread(3, HALF_KEYS), ALU.is_equal).then_inc(keys_matched, 1)
                tt(onehot2[:, k, :, :], iota_rows[:, :, :], spread(4, NKEYS), ALU.is_equal)
                dve.wait_ge(keys_matched, n + 1)
                for part in range(3):
                    i = tt(onehot1[:, k, part, :, :], matched, spread(part, HALF_KEYS), ALU.mult)
                i.then_inc(onehots_ready, 1)

            def apply_gates(n, k, tokens, half, bank0):
                dve.wait_ge(gates_ready, n + 1)
                h = act_store[:, HALF_KEYS * half:HALF_KEYS * (half + 1), tokens]
                g = ps[:, bank0 + k, :].rearrange("p (t i) -> p i t", t=GROUP)
                tt(h, h, g, ALU.mult).then_inc(gates_applied, 1)

            def row_operand(src, n, b, turn=None):
                k, t = b % RING, 0 if turn is None else turn
                dve.wait_ge(x_hi_ready, t * RING + (n + 1))
                part = slice(k * REAL, (k + 1) * REAL)
                tt(x_lo[:, part], src, x_hi[:, part].bitcast(F32), ALU.subtract).then_inc(x_lo_ready, 1)
                ahead(b, turn)

            link(v.tensor_copy(iota_rows[:, :, :], iota[:, :].unsqueeze(2).broadcast_to([P, NKEYS, GROUP])))
            dve.wait_ge(slots_taken, 2)
            link(v.tensor_copy(slots[:, 0, :], gate_f))
            link(tt(gate_rest, gate_f, slots[:, 0, :], ALU.subtract))
            link(v.tensor_copy(slots[:, 1, :], gate_rest))
            link(tt(gate_f, gate_rest, slots[:, 1, :], ALU.subtract))
            link(v.tensor_copy(slots[:, 2, :], gate_f))
            bv = FIRST["expert_v"]
            for half in range(2):
                n0, bank0 = 32 * half, 4 - 4 * half
                tiles_are_taken(dve, TILE0["expert_u"] + HALF_KEYS * (half + 1))

                def turn_of_four(turn):
                    t = 0 if turn is None else turn
                    for k in range(RING):
                        if half:
                            row_operand(act_store[:, t * RING + k, :], ACTS0 + k, bv + k, t)
                        else:
                            ahead(b0 + HALF_KEYS + k, t)
                        at = t * (2 * GROUP) + GROUP * (k // 2)
                        if k % 2 == 0:
                            onehots(t * 2 + (n0 + k // 2), k // 2, bass.ds(at, GROUP), half)
                        elif turn is not None or k > 1:
                            apply_gates(t * 2 + (n0 + k // 2 - 1), 1 - k // 2, bass.ds(at - GROUP, GROUP), half, bank0)

                turn_of_four(None)
                with dve.Fori(1, 16) as i:
                    turn_of_four(i)
                apply_gates(n0 + 31, 1, slice(REAL - GROUP, REAL), half, bank0)
            with dve.Fori(16, 32) as i:
                for k in range(RING):
                    row_operand(act_store[:, i * RING + k, :], ACTS0 + k, bv + k, i)

            def add_sums(n):
                dve.wait_ge(y_ready, n)
                for m in range(4):
                    r = res[:, 2 * m:2 * m + 2, META:]
                    tt(r, r, ps[:, 4 + m, :].rearrange("p (c t) -> p c t", c=2), ALU.add).then_inc(residual, 1)

            add_sums(1)
            link(v.tensor_copy(res[:, :, 0:META], meta_2))
            dve.wait_ge(residual, 4)
            norm(2, res[:, :, META:], "norm_f", res[:, :, META:])
            norm(3, res, "norm_mix", tokens_of(sq_late, T))
            operand_lo(dve, X_MIX, tokens_of(sq_late, T))
            b0, g0 = FIRST["w_in_2_features"], TILE0["w_in_2_features"]
            with dve.Fori(0, 15) as i:
                for k in range(RING):
                    ahead(b0 + k, i)
                    if k % 2:
                        take(g0 + k, feat2[:, i * RING + k, :], T, i * RING)
            value_tiles("w_in_2_values", v2)
            tiles_are_taken(dve, TILE0["w_in_2_values"])
            dve.wait_ge(kiwi_taken, 2)
            dve.wait_ge(vis_ready, 1)
            for t in range(2):
                seen = META + P * (t + 1)
                for h in range(IDX_HEADS):
                    n = 8 * t + h
                    dve.wait_ge(idx_ready, n + 1)
                    out = score[:, t, 0:seen] if h == 0 else rel[:, n % 2, 0:seen]
                    ts(out, ps[:, 4 + n % 2, 0:seen], 0.0, two["wi"][:, n:n + 1], ALU.max,
                       ALU.mult).then_inc(idx_taken, 1)
                    dve.wait_ge(idx_taken, n + 1)
                    if h:
                        link(tt(score[:, t, 0:seen], score[:, t, 0:seen], out, ALU.add))
                part = score[:, t, P * t:seen]
                link(tt(part, part, two["vis"], ALU.add))
            u = feat2[:, CU:CU + 8, :]
            link(tt(u, u, feat2[:, CC:CC + 8, :], ALU.mult))
            at = SMALL["conv"][0]
            for c in range(C):
                w = [small[:, at + C * k + c:at + C * k + c + 1] for k in range(CONV_K)]
                link(ts(yc[:, c, :], u[:, c, META:], w[2], None, ALU.mult))
                for k in (1, 0):
                    off = META - (CONV_K - 1) + k
                    link(stt(yc[:, c, :], u[:, c, off:off + REAL], w[k], yc[:, c, :], ALU.mult, ALU.add))
            tt(yc, yc, feat2[:, CB:CB + 8, META:], ALU.mult).then_inc(conv_ready, 1)
            operand_lo(dve, X_CONV, yc)
            for n in range(8):
                ahead(FIRST["w_conv_out_2"] + n)
            top8 = two["top8"]
            for t in range(2):
                seen = META + P * (t + 1)
                s = score[:, t, 0:seen]
                for r in range(-(-KEEP // 8)):
                    link(v.max(top8[:, 0:8], s))
                    if 8 * (r + 1) > KEEP:
                        link(v.memset(top8[:, KEEP - 8 * r:8], TAKEN))
                    link(v.match_replace(out=s, in_to_replace=top8[:, 0:8], in_values=s, imm_value=TAKEN))
                link(ts(selb[:, t, 0:seen], s, TAKEN, NEG, ALU.not_equal, ALU.mult))
                part = selb[:, t, P * t:seen]
                link(tt(part, part, two["vis"], ALU.add))

            stat = two["stat"]
            def mask_logits(n):
                t = n // 8
                seen = META + P * (t + 1)
                dve.wait_ge(logits_ready, n + 1)
                if n >= 2:
                    dve.wait_ge(probs_ready, n - 1)
                m = lm[:, n % 2, 0:seen]
                link(stt(m, ps[:, n % 2, 0:seen], HEAD_DIM ** -0.5, selb[:, t, 0:seen], ALU.mult, ALU.add))
                link(v.tensor_reduce(stat[:, n:n + 1], m, AX.X, ALU.max))
                ts(stat[:, 16 + n:17 + n], stat[:, n:n + 1], -1.0, None, ALU.mult).then_inc(masked_ready, 1)

            def scale_probs(n):
                seen = META + P * (n // 8 + 1)
                dve.wait_ge(probs_ready, n + 1)
                link(v.reciprocal(stat[:, 48 + n:49 + n], stat[:, 32 + n:33 + n]))
                m = pr[:, n % 2, 0:seen]
                ts(m, m, stat[:, 48 + n:49 + n], None, ALU.mult).then_inc(probs_scaled, 1)

            mask_logits(0)
            for n in range(16):
                if n < 15:
                    mask_logits(n + 1)
                scale_probs(n)

            operand_lo(dve, X_ATTN, ya)
            dve.wait_ge(sigmoid_ready, 1)
            dve.wait_ge(conv_gated, 1)
            for n in range(8):
                ahead(FIRST["w_attn_out_2"] + n)
                g = TILE0["w_attn_out_2"] + n
                dve.wait_ge(tile_ready, g + 1)
                tt(yc[:, n, :], bank_of(g)[:, 0:REAL], feat2[:, GA + n, META:], ALU.mult).then_inc(
                    tile_taken[g % BANKS], 1)
            tiles_are_taken(dve, TILE0["w_out_2"])
            for half in range(2):
                c = slice(4 * half, 4 * half + 4)
                tt(ya[:, c, :], yc[:, c, :], yco[:, c, :], ALU.add).then_inc(mixed_ready, 1)
            operand_lo(dve, X_MIXED, ya)
            add_tiles("w_out_2")
            norm(4, res[:, :, META:], "norm_ffn", tokens_of(sq_late, REAL))
            operand_lo(dve, X_FFN, tokens_of(sq_late, REAL))
            b0, g0 = FIRST["w_gate_up_2"], TILE0["w_gate_up_2"]
            with dve.Fori(0, FF // 2) as i:
                for k in range(RING):
                    ahead(b0 + k, i)
                    if k > 1:
                        g = g0 + k
                        dve.wait_ge(tile_taken[(g - 2) % BANKS], i + ((g - 2) // BANKS + 1))
                        dve.wait_ge(tile_ready, i * RING + (g + 1))
                        tt(hidden[:, i * 2 + (k - 2), :], bank_of(g)[:, 0:REAL], sg[:, k - 2, :],
                           ALU.mult).then_inc(tile_taken[g % BANKS], 1)
            b0 = FIRST["w_down_2"]
            with dve.Fori(0, FF // RING) as i:
                for k in range(RING):
                    row_operand(hidden[:, i * RING + k, :], HIDDEN0 + k, b0 + k, i)
            for n in range(FF // RING * RING, FF):
                row_operand(hidden[:, n, :], HIDDEN0 + n, b0 + n)
            add_sums(2)
            dve.wait_ge(residual, 8)
            norm(5, res[:, :, META:], "norm_final", outT)


def columns_to_blocks(w):
    n = w.shape[1]
    return w.reshape(C, P, n // COLS, COLS).transpose(2, 1, 0, 3).reshape(n // COLS, P, BLOCK)


def rows_to_blocks(w):
    return w.reshape(-1, P, BLOCK)


def kernel(**inputs):
    import concourse.bacc as bacc
    from concourse.bass_utils import run_bass_kernel_spmd

    a = {k: np.asarray(v) for k, v in inputs.items()}
    w1, w2 = a["w_in"][0], a["w_in_2"][0]
    o1 = np.cumsum([0, 512, 512, 512, 256, 256, 512, 512, 16])
    o2 = np.cumsum([0, 1024, 1024, 1024, 512, 64, 8, 1024, 1024, 1024, 1024, 1024])

    def cut(w, o, *ids):
        return np.concatenate([w[:, o[i]:o[i + 1]] for i in ids], axis=1)

    gate = a["w_gate_2"][0].reshape(D, FF // 2, 1, 2 * COLS)
    up = a["w_up_2"][0].reshape(D, FF // 2, 1, 2 * COLS)
    gate_up = np.concatenate([gate, up], axis=2).reshape(D, 2 * D_FF)
    stream = np.concatenate([
        columns_to_blocks(cut(w1, o1, 0, 1, 3, 4, 6)),
        columns_to_blocks(cut(w1, o1, 2, 5)),
        columns_to_blocks(a["w_out"][0]),
        columns_to_blocks(a["w_peer_q"][0]),
        columns_to_blocks(a["expert_u"][0].T),
        rows_to_blocks(a["expert_v"][0]),
        columns_to_blocks(cut(w2, o2, 1, 6, 8, 0, 7, 9, 10, 3)),
        columns_to_blocks(cut(w2, o2, 2)),
        columns_to_blocks(a["w_conv_out_2"][0]),
        columns_to_blocks(a["w_attn_out_2"][0]),
        columns_to_blocks(a["w_out_2"][0]),
        columns_to_blocks(gate_up),
        rows_to_blocks(a["w_down_2"][0]),
    ], axis=0)
    assert stream.shape == (BLOCKS, P, BLOCK)

    def features(w):
        return w.reshape(C, P, -1).transpose(1, 0, 2).reshape(P, -1)

    ki, wi = cut(w2, o2, 4), cut(w2, o2, 5)
    keys = np.concatenate([a["sub_keys1"][0].transpose(2, 0, 1), a["sub_keys2"][0].transpose(2, 0, 1)])
    parts = {
        "glr": features(cut(w1, o1, 7)), "meta_2": features(a["meta_tokens_2"].T),
        "gate_up": np.concatenate([a["w_gate_up"][0]] * (P // GLA_RANK)),
        "norm1": features(a["norm1_g"][0]), "norm2": features(a["norm2_g"][0]),
        "norm_f": features(a["norm_f_g"]), "norm_mix": features(a["norm_mix_g_2"][0]),
        "norm_ffn": features(a["norm_ffn_g_2"][0]), "norm_final": features(a["norm_final_g_2"]),
        "sb_norm": a["sb_norm_g"][0].reshape(4, P).T, "gla_norm": a["gla_norm_g"][0].reshape(4, P).T,
        "b_gate": a["b_gate_up"][0].reshape(2, P).T,
        "conv": a["conv_w_2"][0].reshape(CONV_K * C, P).T,
    }
    small = np.concatenate([parts[k].reshape(P, n) for k, (_, n) in SMALL.items()], axis=1)
    tokens = np.concatenate([a["meta_tokens"], a["x"][0]])
    arrays = {"stream": stream, "small": np.ascontiguousarray(small),
              "keys": np.ascontiguousarray(keys.reshape(P, -1)),
              "kiwi": np.ascontiguousarray(features(np.concatenate([ki, ki, wi], axis=1))),
              "tokens": np.ascontiguousarray(features(tokens.T))}

    nc = bacc.Bacc("TRN2", target_bir_lowering=False, num_devices=1,
                   dynamic_dma_scratch_size=1024)
    dram = {k: nc.dram_tensor(f"in_{k}", v.shape, F32, kind="ExternalInput").ap() for k, v in arrays.items()}
    out = nc.dram_tensor("out_dram", (P, C * REAL), F32, kind="ExternalOutput").ap()
    build(nc, dram["stream"], dram["small"], dram["keys"], dram["kiwi"], dram["tokens"], out)
    r = run_bass_kernel_spmd(nc, [{f"in_{k}": v for k, v in arrays.items()}], core_ids=[0])
    got = r.results[0]["out_dram"]
    return np.ascontiguousarray(got.reshape(P, C, REAL).transpose(2, 1, 0)).reshape(1, REAL, D)
```

```python
import math
from contextlib import ExitStack

import numpy as np

import concourse.bass as bass
from concourse import mybir

F32 = mybir.dt.float32
F32R = mybir.dt.float32r
BF16 = mybir.dt.bfloat16
U32 = mybir.dt.uint32
ALU = mybir.AluOpType
ACT = mybir.ActivationFunctionType
AX = mybir.AxisListType

P = 128
D = 1024
C = D // P
META = 16
REAL = 256
T = META + REAL
EPS = 1e-6

SB_HEADS, SB_DIM = 8, 64
GLA_HEADS, GLA_DK, GLA_DV = 4, 64, 128
GLA_RANK, GLA_TAU = 16, 16.0
SUB = 16
SUBS = REAL // SUB
KEY_BUFS = 4
CLAMP = 40.0

PH, NKEYS, TOPK = 8, 128, 16
SLOTS = PH * TOPK
GROUP = 8
HALF_KEYS = NKEYS // 2

HEADS, HEAD_DIM = 8, 128
IDX_HEADS, IDX_DIM = 8, 64
KEEP = min(256, T // 4)
IDX_SCALE = (IDX_HEADS ** -0.5) * (IDX_DIM ** -0.5)
CONV_K = 3
D_FF = ((8 * D // 3 + 255) // 256) * 256
FF = D_FF // P

NEG = -(2.0 ** 100)
TAKEN = -(2.0 ** 127)

COLS = 128
BLOCK = 1024
RING = 4
LEAD = 2


def stages():
    counts = [("w_in_features", 16), ("w_in_values", 8), ("w_out", 8), ("w_peer_q", 8),
              ("expert_u", NKEYS), ("expert_v", NKEYS), ("w_in_2_features", 44),
              ("w_in_2_values", 8), ("w_in_2_gates", 16), ("w_conv_out_2", 8), ("w_attn_out_2", 8), ("w_out_2", 8),
              ("w_gate_up_2", 2 * D_FF // COLS), ("w_down_2", D_FF // COLS)]
    first, at = {}, 0
    for name, n in counts:
        first[name] = at
        at += n
    return first, dict(counts), at


FIRST, COUNT, BLOCKS = stages()

SMALL = {}
_at = 0
for _name, _n in (("glr", C * GLA_RANK), ("meta_2", C * META), ("gate_up", GLA_HEADS * GLA_DK), ("norm1", C), ("norm2", C),
                  ("norm_f", C), ("norm_mix", C), ("norm_ffn", C), ("norm_final", C), ("sb_norm", 4),
                  ("gla_norm", 4), ("b_gate", 2), ("conv", CONV_K * C)):
    SMALL[_name] = (_at, _n)
    _at += _n
SMALL_COLS = _at
KEYS_COLS = PH * NKEYS
KIWI_COLS = C * (2 * IDX_DIM + IDX_HEADS)

TILE0 = {}
_at = 0
for _name, _n in (("w_in_features", 16), ("w_in_values", 12), ("w_out", 8), ("w_peer_q", 8),
                  ("expert_u", NKEYS), ("w_in_2_features", 44), ("w_in_2_values", 12),
                  ("w_in_2_gates", 16), ("w_conv_out_2", 8), ("w_attn_out_2", 8), ("w_out_2", 8), ("w_gate_up_2", 2 * FF)):
    TILE0[_name] = _at
    _at += _n
BANKS = 4


def build(nc, stream, small_dram, keys_dram, kiwi_dram, x_dram, out_dram):
    with ExitStack() as ctx:
        def sb(name, shape, dt=F32):
            return ctx.enter_context(nc.sbuf_tensor(name, shape, dt))

        def sem(name):
            return ctx.enter_context(nc.semaphore(name))

        ps = ctx.enter_context(nc.psum_tensor("ps", [P, 8, 512], F32))

        work = sb("work", [P, NKEYS * REAL])
        ring = sb("ring", [P, RING, BLOCK])
        res = sb("res", [P, C, T])
        w_hi = sb("w_hi", [P, RING, BLOCK], F32R)
        w_lo = sb("w_lo", [P, RING, BLOCK], F32R)
        x_hi = sb("x_hi", [P, C * T], F32R)
        x_lo = sb("x_lo", [P, C * T], F32R)
        small = sb("small", [P, SMALL_COLS])
        ones = sb("ones", [P, P])
        eps = sb("eps", [P, 1])
        zeros = sb("zeros", [P, P])
        ident = sb("ident", [P, P])
        iota = sb("iota", [P, NKEYS])
        onehot1 = sb("onehot1", [P, 2, 3, HALF_KEYS, GROUP], BF16)
        onehot2 = sb("onehot2", [P, 2, NKEYS, GROUP], BF16)
        iota_rows = sb("iota_rows", [P, NKEYS, GROUP], BF16)
        slots = sb("slots", [P, 5, REAL], BF16)
        spare = sb("spare", [P, 2 * T])
        var, rstd = spare[:, 0:T], spare[:, T:2 * T]
        gate_rest, gate_f = spare[:, 0:REAL], spare[:, REAL:2 * REAL]

        def tokens_of(x, n):
            return x[:, 0:C * n].rearrange("p (c t) -> p c t", c=C)

        x_parts = {n: (tokens_of(x_hi, n), tokens_of(x_lo, n)) for n in (T, REAL)}

        def view(name):
            at, n = SMALL[name]
            return small[:, at:at + n]

        glr_w = view("glr").rearrange("p (c n) -> p c n", c=C)
        meta_2 = view("meta_2").rearrange("p (c t) -> p c t", c=C)
        gate_up_w = view("gate_up")

        one_at = {}

        def carve(sizes, offsets=None):
            at, parts = 0, {}
            for name, n in sizes:
                parts[name] = work[:, at:at + n]
                if offsets is not None:
                    offsets[name] = at
                at += n
            assert at <= NKEYS * REAL, at
            return parts

        W = 3 * P
        one = carve([("feat", 16 * T), ("ones_t", T), ("vtok", 3 * D), ("kbd", 4 * P), ("vbd", 512),
                     ("tri", P), ("bdtri", P), ("rep", P), ("win", 2 * P), ("blk64", P), ("hide", W), ("keep", W),
                     ("bdm", 512), ("zm", 9 * W), ("soft", 2 * W), ("sp", 2 * W), ("glrT", T),
                     ("gx", 2 * T), ("gl", 2 * T), ("nb", 2 * T), ("dq", 2 * REAL),
                     ("ke", KEY_BUFS * T), ("kt", KEY_BUFS * T), ("A", 4 * W), ("A0", 4 * REAL),
                     ("sqh", D), ("rh", 2 * D), ("mix", C * REAL), ("sil", 4 * REAL), ("keys", KEYS_COLS), ("sq", C * T)],
                    one_at)
        feat = one["feat"].rearrange("p (n t) -> p n t", n=16)
        vtok = one["vtok"].rearrange("p (k n) -> p k n", k=3)
        kbd = one["kbd"].rearrange("p (n t) -> p n t", n=4)
        zm = one["zm"].rearrange("p (h n) -> p h n", h=9)
        soft = one["soft"].rearrange("p (h n) -> p h n", h=2)
        sp_ = one["sp"].rearrange("p (h n) -> p h n", h=2)
        gx = one["gx"].rearrange("p (j t) -> p j t", j=2)
        gl = one["gl"].rearrange("p (j t) -> p j t", j=2)
        bcum = gl
        nb = one["nb"].rearrange("p (j t) -> p j t", j=2)
        dq = one["dq"].rearrange("p (j t) -> p j t", j=2)
        qbd_flat = work[:, one_at["soft"]:one_at["soft"] + 4 * REAL]
        qbd = qbd_flat.rearrange("p (j i e s) -> p j i e s", j=2, i=SUBS, e=2)
        ke = one["ke"].rearrange("p (n t) -> p n t", n=KEY_BUFS)
        kt = one["kt"].rearrange("p (n t) -> p n t", n=KEY_BUFS)
        rh = one["rh"].rearrange("p (k n) -> p k n", k=2)
        A = one["A"].rearrange("p (h n) -> p h n", h=4)
        A0 = one["A0"].rearrange("p (h n) -> p h n", h=4)
        mix = one["mix"].rearrange("p (c t) -> p c t", c=C)
        sil = one["sil"].rearrange("p (c t) -> p c t", c=4)
        keys_w = one["keys"].rearrange("p (h k) -> p h k", h=PH)
        sq1 = one["sq"]

        act_store = work[:, :].rearrange("p (i t) -> p i t", i=NKEYS)
        base = HALF_KEYS * REAL
        route = {}
        for name, n in (("qp", PH * REAL), ("sc", 16 * 256), ("tv", 256), ("pos", 256), ("ix", 512),
                        ("af", 256), ("bf", 256), ("eq", 2048), ("i1", 256), ("i2", 256), ("gate", 256),
                        ("row1", 256), ("sum", 16), ("rsum", 16), ("v", 32), ("cand", 256), ("ixf", 512),
                        ("pi", 256)):
            route[name] = work[:, base:base + n]
            base += n
        assert base <= NKEYS * REAL
        qp = route["qp"].rearrange("p (h t) -> p h t", h=PH)
        sc = route["sc"].rearrange("p (c n) -> p c n", c=16)

        two = carve([("feat2", 60 * T), ("v2", 3 * D), ("kidup", T), ("wi", 16), ("score", 2 * T),
                     ("rel", 2 * T), ("selb", 2 * T), ("top8", 16), ("vis", 144), ("lm", 2 * T), ("pr", 2 * T),
                     ("stat", 4 * 16), ("pT", 2 * W), ("ya", C * REAL), ("yc", C * REAL),
                     ("yco", C * REAL)])
        kiwi_w = two["ya"][:, 0:KIWI_COLS].rearrange("p (c n) -> p c n", c=C)
        feat2 = two["feat2"].rearrange("p (n t) -> p n t", n=60)
        v2 = two["v2"].rearrange("p (k n) -> p k n", k=3)
        score = two["score"].rearrange("p (t n) -> p t n", t=2)
        rel = two["rel"].rearrange("p (t n) -> p t n", t=2)
        selb = two["selb"].rearrange("p (t n) -> p t n", t=2)
        lm = two["lm"].rearrange("p (t n) -> p t n", t=2)
        pr = two["pr"].rearrange("p (t n) -> p t n", t=2)
        pT = two["pT"].rearrange("p (t n) -> p t n", t=2)
        ya = two["ya"].rearrange("p (c t) -> p c t", c=C)
        yc = two["yc"].rearrange("p (c t) -> p c t", c=C)
        yco = two["yco"].rearrange("p (c t) -> p c t", c=C)
        QI, CU, CC, CB, KF, QF, GA, GB = 0, *range(4, 60, 8)
        ffa = carve([("ffa", FF * REAL), ("sg", 2 * REAL), ("outT", C * REAL)])
        hidden = ffa["ffa"].rearrange("p (n t) -> p n t", n=FF)
        sg = ffa["sg"].rearrange("p (n t) -> p n t", n=2)
        outT = ffa["outT"].rearrange("p (c t) -> p c t", c=C)
        sq_late = work[:, NKEYS * REAL - C * T:]

        landed = [sem(f"landed{i}") for i in range(RING)]
        block_begun, w_hi_ready, w_lo_ready = sem("block_begun"), sem("w_hi_ready"), sem("w_lo_ready")
        x_hi_ready, x_lo_ready = sem("x_hi_ready"), sem("x_lo_ready")
        keys_landed, kiwi_landed = sem("keys_landed"), sem("kiwi_landed")
        x_landed = [sem(f"x_landed{i}") for i in range(4)]
        small_landed, stored = sem("small_landed"), sem("stored")
        zeroed, consts = sem("zeroed"), sem("consts")
        vec_step, act_step, pool_step = sem("vec_step"), sem("act_step"), sem("pool_step")
        tile_ready = sem("tile_ready")
        tile_taken = [sem(f"tile_taken{i}") for i in range(BANKS)]
        squares_ready, folded, sum_ready, root_ready, normed = (
            sem(n) for n in ("squares_ready", "folded", "sum_ready", "root_ready", "normed"))
        glr_ready, glr_taken, gate_logits_ready, gate_biased, gate_soft = (
            sem(n) for n in ("glr_ready", "glr_taken", "gate_logits_ready", "gate_biased",
                             "gate_soft"))
        kbd_ready, z0_ready, z_ready, z_taken, soft_ready, sp_ready, s_ready, d_ready, a_ready = (
            sem(n) for n in ("kbd_ready", "z0_ready", "z_ready", "z_taken", "soft_ready", "sp_ready",
                             "s_ready", "d_ready", "a_ready"))
        vbd_ready, sb_out_ready, sb_mixed, pe_used_sp = (
            sem(n) for n in ("vbd_ready", "sb_out_ready", "sb_mixed", "pe_used_sp"))
        z0_taken, qbd_zeroed = sem("z0_taken"), sem("qbd_zeroed")
        head_sq, head_sum, head_logged, head_rooted = (
            sem(n) for n in ("head_sq", "head_sum", "head_logged", "head_rooted"))
        q_exp_in, q_exp, q_decayed, k_exp, k_decayed, k_used = (
            sem(n) for n in ("q_exp_in", "q_exp", "q_decayed", "k_exp", "k_decayed", "k_used"))
        gla_masked, gla_meta_taken, gla_out_ready, silu_ready, gla_mixed = (
            sem(n) for n in ("gla_masked", "gla_meta_taken", "gla_out_ready", "silu_ready", "gla_mixed"))
        residual, meta_values_ready = sem("residual"), sem("meta_values_ready")
        key_scores_ready, key_scores_taken, tops_shifted, tops_exp, routed, slots_ready, slots_taken = (
            sem(n) for n in ("key_scores_ready", "key_scores_taken", "tops_shifted", "tops_exp", "routed",
                             "slots_ready", "slots_taken"))
        keys_matched, onehots_ready, gates_ready, gates_applied, y_ready = (
            sem(n) for n in ("keys_matched", "onehots_ready", "gates_ready", "gates_applied", "y_ready"))
        kiwi_ready, kiwi_taken, idx_ready, idx_taken = (
            sem(n) for n in ("kiwi_ready", "kiwi_taken", "idx_ready", "idx_taken"))
        logits_ready, masked_ready, probs_ready, probs_scaled, probs_turned, turned_taken = (
            sem(n) for n in ("logits_ready", "masked_ready", "probs_ready", "probs_scaled",
                             "probs_turned", "turned_taken"))
        attn_ready, attn_taken, conv_ready, sigmoid_ready, conv_gated, mixed_ready = (
            sem(n) for n in ("attn_ready", "attn_taken", "conv_ready", "sigmoid_ready", "conv_gated",
                             "mixed_ready"))
        vis_ready = sem("vis_ready")

        ACTS0 = 2 * 3
        X_MIX = (ACTS0 + NKEYS) // 2
        X_CONV, X_ATTN, X_MIXED, X_FFN = X_MIX + 1, X_MIX + 2, X_MIX + 3, X_MIX + 4
        HIDDEN0 = 2 * (X_FFN + 1)

        def split_hi(act, b, turn=None):
            if b >= BLOCKS:
                return
            t, k = (0, b % RING) if turn is None else (turn, b % RING)
            act.wait_ge(landed[k], t * 16 + 16 * (b // RING + 1))
            if turn is not None or b >= RING:
                act.wait_ge(block_begun, t * RING + (b - RING + 2))
            nc.scalar.activation(w_hi[:, k, :], ring[:, k, :], ACT.Copy).then_inc(w_hi_ready, 1)

        def split_lo(dve, b, turn=None):
            if b >= BLOCKS:
                return
            t, k = (0, b % RING) if turn is None else (turn, b % RING)
            dve.wait_ge(w_hi_ready, t * RING + (b + 1))
            nc.vector.tensor_tensor(w_lo[:, k, :], ring[:, k, :], w_hi[:, k, :].bitcast(F32),
                                    ALU.subtract).then_inc(w_lo_ready, 1)

        def operand_hi(act, n, src, ready, value, each=1, halves=(0, 1)):
            tokens = src.shape[2]
            for half in halves:
                if ready is not None:
                    act.wait_ge(ready, value + each * half)
                c = slice(4 * half, 4 * half + 4)
                nc.scalar.activation(x_parts[tokens][0][:, c, :], src[:, c, :], ACT.Copy).then_inc(x_hi_ready, 1)

        def operand_lo(dve, n, src, halves=(0, 1)):
            tokens = src.shape[2]
            for half in halves:
                dve.wait_ge(x_hi_ready, 2 * n + half + 1)
                c = slice(4 * half, 4 * half + 4)
                nc.vector.tensor_tensor(x_parts[tokens][1][:, c, :], src[:, c, :],
                                        x_parts[tokens][0][:, c, :].bitcast(F32),
                                        ALU.subtract).then_inc(x_lo_ready, 1)

        def bank_is_free(eng, g, turn=None):
            if turn is not None:
                eng.wait_ge(tile_taken[g % BANKS], turn + g // BANKS)
            elif g >= BANKS:
                eng.wait_ge(tile_taken[g % BANKS], g // BANKS)

        def tile_is_taken(eng, g):
            eng.wait_ge(tile_taken[g % BANKS], g // BANKS + 1)

        def tiles_are_taken(eng, g):
            for bank in range(BANKS):
                eng.wait_ge(tile_taken[bank], (g - bank + BANKS - 1) // BANKS)

        def norm_bank(k):
            return 2 if k in (2, 5) else 7

        def bank_of(g):
            return ps[:, g % BANKS, :]

        block = ctx.enter_context(nc.Block())

        @block.sync
        def _(sp):
            for piece in range(4):
                sp.dma_start(res[:, 2 * piece:2 * piece + 2, :].rearrange("p c t -> p (c t)"),
                             x_dram[:, 2 * T * piece:2 * T * (piece + 1)]).then_inc(x_landed[piece], 16)
            sp.dma_start(small[:, :], small_dram).then_inc(small_landed, 16)
            for b in range(RING):
                sp.dma_start(ring[:, b, :], stream[b]).then_inc(landed[b], 16)
            sp.dma_start(one["keys"], keys_dram).then_inc(keys_landed, 16)
            with sp.Fori(1, BLOCKS // RING) as i:
                for k in range(RING):
                    sp.wait_ge(w_lo_ready, i * RING + (k + 1 - RING))
                    sp.dma_start(ring[:, k, :], stream[i * RING + k]).then_inc(landed[k], 16)
            for b in range(BLOCKS // RING * RING, BLOCKS):
                sp.wait_ge(w_lo_ready, b + 1 - RING)
                sp.dma_start(ring[:, b % RING, :], stream[b]).then_inc(landed[b % RING], 16)
            for half in range(2):
                sp.wait_ge(normed, 2 * 5 + half + 1)
                part = slice(half * 4 * REAL, (half + 1) * 4 * REAL)
                sp.dma_start(out_dram[:, part], outT.rearrange("p c t -> p (c t)")[:, part]).then_inc(stored, 16)
            sp.wait_ge(stored, 32)

        @block.gpsimd
        def _(pool):
            g = nc.gpsimd
            for tile, value in ((ones[:, :], 1.0), (eps[:, :], EPS), (one["ones_t"], 1.0), (zeros[:, :], 0.0), (ident[:, :], 0.0),
                                (one["tri"], 1.0), (one["rep"], 0.0), (one["bdtri"], 1.0), (one["win"], 0.0),
                                (one["blk64"], 1.0), (one["hide"], 0.0), (one["keep"], 1.0),
                                (one["bdm"], 1.0), (one["kbd"], 0.0)):
                g.memset(tile, value).then_inc(zeroed, 1)
            pool.wait_ge(zeroed, 14)
            g.iota(iota[:, :], [[1, NKEYS]], base=0, channel_multiplier=0,
                   allow_small_or_imprecise_dtypes=True).then_inc(consts, 1)
            g.affine_select(out=ident[:, :], in_=ident[:, :], compare_op=ALU.not_equal, fill=1.0, base=0,
                            pattern=[[-1, P]], channel_multiplier=1).then_inc(consts, 1)
            g.affine_select(out=one["tri"], in_=one["tri"], compare_op=ALU.is_ge, fill=0.0, base=0,
                            pattern=[[-1, P]], channel_multiplier=1).then_inc(consts, 1)
            v = one["rep"][0:META, :].rearrange("p (h m) -> p h m", m=META)
            g.affine_select(out=v, in_=v, compare_op=ALU.not_equal, fill=1.0, base=0,
                            pattern=[[0, P // META], [-1, META]], channel_multiplier=1).then_inc(consts, 1)
            g.memset(one["win"][:, P - META:P], 1.0).then_inc(consts, 1)
            for name, fill, off in (("keep", 0.0, 0), ("hide", NEG, -1)):
                for at, n in ((0, 2 * P), (2 * P, P)):
                    v = one[name][:, at:at + n]
                    g.affine_select(out=v, in_=v, compare_op=ALU.is_ge, fill=fill, base=off,
                                    pattern=[[1, n]], channel_multiplier=-1).then_inc(consts, 1)
            for n, (name, groups, size, inner) in enumerate((("bdtri", 8, META, META), ("blk64", 2, 64, 64),
                                                             ("bdm", 8, META, 64))):
                v = one[name].rearrange("p (g n) -> p g n", g=groups)
                g.affine_select(out=v, in_=v, compare_op=ALU.is_ge, fill=0.0, base=size - 1,
                                pattern=[[size, groups], [0, inner]],
                                channel_multiplier=-1).then_inc(pool_step, 1)
                pool.wait_ge(pool_step, n + 1)
                g.affine_select(out=v, in_=v, compare_op=ALU.is_ge, fill=0.0, base=0,
                                pattern=[[-size, groups], [-1 if name == "bdtri" else 0, inner]],
                                channel_multiplier=1).then_inc(consts, 1)
            pool.wait_ge(d_ready, 9)
            g.memset(qbd_flat, 0.0).then_inc(qbd_zeroed, 1)
            pool.wait_ge(y_ready, 1)
            g.memset(two["vis"], 0.0).then_inc(pool_step, 1)
            pool.wait_ge(pool_step, 4)
            g.affine_select(out=two["vis"], in_=two["vis"], compare_op=ALU.is_ge, fill=NEG, base=META,
                            pattern=[[-1, META + P]], channel_multiplier=1).then_inc(vis_ready, 1)
            pool.wait_ge(sigmoid_ready, 1)
            for n in range(C):
                tile_is_taken(pool, TILE0["w_conv_out_2"] + n)
                g.tensor_tensor(yco[:, n, :], yco[:, n, :], feat2[:, GB + n, META:],
                                ALU.mult).then_inc(conv_gated, 1)

        CONSTS = 12
        GLR_AFTER = 4

        @block.tensor
        def _(pe):
            mm = nc.tensor.matmul

            def norm(k, tokens):
                pe.wait_ge(folded, k + 1)
                mm(ps[:, norm_bank(k), 0:tokens], ones[:, 0:P], var[:, 0:tokens], start=True,
                   stop=True).then_inc(sum_ready, 1)

            def parts_ready(b, turn=0):
                pe.wait_ge(w_lo_ready, turn * RING + (b + 1))

            def column_block(b, g, tokens, turn=0, tile_turn=None, owed=False, operand=None):
                parts_ready(b, turn)
                bank_is_free(pe, g, tile_turn)
                k, (xh, xl), out = b % RING, x_parts[tokens], bank_of(g)[:, 0:tokens]
                products = [(c, part) for c in range(C) for part in ("hh", "hl")] + [(c, "lh") for c in range(C)]
                if operand is not None:
                    products = [(c, part) for part in ("hh", "lh", "hl") for c in range(C)]
                for n, (c, part) in enumerate(products):
                    w = w_lo if part == "lh" else w_hi
                    x = xl if part == "hl" else xh
                    if operand is not None and c % 4 == 0 and part != "lh":
                        pe.wait_ge(x_hi_ready if part == "hh" else x_lo_ready, 2 * operand + c // 4 + 1)
                    last = mm(out, w[:, k, c * P:(c + 1) * P], x[:, c, :], start=n == 0, stop=n == 3 * C - 1)
                    if n == 0 or n == 1 and owed:
                        last.then_inc(block_begun, 1)
                last.then_inc(tile_ready, 1)

            def columns(name, tokens, operand, owed=False):
                b0, g0, n = FIRST[name], TILE0[name], COUNT[name]
                looped = n // RING if n > 4 * RING else 0
                if looped:
                    for k in range(RING):
                        column_block(b0 + k, g0 + k, tokens, operand=operand if k == 0 else None)
                    with pe.Fori(1, looped) as i:
                        for k in range(RING):
                            column_block(b0 + k, g0 + k, tokens, i, i)
                for k in range(looped * RING, n):
                    column_block(b0 + k, g0 + k, tokens, owed=owed and k == 0, operand=operand if k == 0 else None)

            def value_blocks(name, between=None):
                xh, xl = x_parts[T]
                for n in range(COUNT[name] // 2):
                    b, g = FIRST[name] + 2 * n, TILE0[name] + 3 * n
                    k = b % RING
                    parts_ready(b + 1)
                    for j in range(3):
                        bank_is_free(pe, g + j)
                        out = bank_of(g + j)[:, 0:2 * COLS].rearrange("p (k n) -> p k n", k=2)
                        at = META + (j - 1) * P if j else 0
                        for c in range(C):
                            hi = w_hi[:, k:k + 2, c * P:(c + 1) * P]
                            lo = w_lo[:, k:k + 2, c * P:(c + 1) * P]
                            i = mm(out, xh[:, c, at:at + P], hi, start=c == 0, stop=False)
                            if c == j == 0:
                                i.then_inc(block_begun, 1)
                            i = mm(out, xh[:, c, at:at + P], lo, start=False, stop=False)
                            if c == j == 0 and n:
                                i.then_inc(block_begun, 1)
                            last = mm(out, xl[:, c, at:at + P], hi, start=False, stop=c == C - 1)
                        last.then_inc(tile_ready, 1)
                        if between is not None:
                            between(3 * n + j)

            pe.wait_ge(zeroed, 14)
            norm(0, T)
            pe.wait_ge(normed, 2)
            pe.wait_ge(small_landed, 16)
            xn = tokens_of(sq1, T)
            for n in range(16):
                column_block(n, n, T, operand=0 if n == 0 else None)
                if n == GLR_AFTER:
                    for c in range(C):
                        last = mm(ps[0:GLA_RANK, 6, 0:T], glr_w[:, c, :], xn[:, c, :], start=c == 0,
                                  stop=c == C - 1)
                    last.then_inc(glr_ready, 1)
            pe.wait_ge(consts, CONSTS)
            pe.wait_ge(glr_taken, 1)
            for j in range(2):
                last = mm(ps[:, 4 + j, 0:T], gate_up_w[0:GLA_RANK, j * P:(j + 1) * P],
                          one["glrT"][0:GLA_RANK, :], start=True, stop=True)
            last.then_inc(gate_logits_ready, 1)

            def meta_scores():
                pe.wait_ge(kbd_ready, 1)
                for p in range(4):
                    last = mm(ps[:, 4, 0:REAL], kbd[:, p, :], feat[:, p, META:], start=p == 0, stop=p == 3)
                last.then_inc(z0_ready, 1)

            def head_scores(h):
                rows = slice(64 * (h % 2), 64 * (h % 2) + 64)
                q, k = feat[rows, h // 2, :], feat[rows, 4 + h // 2, :]
                if h >= 2:
                    pe.wait_ge(z_taken, h - 1)
                z = ps[:, 5 + h % 2, :]
                mm(z[:, 0:2 * P], k[:, META:META + P], q[:, META:], start=True, stop=True)
                mm(z[:, 2 * P:W], k[:, META + P:], q[:, META + P:], start=True,
                   stop=True).then_inc(z_ready, 1)

            def suffix_sums(h):
                pe.wait_ge(sp_ready, h + 1)
                if h < 8:
                    if h:
                        pe.wait_ge(d_ready, h)
                    else:
                        pe.wait_ge(z0_taken, 1)
                    s = sp_[:, h % 2, :]
                    mm(ps[:, 7, 0:W], one["tri"], s, start=True, stop=True)
                    mm(ps[:, 7, P:2 * P], ones[:, 0:P], s[:, 2 * P:W], start=False, stop=True,
                       skip_group_check=True).then_inc(s_ready, 1)
                    at = P - META - META * h
                    mm(ps[:, 4, 0:2 * P], one["win"][:, at:at + P], s[:, 0:2 * P], start=h == 0, stop=False)
                    mm(ps[:, 4, P:2 * P], one["win"][:, at:at + P], s[:, 2 * P:W], start=False,
                       stop=False).then_inc(pe_used_sp, 1)
                else:
                    mm(ps[:, 4, 0:2 * P], one["bdtri"], sp_[:, 0, 0:2 * P], start=False,
                       stop=True).then_inc(s_ready, 1)

            def stick_breaking(step):
                if step == 0:
                    pe.wait_ge(gate_biased, 2)
                    tiles_are_taken(pe, TILE0["w_in_values"])
                    head_scores(0)
                    head_scores(1)
                elif step == 1:
                    meta_scores()
                elif step < 11:
                    suffix_sums(step - 2)
                    if step < 8:
                        head_scores(step)
                else:
                    pe.wait_ge(z_taken, 8)
                    tiles_are_taken(pe, TILE0["w_in_values"] + 6)
                    mm(ps[:, 6, :], one["rep"][0:META, :], vtok[0:META, 0, 0:512], start=True,
                       stop=True).then_inc(meta_values_ready, 1)

            value_blocks("w_in_values", stick_breaking)
            tiles_are_taken(pe, TILE0["w_out"])
            pe.wait_ge(a_ready, 9)
            pe.wait_ge(vbd_ready, 1)
            for h in range(8):
                o = ps[64 * (h % 2):64 * (h % 2) + 64, 2 + h // 4, 256 * (h // 2 % 2):256 * (h // 2 % 2) + 256]
                cols = slice(64 * h, 64 * h + 64)
                mm(o, vtok[:, 1, cols], zm[:, h, 0:2 * P], start=True, stop=False)
                mm(o[:, P:2 * P], vtok[:, 2, cols], zm[:, h, 2 * P:W], start=False, stop=False)
                last = mm(o, one["vbd"][:, cols], zm[:, 8, 0:2 * P], start=False, stop=True)
            last.then_inc(sb_out_ready, 1)
            pe.wait_ge(head_sq, 1)
            for j in range(2):
                last = mm(ps[:, 4 + j, :], one["blk64"], one["sqh"][:, 512 * j:512 * j + 512],
                          start=True, stop=True)
            last.then_inc(head_sum, 1)

            pe.wait_ge(q_decayed, 2)
            pe.wait_ge(head_logged, 1)
            for i in range(SUBS):
                for j in range(2):
                    n = 2 * i + j
                    pe.wait_ge(k_decayed, n + 1)
                    q, k = qbd[:, j, i, :, :], kt[:, n % KEY_BUFS, :]
                    cols = slice(2 * SUB * i, 2 * SUB * (i + 1))
                    mm(ps[:, 4 + j, cols], k[:, META:META + P], q, start=True, stop=True)
                    last = mm(ps[0:META, j, cols], k[:, 0:META], q, start=True, stop=True)
                    if i >= SUBS // 2:
                        at = 256 * j + 2 * SUB * (i - SUBS // 2)
                        last = mm(ps[:, 6, at:at + 2 * SUB], k[:, META + P:], q, start=True, stop=True)
                    last.then_inc(k_used, 1)
            pe.wait_ge(gla_masked, 4)
            pe.wait_ge(gla_meta_taken, 2)
            for h in range(GLA_HEADS):
                o = ps[:, h // 2, 256 * (h % 2):256 * (h % 2) + 256]
                cols = slice(512 + GLA_DV * h, 512 + GLA_DV * h + GLA_DV)
                mm(o, vtok[:, 1, cols], A[:, h, 0:2 * P], start=True, stop=False)
                mm(o[:, P:2 * P], vtok[:, 2, cols], A[:, h, 2 * P:W], start=False, stop=False)
                last = mm(o, vtok[0:META, 0, cols], A0[0:META, h, :], start=False, stop=True)
            last.then_inc(gla_out_ready, 1)
            pe.wait_ge(head_sq, 2)
            for j in range(2):
                last = mm(ps[:, 4 + j, :], ones[:, 0:P], one["sqh"][:, 512 * j:512 * j + 512],
                          start=True, stop=True)
            last.then_inc(head_sum, 1)

            pe.wait_ge(sb_mixed, 1)
            pe.wait_ge(gla_mixed, 1)
            columns("w_out", REAL, 1, owed=True)
            norm(1, REAL)
            columns("w_peer_q", REAL, 2)
            pe.wait_ge(keys_landed, 16)
            tiles_are_taken(pe, TILE0["expert_u"])
            for h in range(PH):
                if h >= 2:
                    pe.wait_ge(key_scores_taken, 2 * (h - 1))
                for half in range(2):
                    rows = slice(64 * half, 64 * half + 64)
                    for t in range(2):
                        last = mm(ps[:, 4 + 2 * (h % 2) + half, t * P:t * P + P], qp[rows, h, t * P:t * P + P],
                                  keys_w[rows, h, :], start=True, stop=True)
                    last.then_inc(key_scores_ready, 1)

            b0, g0 = FIRST["expert_u"], TILE0["expert_u"]

            def gate_tables(n, k, bank0):
                pe.wait_ge(onehots_ready, n + 1)
                for j in range(GROUP):
                    for part in range(3):
                        last = mm(ps[:, bank0 + k, HALF_KEYS * j:HALF_KEYS * (j + 1)], onehot2[:, k, :, j],
                                  onehot1[:, k, part, :, j], start=part == 0, stop=part == 2)
                last.then_inc(gates_ready, 1)

            with pe.Fori(0, 16) as i:
                for k in range(RING):
                    column_block(b0 + k, g0 + k, REAL, i, i)
            pe.wait_ge(routed, 1)
            for t in range(2):
                for j, name in enumerate(("gate", "i1", "i2")):
                    last = nc.tensor.transpose(ps[:, 4 + t, P * j:P * j + P],
                                               route[name][:, t * P:(t + 1) * P], ident[:, :])
            last.then_inc(slots_ready, 1)
            pe.wait_ge(slots_taken, 2)
            with pe.Fori(16, 32) as i:
                for k in range(RING):
                    column_block(b0 + k, g0 + k, REAL, i, i)
                    if k % 2:
                        gate_tables(i * 2 + (k // 2 - 32), k // 2, 4)

            tiles_are_taken(pe, TILE0["w_in_2_features"])
            pe.wait_ge(gates_applied, 32)

            def open_sums():
                for n in range(4):
                    mm(ps[:, 4 + n, :], zeros[:, :], res[:, 0:2, 0:REAL], start=True, stop=True)

            xh4, xl4 = x_hi[:, 0:RING * REAL], x_lo[:, 0:RING * REAL]

            def row_block(b, turn=0, n=0):
                parts_ready(b, turn)
                pe.wait_ge(x_lo_ready, turn * RING + (n + 1))
                k = b % RING
                xh, xl = xh4[:, k * REAL:(k + 1) * REAL], xl4[:, k * REAL:(k + 1) * REAL]
                for n, (w, x) in enumerate([(w_hi, xh), (w_hi, xl), (w_lo, xh)]):
                    for m in range(C):
                        i = mm(ps[:, 4 + m // 2, 256 * (m % 2):256 * (m % 2) + 256], w[:, k, m * P:(m + 1) * P],
                               x, start=False, stop=True, skip_group_check=True)
                        if n == m == 0:
                            i.then_inc(block_begun, 1)

            def close_sums():
                mm(ps[:, 7, 0:1], zeros[:, :], ones[:, 0:1], start=False, stop=True,
                   skip_group_check=True).then_inc(y_ready, 1)

            open_sums()
            b0 = FIRST["expert_v"]
            with pe.Fori(0, 16) as i:
                for k in range(RING):
                    row_block(b0 + k, i, ACTS0 + k)
                    if k % 2:
                        gate_tables(i * 2 + (32 + k // 2), k // 2, 0)
            with pe.Fori(16, 32) as i:
                for k in range(RING):
                    row_block(b0 + k, i, ACTS0 + k)
            close_sums()

            norm(2, REAL)
            norm(3, T)
            b0, g0 = FIRST["w_in_2_features"], TILE0["w_in_2_features"]
            for n in range(4):
                column_block(b0 + n, g0 + n, T, operand=X_MIX if n == 0 else None)
            xn = tokens_of(sq_late, T)
            pe.wait_ge(kiwi_landed, 16)
            for c in range(C):
                mm(ps[:, 4, 0:T], kiwi_w[:, c, 0:P], xn[:, c, :], start=c == 0, stop=c == C - 1)
            for t in range(2):
                for c in range(C):
                    last = mm(ps[:, 5, 8 * t:8 * t + 8], xn[:, c, META + P * t:META + P * t + P],
                              kiwi_w[:, c, P:P + IDX_HEADS], start=c == 0, stop=c == C - 1)
            last.then_inc(kiwi_ready, 1)
            for n in range(16):
                t, h = n // 8, n % 8
                if n % 2 == 0:
                    column_block(b0 + 4 + n // 2, g0 + 4 + n // 2, T)
                if n == 0:
                    tiles_are_taken(pe, g0 + 4)
                    pe.wait_ge(kiwi_taken, 2)
                elif n > 1:
                    pe.wait_ge(idx_taken, n - 1)
                seen = META + P * (t + 1)
                rows = slice(64 * (h % 2), 64 * (h % 2) + 64)
                mm(ps[:, 4 + n % 2, 0:seen], feat2[rows, QI + h // 2, META + P * t:META + P * t + P],
                   two["kidup"][rows, 0:seen], start=True, stop=True).then_inc(idx_ready, 1)
            with pe.Fori(3, 11) as i:
                for k in range(RING):
                    column_block(b0 + k, g0 + k, T, i, i)
            value_blocks("w_in_2_values")

            def attention_scores(n):
                t, h = n // 8, n % 8
                seen = META + P * (t + 1)
                if n:
                    pe.wait_ge(masked_ready, n)
                mm(ps[:, 4, 0:seen], feat2[:, QF + h, META + P * t:META + P * t + P],
                   feat2[:, KF + h, 0:seen], start=True, stop=True).then_inc(logits_ready, 1)

            def attention_turn(n):
                t = n // 8
                pe.wait_ge(probs_scaled, n + 1)
                if n:
                    pe.wait_ge(turned_taken, n)
                turned = ps[:, 5, :]
                p = pr[:, n % 2, :]
                last = nc.tensor.transpose(turned[0:META, 0:P], p[:, 0:META], ident[:, :])
                for c in range(t + 1):
                    last = nc.tensor.transpose(turned[:, P * (c + 1):P * (c + 2)],
                                               p[:, META + P * c:META + P * (c + 1)], ident[:, :])
                last.then_inc(probs_turned, 1)

            def attention_values(n):
                t, h = n // 8, n % 8
                pe.wait_ge(turned_taken, n + 1)
                if n >= 8 and n % 4 == 0:
                    pe.wait_ge(attn_taken, n // 4 - 1)
                o = ps[:, 6 + n // 4 % 2, P * (h % 4):P * (h % 4) + P]
                cols = slice(P * h, P * h + P)
                mm(o, v2[0:META, 0, cols], pT[0:META, n % 2, 0:P], start=True, stop=False)
                for c in range(t + 1):
                    last = mm(o, v2[:, 1 + c, cols], pT[:, n % 2, P * (c + 1):P * (c + 2)], start=False,
                              stop=c == t)
                last.then_inc(attn_ready, 1)

            b0, g0 = FIRST["w_in_2_gates"], TILE0["w_in_2_gates"]
            pe.wait_ge(idx_taken, 16)
            attention_scores(0)
            for n in range(18):
                if n < 16:
                    column_block(b0 + n, g0 + n, T, owed=n == 0)
                else:
                    column_block(FIRST["w_conv_out_2"] + n - 16, TILE0["w_conv_out_2"] + n - 16, REAL,
                                 operand=X_CONV if n == 16 else None)
                if n == 0:
                    tiles_are_taken(pe, g0)
                if n >= 2:
                    attention_values(n - 2)
                if 1 <= n < 17:
                    attention_turn(n - 1)
                if n < 15:
                    attention_scores(n + 1)
            for n in range(2, 8):
                column_block(FIRST["w_conv_out_2"] + n, TILE0["w_conv_out_2"] + n, REAL)
            columns("w_attn_out_2", REAL, X_ATTN)
            columns("w_out_2", REAL, X_MIXED)
            norm(4, REAL)
            columns("w_gate_up_2", REAL, X_FFN)
            open_sums()
            b0, turns = FIRST["w_down_2"], FF // RING
            with pe.Fori(0, turns) as i:
                for k in range(RING):
                    row_block(b0 + k, i, HIDDEN0 + k)
            for k in range(turns * RING, FF):
                row_block(b0 + k, 0, HIDDEN0 + k)
            close_sums()
            norm(5, REAL)

        @block.scalar
        def _(act):
            a = nc.scalar.activation
            steps = [0]

            def link(ins):
                steps[0] += 1
                ins.then_inc(act_step, 1)
                act.wait_ge(act_step, steps[0])


            def square(src, sq, piece):
                c = slice(2 * piece, 2 * piece + 2)
                a(sq[:, c, :], src[:, c, :], ACT.Square).then_inc(squares_ready, 1)

            def root(k):
                nc.scalar.preload_act_table_set("natural_log_exp_and_others")
                act.wait_ge(sum_ready, k + 1)
                n = T if k in (0, 3) else REAL
                link(a(rstd[:, 0:n], ps[:, norm_bank(k), 0:n], ACT.Ln, scale=1.0 / D, bias=eps[:, 0:1]))
                a(rstd[:, 0:n], rstd[:, 0:n], ACT.Exp, scale=-0.5).then_inc(root_ready, 1)

            def take(g, out, tokens, turn=0, rows=P):
                act.wait_ge(tile_ready, turn + g + 1)
                a(out, bank_of(g)[0:rows, 0:tokens], ACT.Copy).then_inc(tile_taken[g % BANKS], 1)

            def ahead(b, turn=None):
                split_hi(act, b + LEAD, turn)

            def value_tiles(name, out):
                for n in range(COUNT[name] // 2):
                    ahead(FIRST[name] + 2 * n)
                    ahead(FIRST[name] + 2 * n + 1)
                    for j in range(n % 2, 3, 2):
                        take(TILE0[name] + 3 * n + j, out[:, j, 2 * COLS * n:2 * COLS * (n + 1)], 2 * COLS)

            for piece in range(4):
                act.wait_ge(x_landed[piece], 16)
                square(res, tokens_of(sq1, T), piece)
            root(0)
            ahead(-2)
            ahead(-1)
            operand_hi(act, 0, tokens_of(sq1, T), normed, 1)
            for n in range(16):
                ahead(n)
                if n % 2 == 0:
                    take(n, feat[:, n, :], T)
                if n == GLR_AFTER:
                    act.wait_ge(glr_ready, 1)
                    a(one["glrT"][0:GLA_RANK, :], ps[0:GLA_RANK, 6, 0:T], ACT.Copy).then_inc(glr_taken, 1)
            tiles_are_taken(act, TILE0["w_in_values"])
            a(sil, feat[:, 12:16, META:], ACT.Silu).then_inc(silu_ready, 1)
            nc.scalar.preload_act_table_set("natural_log_exp_and_others")
            act.wait_ge(gate_biased, 2)
            link(a(gl, gx, ACT.Abs))
            link(a(gl, gl, ACT.Exp, scale=-1.0))
            a(gl, gl, ACT.Ln, bias=1.0).then_inc(gate_soft, 1)

            def softness(n, cols):
                if n < 8:
                    act.wait_ge(z_taken, n + 1)
                else:
                    act.wait_ge(z0_taken, 1)
                if n >= 2:
                    act.wait_ge(sp_ready, n - 1)
                s = soft[:, n % 2, 0:cols]
                link(a(s, zm[:, n, 0:cols], ACT.Abs))
                link(a(s, s, ACT.Exp, scale=-1.0))
                a(s, s, ACT.Ln, bias=1.0).then_inc(soft_ready, 1)

            def weights(n, cols):
                act.wait_ge(d_ready, n + 1)
                a(zm[:, n, 0:cols], zm[:, n, 0:cols], ACT.Exp).then_inc(a_ready, 1)

            for n in range(12):
                if n % 3 == 0:
                    ahead(FIRST["w_in_values"] + 2 * (n // 3))
                    ahead(FIRST["w_in_values"] + 2 * (n // 3) + 1)
                if n % 2 == 0:
                    cols = 2 * COLS * (n // 3)
                    take(TILE0["w_in_values"] + n, vtok[:, n % 3, cols:cols + 2 * COLS], 2 * COLS)
                if 1 <= n < 10:
                    softness(n - 1, W if n < 9 else REAL)
                if n >= 3:
                    weights(n - 3, W if n < 11 else REAL)

            def head_squares(banks, ready):
                act.wait_ge(ready, 1)
                a(one["sqh"].rearrange("p (b n) -> p b n", b=2), ps[:, banks:banks + 2, :],
                  ACT.Square).then_inc(head_sq, 1)

            def head_root(k, width):
                act.wait_ge(head_sum, k + 1)
                i = a(rh[:, k, :].rearrange("p (b n) -> p b n", b=2), ps[:, 4:6, :], ACT.Ln, scale=1.0 / width,
                      bias=eps[:, 0:1])
                i.then_inc(head_logged, 1)
                act.wait_ge(head_logged, k + 1)
                a(rh[:, k, :], rh[:, k, :], ACT.Exp, scale=-0.5).then_inc(head_rooted, 1)

            act.wait_ge(q_exp_in, 1)
            a(dq, dq, ACT.Exp).then_inc(q_exp, 1)
            head_squares(2, sb_out_ready)
            for n in range(2 * SUBS):
                i, j = n // 2, n % 2
                seen = META + P * (1 + (i >= SUBS // 2))
                mid = META + SUB * i + SUB // 2 - 1
                if n >= KEY_BUFS:
                    act.wait_ge(k_decayed, n - KEY_BUFS + 1)
                a(ke[:, n % KEY_BUFS, 0:seen], nb[:, j, 0:seen], ACT.Exp,
                  bias=bcum[:, j, mid:mid + 1]).then_inc(k_exp, 1)
                if n == KEY_BUFS - 1:
                    head_root(0, SB_DIM)
            act.wait_ge(sb_mixed, 1)
            operand_hi(act, 1, mix, None, 0, halves=(0,))
            act.wait_ge(k_used, 2 * SUBS)
            for j in range(2):
                a(A0[0:META, 2 * j:2 * j + 2, :].rearrange("p e (i s) -> p e i s", s=SUB),
                  ps[0:META, j, :].rearrange("p (i e s) -> p e i s", e=2, s=SUB),
                  ACT.Copy).then_inc(gla_meta_taken, 1)
            head_squares(0, gla_out_ready)
            head_root(1, GLA_DV)
            act.wait_ge(gla_mixed, 1)
            operand_hi(act, 1, mix, None, 0, halves=(1,))
            for n in range(8):
                ahead(FIRST["w_out"] + n)
                if n % 2:
                    tile_is_taken(act, TILE0["w_out"] + n - 1)
                    tile_is_taken(act, TILE0["w_out"] + n)
                    square(res[:, :, META:], tokens_of(sq1, REAL), n // 2)
            root(1)
            operand_hi(act, 2, tokens_of(sq1, REAL), normed, 3)
            for h in range(PH):
                ahead(FIRST["w_peer_q"] + h)
                take(TILE0["w_peer_q"] + h, qp[:, h, :], REAL)
            for n in range(2 * PH):
                h, half = n // 2, n % 2
                act.wait_ge(key_scores_ready, n + 1)
                a(sc[:, h:h + 9:8, half * P:half * P + P],
                  ps[:, 4 + 2 * (h % 2) + half, 0:2 * P].rearrange("p (t k) -> p t k", t=2),
                  ACT.Copy).then_inc(key_scores_taken, 1)

            b0, g0 = FIRST["expert_u"], TILE0["expert_u"]

            def experts(first, last):
                with act.Fori(first, last) as i:
                    for k in range(RING):
                        ahead(b0 + k, i)
                        act.wait_ge(tile_ready, i * RING + (g0 + k + 1))
                        a(act_store[:, i * RING + k, :], bank_of(g0 + k)[:, 0:REAL],
                          ACT.Gelu).then_inc(tile_taken[(g0 + k) % BANKS], 1)

            nc.scalar.preload_act_table_set("gelu_and_others")
            experts(0, 13)
            act.wait_ge(tops_shifted, 1)
            a(route["gate"], route["gate"], ACT.Exp).then_inc(tops_exp, 1)
            nc.scalar.preload_act_table_set("gelu_and_others")
            experts(13, 16)
            act.wait_ge(slots_ready, 1)
            a(gate_f.rearrange("p (t n) -> p t n", t=2), ps[:, 4:6, 0:P], ACT.Copy).then_inc(slots_taken, 1)
            a(slots[:, 3:5, :].rearrange("p j (t n) -> p t j n", t=2),
              ps[:, 4:6, P:3 * P].rearrange("p t (j n) -> p t j n", j=2), ACT.Copy).then_inc(slots_taken, 1)
            experts(16, 32)

            def row_operand(src, b, turn=None):
                ahead(b, turn)
                k = b % RING
                a(x_hi[:, k * REAL:(k + 1) * REAL], src, ACT.Copy).then_inc(x_hi_ready, 1)

            b0 = FIRST["expert_v"]
            for half in range(2):
                act.wait_ge(gates_applied, 32 * (half + 1))
                with act.Fori(16 * half, 16 * half + 16) as i:
                    for k in range(RING):
                        row_operand(act_store[:, i * RING + k, :], b0 + k, i)

            sq = tokens_of(sq_late, T)
            sq_r = tokens_of(sq_late, REAL)
            act.wait_ge(y_ready, 1)
            act.dma_start(two["ya"][:, 0:KIWI_COLS], kiwi_dram).then_inc(kiwi_landed, 16)
            for piece in range(4):
                act.wait_ge(residual, piece + 1)
                square(res[:, :, META:], sq_r, piece)
            root(2)
            for piece in range(4):
                act.wait_ge(normed, 2 * 2 + piece // 2 + 1)
                square(res, sq, piece)
            root(3)
            operand_hi(act, X_MIX, sq, normed, 2 * 3 + 1)
            b0, g0 = FIRST["w_in_2_features"], TILE0["w_in_2_features"]
            for n in range(4):
                ahead(b0 + n)
                take(g0 + n, feat2[:, n, :], T)
            ahead(b0 + 4)
            act.wait_ge(kiwi_ready, 1)
            a(two["kidup"], ps[:, 4, 0:T], ACT.Copy).then_inc(kiwi_taken, 1)
            a(two["wi"], ps[:, 5, 0:16], ACT.Copy, scale=IDX_SCALE).then_inc(kiwi_taken, 1)
            for n in range(4, 12):
                if n > 4:
                    ahead(b0 + n)
                take(g0 + n, feat2[:, n, :], T)
            with act.Fori(3, 11) as i:
                for k in range(RING):
                    ahead(b0 + k, i)
                    take(g0 + k, feat2[:, i * RING + k, :], T, i * RING)
            value_tiles("w_in_2_values", v2)
            stat = two["stat"]
            def probs(n):
                seen = META + P * (n // 8 + 1)
                act.wait_ge(masked_ready, n + 1)
                if n >= 2:
                    act.wait_ge(probs_turned, n - 1)
                a(pr[:, n % 2, 0:seen], lm[:, n % 2, 0:seen], ACT.Exp, bias=stat[:, 16 + n:17 + n],
                  accum_out=stat[:, 32 + n:33 + n]).then_inc(probs_ready, 1)

            def turned(n):
                t = n // 8
                act.wait_ge(probs_turned, n + 1)
                if n >= 2:
                    act.wait_ge(attn_ready, n - 1)
                link(a(pT[0:META, n % 2, 0:P], ps[0:META, 5, 0:P], ACT.Copy))
                end = P * (t + 2)
                a(pT[:, n % 2, P:end], ps[:, 5, P:end], ACT.Copy).then_inc(turned_taken, 1)

            def outputs(n):
                t, q = n // 2, n % 2
                act.wait_ge(attn_ready, 4 * (n + 1))
                a(ya[:, 4 * q:4 * q + 4, P * t:P * t + P],
                  ps[:, 6 + n % 2, :].rearrange("p (h m) -> p h m", h=4), ACT.Copy).then_inc(attn_taken, 1)

            for n in range(18):
                if n < 16:
                    ahead(FIRST["w_in_2_gates"] + n)
                else:
                    ahead(FIRST["w_conv_out_2"] + n - 16)
                if n < 16:
                    probs(n)
                    take(TILE0["w_in_2_gates"] + n, feat2[:, GA + n, :], T)
                if n == 15:
                    act.wait_ge(conv_ready, 1)
                    operand_hi(act, X_CONV, yc, None, 0)
                if n > 15:
                    take(TILE0["w_conv_out_2"] + n - 16, yco[:, n - 16, :], REAL)
                if 1 <= n < 17:
                    turned(n - 1)
                if n >= 2 and (n - 2) % 4 == 3:
                    outputs((n - 2) // 4)
            for n in range(2, 8):
                ahead(FIRST["w_conv_out_2"] + n)
                take(TILE0["w_conv_out_2"] + n, yco[:, n, :], REAL)
                if n == 2:
                    a(feat2[:, GA:GA + 16, :], feat2[:, GA:GA + 16, :], ACT.Sigmoid).then_inc(sigmoid_ready, 1)
            tiles_are_taken(act, TILE0["w_attn_out_2"])
            operand_hi(act, X_ATTN, ya, None, 0)
            for n in range(8):
                ahead(FIRST["w_attn_out_2"] + n)
            act.wait_ge(tile_ready, TILE0["w_out_2"])
            operand_hi(act, X_MIXED, ya, mixed_ready, 1)
            for n in range(8):
                ahead(FIRST["w_out_2"] + n)
                if n % 2:
                    tile_is_taken(act, TILE0["w_out_2"] + n - 1)
                    tile_is_taken(act, TILE0["w_out_2"] + n)
                    square(res[:, :, META:], sq_r, n // 2)
            root(4)
            operand_hi(act, X_FFN, tokens_of(sq_late, REAL), normed, 2 * 4 + 1)
            b0, g0 = FIRST["w_gate_up_2"], TILE0["w_gate_up_2"]

            def gate_tiles(turn=None):
                t = 0 if turn is None else turn
                for k in range(RING):
                    ahead(b0 + k, t)
                    if k < 2:
                        g = g0 + k
                        act.wait_ge(tile_ready, t * RING + (g + 1))
                        if turn is not None:
                            act.wait_ge(tile_taken[(g + 2) % BANKS], t + (g + 2) // BANKS)
                        a(sg[:, k, :], bank_of(g)[:, 0:REAL], ACT.Silu).then_inc(tile_taken[g % BANKS], 1)

            gate_tiles()
            with act.Fori(1, FF // 2) as i:
                gate_tiles(i)
            tiles_are_taken(act, g0 + 2 * FF)
            b0 = FIRST["w_down_2"]
            with act.Fori(0, FF // RING) as i:
                for k in range(RING):
                    row_operand(hidden[:, i * RING + k, :], b0 + k, i)
            for n in range(FF // RING * RING, FF):
                row_operand(hidden[:, n, :], b0 + n)
            for piece in range(4):
                act.wait_ge(residual, 4 + piece + 1)
                square(res[:, :, META:], sq_r, piece)
            root(5)

        @block.vector
        def _(dve):
            v = nc.vector
            steps = [0]

            def link(ins):
                steps[0] += 1
                ins.then_inc(vec_step, 1)
                dve.wait_ge(vec_step, steps[0])

            tt, ts, stt = v.tensor_tensor, v.tensor_scalar, v.scalar_tensor_tensor

            def fold(k, sq, piece):
                n = T if k in (0, 3) else REAL
                dve.wait_ge(squares_ready, 4 * k + piece + 1)
                if piece:
                    link(tt(sq[:, 0:2, :], sq[:, 0:2, :], sq[:, 2 * piece:2 * piece + 2, :], ALU.add))
                if piece == 3:
                    tt(var[:, 0:n], sq[:, 0, :], sq[:, 1, :], ALU.add).then_inc(folded, 1)
                    dve.wait_ge(folded, k + 1)

            def norm(k, src, gain, dst, sq=None):
                n = T if k in (0, 3) else REAL
                at = SMALL[gain][0]
                for piece in range(4):
                    if sq is not None:
                        fold(k, sq, piece)
                for half in range(2):
                    c = slice(4 * half, 4 * half + 4)
                    link(tt(dst[:, c, :], src[:, c, :], small[:, at + 4 * half:at + 4 * half + 4].unsqueeze(2)
                            .broadcast_to([P, 4, n]), ALU.mult))
                dve.wait_ge(root_ready, k + 1)
                for half in range(2):
                    c = slice(4 * half, 4 * half + 4)
                    tt(dst[:, c, :], dst[:, c, :], rstd[:, 0:n].unsqueeze(1).broadcast_to([P, 4, n]),
                       ALU.mult).then_inc(normed, 1)

            def take(g, out, tokens, turn=0, rows=P):
                dve.wait_ge(tile_ready, turn + g + 1)
                v.tensor_copy(out, bank_of(g)[0:rows, 0:tokens]).then_inc(tile_taken[g % BANKS], 1)

            def ahead(b, turn=None):
                split_lo(dve, b + LEAD, turn)

            def value_tiles(name, out):
                for n in range(COUNT[name] // 2):
                    ahead(FIRST[name] + 2 * n)
                    ahead(FIRST[name] + 2 * n + 1)
                    for j in range(1 - n % 2, 3, 2):
                        take(TILE0[name] + 3 * n + j, out[:, j, 2 * COLS * n:2 * COLS * (n + 1)], 2 * COLS)

            for piece in range(4):
                fold(0, tokens_of(sq1, T), piece)
            for piece in range(4):
                dve.wait_ge(x_landed[piece], 16)
            dve.wait_ge(small_landed, 16)
            norm(0, res, "norm1", tokens_of(sq1, T))
            ahead(-2)
            operand_lo(dve, 0, tokens_of(sq1, T))
            ahead(-1)
            for n in range(16):
                ahead(n)
                if n % 2:
                    take(n, feat[:, n, :], T)
            dve.wait_ge(gate_logits_ready, 1)
            bg = SMALL["b_gate"][0]
            for j in range(2):
                ts(gx[:, j, :], ps[:, 4 + j, 0:T], small[:, bg + j:bg + j + 1], None, ALU.add).then_inc(gate_biased, 1)
            tiles_are_taken(dve, 16)
            for h in range(8):
                rows = slice(64 * (h % 2), 64 * (h % 2) + 64)
                i = v.tensor_copy(kbd[rows, h // 2, META * h:META * h + META], feat[rows, 4 + h // 2, 0:META])
                link(i) if h < 7 else i.then_inc(kbd_ready, 1)
            def scaled(n):
                if n < 8:
                    dve.wait_ge(z_ready, n + 1)
                    stt(zm[:, n, :], ps[:, 5 + n % 2, 0:W], SB_DIM ** -0.5, one["hide"], ALU.mult,
                        ALU.add).then_inc(z_taken, 1)
                else:
                    dve.wait_ge(z0_ready, 1)
                    ts(zm[:, n, 0:REAL], ps[:, 4, 0:REAL], SB_DIM ** -0.5, None, ALU.mult).then_inc(z0_taken, 1)

            def softplus(n, cols):
                dve.wait_ge(soft_ready, n + 1)
                if n >= 2:
                    dve.wait_ge(pe_used_sp, n - 1)
                stt(sp_[:, n % 2, 0:cols], zm[:, n, 0:cols], 0.0, soft[:, n % 2, 0:cols], ALU.max,
                    ALU.add).then_inc(sp_ready, 1)

            def log_weight(n, cols):
                dve.wait_ge(s_ready, n + 1)
                bank = 4 if n == 8 else 7
                tt(zm[:, n, 0:cols], zm[:, n, 0:cols], ps[:, bank, 0:cols], ALU.subtract).then_inc(d_ready, 1)

            for n in range(12):
                if n % 3 == 0:
                    ahead(FIRST["w_in_values"] + 2 * (n // 3))
                    ahead(FIRST["w_in_values"] + 2 * (n // 3) + 1)
                if n % 2:
                    cols = 2 * COLS * (n // 3)
                    take(TILE0["w_in_values"] + n, vtok[:, n % 3, cols:cols + 2 * COLS], 2 * COLS)
                if n >= 2 and n < 11:
                    log_weight(n - 2, W if n < 10 else REAL)
                if 1 <= n < 10:
                    softplus(n - 1, W if n < 9 else REAL)
                if n == 0:
                    scaled(0)
                    scaled(1)
                elif n == 1:
                    scaled(8)
                elif n < 8:
                    scaled(n)
            dve.wait_ge(meta_values_ready, 1)
            tt(one["vbd"], ps[:, 6, :], one["bdm"], ALU.mult).then_inc(vbd_ready, 1)

            dve.wait_ge(gate_soft, 1)
            link(stt(gx, gx, 0.0, gl, ALU.min, ALU.subtract))
            for j in range(2):
                link(v.tensor_tensor_scan(gl[:, j, :], one["ones_t"], gx[:, j, :], 0.0, ALU.mult, ALU.add))
            link(ts(nb, gl, -1.0 / GLA_TAU, None, ALU.mult))
            link(ts(bcum, gl, 1.0 / GLA_TAU, None, ALU.mult))
            for j in range(2):
                grp = bcum[:, j, META:].rearrange("p (i s) -> p i s", s=SUB)
                link(tt(dq[:, j, :].rearrange("p (i s) -> p i s", s=SUB), grp,
                             grp[:, :, SUB // 2 - 1:SUB // 2].broadcast_to([P, SUBS, SUB]), ALU.subtract))
            ts(dq, dq, -CLAMP, CLAMP, ALU.max, ALU.min).then_inc(q_exp_in, 1)

            def sb_normed():
                dve.wait_ge(head_rooted, 1)
                at = SMALL["sb_norm"][0]
                for p in range(4):
                    i = stt(mix[:, p, :], ps[:, 2 + p // 2, 256 * (p % 2):256 * (p % 2) + 256],
                            small[:, at + p:at + p + 1], rh[:, 0, 256 * p:256 * p + 256], ALU.mult, ALU.mult)
                i.then_inc(sb_mixed, 1)

            dve.wait_ge(consts, 1)
            link(v.tensor_copy(iota_rows[:, :, :], iota[:, :].unsqueeze(2).broadcast_to([P, NKEYS, GROUP])))
            dve.wait_ge(q_exp, 1)
            dve.wait_ge(qbd_zeroed, 1)
            for e in range(2):
                rows = slice(64 * e, 64 * e + 64)
                stt(qbd[rows, :, :, e, :], feat[rows, 8:10, META:].rearrange("p j (i s) -> p j i s", s=SUB),
                    GLA_DK ** -0.5, dq[rows, :, :].rearrange("p j (i s) -> p j i s", s=SUB), ALU.mult,
                    ALU.mult).then_inc(q_decayed, 1)

            for n in range(2 * SUBS):
                i, j = n // 2, n % 2
                seen = META + P * (1 + (i >= SUBS // 2))
                dve.wait_ge(k_exp, n + 1)
                if n >= KEY_BUFS:
                    dve.wait_ge(k_used, n - KEY_BUFS + 1)
                stt(kt[:, n % KEY_BUFS, 0:seen], ke[:, n % KEY_BUFS, 0:seen], math.exp(CLAMP),
                    feat[:, 10 + j, 0:seen], ALU.min, ALU.mult).then_inc(k_decayed, 1)
                if n == 2 * KEY_BUFS:
                    sb_normed()
            dve.wait_ge(k_used, 2 * SUBS)
            for j in range(2):
                for cols, bank, at in ((slice(0, 2 * P), 4 + j, 0), (slice(2 * P, W), 6, 256 * j)):
                    n = cols.stop - cols.start
                    keep = one["keep"][:, cols].rearrange("p (i s) -> p i s", s=SUB)
                    tt(A[:, 2 * j:2 * j + 2, cols].rearrange("p e (i s) -> p e i s", s=SUB),
                       ps[:, bank, at:at + 2 * n].rearrange("p (i e s) -> p e i s", e=2, s=SUB),
                       keep.unsqueeze(1).broadcast_to([P, 2, n // SUB, SUB]), ALU.mult).then_inc(gla_masked, 1)
            operand_lo(dve, 1, mix, halves=(0,))
            at = SMALL["gla_norm"][0]
            dve.wait_ge(silu_ready, 1)
            dve.wait_ge(head_sq, 2)
            for h in range(4):
                i = stt(mix[:, 4 + h, :], ps[:, h // 2, 256 * (h % 2):256 * (h % 2) + 256],
                        small[:, at + h:at + h + 1], sil[:, h, :], ALU.mult, ALU.mult)
            link(i)
            dve.wait_ge(head_rooted, 2)
            tt(mix[:, 4:8, :], mix[:, 4:8, :], rh[:, 1, :].rearrange("p (h t) -> p h t", h=4),
               ALU.mult).then_inc(gla_mixed, 1)
            operand_lo(dve, 1, mix, halves=(1,))

            def add_tiles(name, norm_id, sq):
                for n in range(8):
                    ahead(FIRST[name] + n)
                    g = TILE0[name] + n
                    dve.wait_ge(tile_ready, g + 1)
                    tt(res[:, n, META:], res[:, n, META:], bank_of(g)[:, 0:REAL], ALU.add).then_inc(
                        tile_taken[g % BANKS], 1)
                    if n % 2 == 0 and n:
                        fold(norm_id, sq, n // 2 - 1)
                fold(norm_id, sq, 3)

            add_tiles("w_out", 1, tokens_of(sq1, REAL))
            norm(1, res[:, :, META:], "norm2", tokens_of(sq1, REAL))
            operand_lo(dve, 2, tokens_of(sq1, REAL))
            for n in range(8):
                ahead(FIRST["w_peer_q"] + n)

            R = route
            dve.wait_ge(key_scores_taken, 16)

            last_step = {}

            def best16(chains, after):
                for step in range(5):
                    for name, values, out, index in chains:
                        dve.wait_ge(vec_step, last_step[name])
                        if step == 0:
                            i = v.max(out[:, 0:8], values)
                        elif step == 1:
                            i = v.max_index(index[:, 0:8], out[:, 0:8], values)
                        elif step == 2:
                            i = v.match_replace(out=values, in_to_replace=out[:, 0:8], in_values=values,
                                                imm_value=TAKEN)
                        elif step == 3:
                            i = v.max(out[:, 8:16], values)
                        else:
                            i = v.max_index(index[:, 8:16], out[:, 8:16], values)
                        i.then_inc(vec_step, 1)
                        steps[0] += 1
                        last_step[name] = steps[0]
                    after(step)

            rows = {k: R[k].rearrange("p (c k) -> p c k", c=16) for k in ("tv", "pos", "ix")}
            cand = R["cand"][:, 0:TOPK + 8 * (TOPK - 1)]
            v1, v2_ = R["v"][:, 0:TOPK], R["v"][:, TOPK:2 * TOPK]
            b0 = FIRST["expert_u"]
            b = [b0]

            def next_block():
                ahead(b[0])
                b[0] += 1

            for name in ("first", "second", "sums"):
                last_step[name] = steps[0]
            for c in range(17):
                chains = []
                if c < 16:
                    index = rows["ix"][:, c, :].bitcast(U32)
                    chains += [("first", sc[:, c, 0:P], v1, index[:, 0:TOPK]),
                               ("second", sc[:, c, P:2 * P], v2_, index[:, TOPK:])]
                if c:
                    chains.append(("sums", cand, rows["tv"][:, c - 1, :],
                                   rows["pos"][:, c - 1, :].bitcast(U32)))

                def after(step):
                    if c < 16 and (step == 1 or step == 3 and c % 2):
                        next_block()

                best16(chains, after)
                if c < 16:
                    dve.wait_ge(vec_step, steps[0])
                    ts(cand[:, 0:TOPK], v2_, v1[:, 0:1], None, ALU.add)
                    tt(cand[:, TOPK:].rearrange("p (a b) -> p a b", b=8),
                       v1[:, 1:TOPK].unsqueeze(2).broadcast_to([P, TOPK - 1, 8]),
                       v2_[:, 0:8].unsqueeze(1).broadcast_to([P, TOPK - 1, 8]), ALU.add).then_inc(vec_step, 1)
                    steps[0] += 1
                    for name in ("first", "second", "sums"):
                        last_step[name] = steps[0]
                    next_block()
            dve.wait_ge(vec_step, steps[0])
            ixf = R["ixf"]
            link(v.tensor_copy(ixf, R["ix"].bitcast(U32)))

            tv = R["tv"].rearrange("p (c k) -> p c k", c=16)
            gate = R["gate"].rearrange("p (c k) -> p c k", c=16)
            tt(gate, tv, tv[:, :, 0:1].broadcast_to([P, 16, TOPK]), ALU.subtract).then_inc(tops_shifted, 1)
            pos, pi = R["pos"].bitcast(U32), R["pi"].bitcast(U32)
            next_block()
            link(ts(pi, pos, 3, None, ALU.logical_shift_right))
            link(v.tensor_copy(R["bf"], pi))
            link(ts(R["af"], R["bf"], -1.0, 0.0, ALU.add, ALU.max))
            link(ts(R["row1"], R["bf"], 1.0, 8.0, ALU.is_equal, ALU.mult))
            link(ts(pi, pos, 7, None, ALU.bitwise_and))
            next_block()
            link(v.tensor_copy(R["bf"], pi))
            link(tt(R["bf"], R["bf"], R["row1"], ALU.add))
            ix = ixf.rearrange("p (c h k) -> p c h k", c=16, h=2)
            for t in range(2):
                for half, (digit, out) in enumerate(((R["af"], R["i1"]), (R["bf"], R["i2"]))):
                    part = slice(SLOTS * t, SLOTS * t + SLOTS)
                    next_block()
                    eq = R["eq"].rearrange("p (s a) -> p s a", a=TOPK)
                    link(tt(eq, digit[:, part].unsqueeze(2).broadcast_to([P, SLOTS, TOPK]),
                                 iota[:, 0:TOPK].unsqueeze(1).broadcast_to([P, SLOTS, TOPK]), ALU.is_equal))
                    next_block()
                    eq4 = R["eq"].rearrange("p (c k a) -> p c k a", c=PH, a=TOPK)
                    link(tt(eq4, eq4, ix[:, PH * t:PH * t + PH, half, :].unsqueeze(2).broadcast_to(
                        [P, PH, TOPK, TOPK]), ALU.mult))
                    next_block()
                    link(v.tensor_reduce(out[:, part], eq, AX.X, ALU.add))
                    next_block()
            while b[0] < b0 + HALF_KEYS - 4:
                next_block()
            dve.wait_ge(tops_exp, 1)
            link(v.tensor_reduce(R["sum"], gate, AX.X, ALU.add))
            link(v.reciprocal(R["rsum"], R["sum"]))
            tt(gate, gate, R["rsum"].unsqueeze(2).broadcast_to([P, 16, TOPK]), ALU.mult).then_inc(routed, 1)

            while b[0] < b0 + HALF_KEYS:
                next_block()

            def onehots(n, k, tokens, half):
                first = iota_rows[:, HALF_KEYS * half:HALF_KEYS * (half + 1), :]

                def spread(row, width):
                    return slots[:, row, tokens].unsqueeze(1).broadcast_to([P, width, GROUP])

                matched = onehot1[:, k, 2, :, :]
                tt(matched, first, spread(3, HALF_KEYS), ALU.is_equal).then_inc(keys_matched, 1)
                tt(onehot2[:, k, :, :], iota_rows[:, :, :], spread(4, NKEYS), ALU.is_equal)
                dve.wait_ge(keys_matched, n + 1)
                for part in range(3):
                    i = tt(onehot1[:, k, part, :, :], matched, spread(part, HALF_KEYS), ALU.mult)
                i.then_inc(onehots_ready, 1)

            def apply_gates(n, k, tokens, half, bank0):
                dve.wait_ge(gates_ready, n + 1)
                h = act_store[:, HALF_KEYS * half:HALF_KEYS * (half + 1), tokens]
                g = ps[:, bank0 + k, :].rearrange("p (t i) -> p i t", t=GROUP)
                tt(h, h, g, ALU.mult).then_inc(gates_applied, 1)

            def row_operand(src, n, b, turn=None):
                k, t = b % RING, 0 if turn is None else turn
                dve.wait_ge(x_hi_ready, t * RING + (n + 1))
                part = slice(k * REAL, (k + 1) * REAL)
                tt(x_lo[:, part], src, x_hi[:, part].bitcast(F32), ALU.subtract).then_inc(x_lo_ready, 1)
                ahead(b, turn)

            dve.wait_ge(slots_taken, 2)
            link(v.tensor_copy(slots[:, 0, :], gate_f))
            link(tt(gate_rest, gate_f, slots[:, 0, :], ALU.subtract))
            link(v.tensor_copy(slots[:, 1, :], gate_rest))
            link(tt(gate_f, gate_rest, slots[:, 1, :], ALU.subtract))
            link(v.tensor_copy(slots[:, 2, :], gate_f))
            bv = FIRST["expert_v"]
            for half in range(2):
                n0, bank0 = 32 * half, 4 - 4 * half
                tiles_are_taken(dve, TILE0["expert_u"] + HALF_KEYS * (half + 1))

                def turn_of_four(turn):
                    t = 0 if turn is None else turn
                    for k in range(RING):
                        if half:
                            row_operand(act_store[:, t * RING + k, :], ACTS0 + k, bv + k, t)
                        else:
                            ahead(b0 + HALF_KEYS + k, t)
                        at = t * (2 * GROUP) + GROUP * (k // 2)
                        if k % 2 == 0:
                            onehots(t * 2 + (n0 + k // 2), k // 2, bass.ds(at, GROUP), half)
                        elif turn is not None or k > 1:
                            apply_gates(t * 2 + (n0 + k // 2 - 1), 1 - k // 2, bass.ds(at - GROUP, GROUP), half, bank0)

                turn_of_four(None)
                with dve.Fori(1, 16) as i:
                    turn_of_four(i)
                apply_gates(n0 + 31, 1, slice(REAL - GROUP, REAL), half, bank0)
            with dve.Fori(16, 32) as i:
                for k in range(RING):
                    row_operand(act_store[:, i * RING + k, :], ACTS0 + k, bv + k, i)

            def add_sums(n):
                dve.wait_ge(y_ready, n)
                for m in range(4):
                    r = res[:, 2 * m:2 * m + 2, META:]
                    tt(r, r, ps[:, 4 + m, :].rearrange("p (c t) -> p c t", c=2), ALU.add).then_inc(residual, 1)

            add_sums(1)
            link(v.tensor_copy(res[:, :, 0:META], meta_2))
            dve.wait_ge(residual, 4)
            norm(2, res[:, :, META:], "norm_f", res[:, :, META:], tokens_of(sq_late, REAL))
            norm(3, res, "norm_mix", tokens_of(sq_late, T), tokens_of(sq_late, T))
            operand_lo(dve, X_MIX, tokens_of(sq_late, T))
            b0, g0 = FIRST["w_in_2_features"], TILE0["w_in_2_features"]
            for n in range(5):
                ahead(b0 + n)
            dve.wait_ge(kiwi_taken, 2)
            dve.wait_ge(vis_ready, 1)
            for t in range(2):
                seen = META + P * (t + 1)
                for h in range(IDX_HEADS):
                    n = 8 * t + h
                    if n % 2 == 0 and n:
                        ahead(b0 + 4 + n // 2)
                    dve.wait_ge(idx_ready, n + 1)
                    out = score[:, t, 0:seen] if h == 0 else rel[:, n % 2, 0:seen]
                    ts(out, ps[:, 4 + n % 2, 0:seen], 0.0, two["wi"][:, n:n + 1], ALU.max,
                       ALU.mult).then_inc(idx_taken, 1)
                    dve.wait_ge(idx_taken, n + 1)
                    if h:
                        link(tt(score[:, t, 0:seen], score[:, t, 0:seen], out, ALU.add))
                part = score[:, t, P * t:seen]
                link(tt(part, part, two["vis"], ALU.add))
            top8 = two["top8"]
            b = b0 + 12
            for t in range(2):
                seen = META + P * (t + 1)
                s = score[:, t, 0:seen]
                for r in range(-(-KEEP // 8)):
                    ahead(b)
                    b += 1
                    link(v.max(top8[:, 0:8], s))
                    if 8 * (r + 1) > KEEP:
                        link(v.memset(top8[:, KEEP - 8 * r:8], TAKEN))
                    link(v.match_replace(out=s, in_to_replace=top8[:, 0:8], in_values=s, imm_value=TAKEN))
                link(ts(selb[:, t, 0:seen], s, TAKEN, NEG, ALU.not_equal, ALU.mult))
                part = selb[:, t, P * t:seen]
                link(tt(part, part, two["vis"], ALU.add))
            at = SMALL["conv"][0]
            u = feat2[:, CU:CU + 8, :]
            for c in range(C):
                ahead(b)
                b += 1
                if c == 0:
                    tiles_are_taken(dve, g0 + CB + 8)
                w = [small[:, at + C * k + c:at + C * k + c + 1] for k in range(CONV_K)]
                link(tt(u[:, c, :], u[:, c, :], feat2[:, CC + c, :], ALU.mult))
                link(ts(yc[:, c, :], u[:, c, META:], w[2], None, ALU.mult))
                for k in (1, 0):
                    off = META - (CONV_K - 1) + k
                    link(stt(yc[:, c, :], u[:, c, off:off + REAL], w[k], yc[:, c, :], ALU.mult, ALU.add))
                i = tt(yc[:, c, :], yc[:, c, :], feat2[:, CB + c, META:], ALU.mult)
                link(i) if c < C - 1 else i.then_inc(conv_ready, 1)
            for n in range(b, b0 + COUNT["w_in_2_features"]):
                ahead(n)
            value_tiles("w_in_2_values", v2)

            stat = two["stat"]
            def mask_logits(n):
                t = n // 8
                seen = META + P * (t + 1)
                dve.wait_ge(logits_ready, n + 1)
                if n >= 2:
                    dve.wait_ge(probs_ready, n - 1)
                m = lm[:, n % 2, 0:seen]
                link(stt(m, ps[:, 4, 0:seen], HEAD_DIM ** -0.5, selb[:, t, 0:seen], ALU.mult, ALU.add))
                link(v.tensor_reduce(stat[:, n:n + 1], m, AX.X, ALU.max))
                ts(stat[:, 16 + n:17 + n], stat[:, n:n + 1], -1.0, None, ALU.mult).then_inc(masked_ready, 1)

            def scale_probs(n):
                seen = META + P * (n // 8 + 1)
                dve.wait_ge(probs_ready, n + 1)
                link(v.reciprocal(stat[:, 48 + n:49 + n], stat[:, 32 + n:33 + n]))
                m = pr[:, n % 2, 0:seen]
                ts(m, m, stat[:, 48 + n:49 + n], None, ALU.mult).then_inc(probs_scaled, 1)

            mask_logits(0)
            for n in range(16):
                ahead(FIRST["w_in_2_gates"] + n)
                scale_probs(n)
                if n < 15:
                    mask_logits(n + 1)
            operand_lo(dve, X_CONV, yc)
            for n in range(8):
                ahead(FIRST["w_conv_out_2"] + n)
            operand_lo(dve, X_ATTN, ya)
            dve.wait_ge(sigmoid_ready, 1)
            for n in range(8):
                ahead(FIRST["w_attn_out_2"] + n)
                g = TILE0["w_attn_out_2"] + n
                dve.wait_ge(tile_ready, g + 1)
                gated = tt(yc[:, n, :], bank_of(g)[:, 0:REAL], feat2[:, GA + n, META:], ALU.mult)
                gated.then_inc(tile_taken[g % BANKS], 1)
                dve.wait_ge(tile_taken[g % BANKS], g // BANKS + 1)
                dve.wait_ge(conv_gated, n + 1)
                i = tt(ya[:, n, :], yc[:, n, :], yco[:, n, :], ALU.add)
                if n % 4 == 3:
                    i.then_inc(mixed_ready, 1)
            operand_lo(dve, X_MIXED, ya)
            add_tiles("w_out_2", 4, tokens_of(sq_late, REAL))
            norm(4, res[:, :, META:], "norm_ffn", tokens_of(sq_late, REAL))
            operand_lo(dve, X_FFN, tokens_of(sq_late, REAL))
            b0, g0 = FIRST["w_gate_up_2"], TILE0["w_gate_up_2"]
            with dve.Fori(0, FF // 2) as i:
                for k in range(RING):
                    ahead(b0 + k, i)
                    if k > 1:
                        g = g0 + k
                        dve.wait_ge(tile_taken[(g - 2) % BANKS], i + ((g - 2) // BANKS + 1))
                        dve.wait_ge(tile_ready, i * RING + (g + 1))
                        tt(hidden[:, i * 2 + (k - 2), :], bank_of(g)[:, 0:REAL], sg[:, k - 2, :],
                           ALU.mult).then_inc(tile_taken[g % BANKS], 1)
            b0 = FIRST["w_down_2"]
            with dve.Fori(0, FF // RING) as i:
                for k in range(RING):
                    row_operand(hidden[:, i * RING + k, :], HIDDEN0 + k, b0 + k, i)
            for n in range(FF // RING * RING, FF):
                row_operand(hidden[:, n, :], HIDDEN0 + n, b0 + n)
            add_sums(2)
            dve.wait_ge(residual, 8)
            norm(5, res[:, :, META:], "norm_final", outT, tokens_of(sq_late, REAL))


def columns_to_blocks(w):
    n = w.shape[1]
    return w.reshape(C, P, n // COLS, COLS).transpose(2, 1, 0, 3).reshape(n // COLS, P, BLOCK)


def rows_to_blocks(w):
    return w.reshape(-1, P, BLOCK)


def kernel(**inputs):
    import concourse.bacc as bacc
    from concourse.bass_utils import run_bass_kernel_spmd

    a = {k: np.asarray(v) for k, v in inputs.items()}
    w1, w2 = a["w_in"][0], a["w_in_2"][0]
    o1 = np.cumsum([0, 512, 512, 512, 256, 256, 512, 512, 16])
    o2 = np.cumsum([0, 1024, 1024, 1024, 512, 64, 8, 1024, 1024, 1024, 1024, 1024])

    def cut(w, o, *ids):
        return np.concatenate([w[:, o[i]:o[i + 1]] for i in ids], axis=1)

    gate = a["w_gate_2"][0].reshape(D, FF // 2, 1, 2 * COLS)
    up = a["w_up_2"][0].reshape(D, FF // 2, 1, 2 * COLS)
    gate_up = np.concatenate([gate, up], axis=2).reshape(D, 2 * D_FF)
    stream = np.concatenate([
        columns_to_blocks(cut(w1, o1, 0, 1, 3, 4, 6)),
        columns_to_blocks(cut(w1, o1, 2, 5)),
        columns_to_blocks(a["w_out"][0]),
        columns_to_blocks(a["w_peer_q"][0]),
        columns_to_blocks(a["expert_u"][0].T),
        rows_to_blocks(a["expert_v"][0]),
        columns_to_blocks(cut(w2, o2, 3, 6, 8, 7, 1, 0)),
        columns_to_blocks(cut(w2, o2, 2)),
        columns_to_blocks(cut(w2, o2, 9, 10)),
        columns_to_blocks(a["w_conv_out_2"][0]),
        columns_to_blocks(a["w_attn_out_2"][0]),
        columns_to_blocks(a["w_out_2"][0]),
        columns_to_blocks(gate_up),
        rows_to_blocks(a["w_down_2"][0]),
    ], axis=0)
    assert stream.shape == (BLOCKS, P, BLOCK)

    def features(w):
        return w.reshape(C, P, -1).transpose(1, 0, 2).reshape(P, -1)

    ki, wi = cut(w2, o2, 4), cut(w2, o2, 5)
    keys = np.concatenate([a["sub_keys1"][0].transpose(2, 0, 1), a["sub_keys2"][0].transpose(2, 0, 1)])
    parts = {
        "glr": features(cut(w1, o1, 7)), "meta_2": features(a["meta_tokens_2"].T),
        "gate_up": np.concatenate([a["w_gate_up"][0]] * (P // GLA_RANK)),
        "norm1": features(a["norm1_g"][0]), "norm2": features(a["norm2_g"][0]),
        "norm_f": features(a["norm_f_g"]), "norm_mix": features(a["norm_mix_g_2"][0]),
        "norm_ffn": features(a["norm_ffn_g_2"][0]), "norm_final": features(a["norm_final_g_2"]),
        "sb_norm": a["sb_norm_g"][0].reshape(4, P).T, "gla_norm": a["gla_norm_g"][0].reshape(4, P).T,
        "b_gate": a["b_gate_up"][0].reshape(2, P).T,
        "conv": a["conv_w_2"][0].reshape(CONV_K * C, P).T,
    }
    small = np.concatenate([parts[k].reshape(P, n) for k, (_, n) in SMALL.items()], axis=1)
    tokens = np.concatenate([a["meta_tokens"], a["x"][0]])
    arrays = {"stream": stream, "small": np.ascontiguousarray(small),
              "keys": np.ascontiguousarray(keys.reshape(P, -1)),
              "kiwi": np.ascontiguousarray(features(np.concatenate([ki, ki, wi], axis=1))),
              "tokens": np.ascontiguousarray(features(tokens.T))}

    nc = bacc.Bacc("TRN2", target_bir_lowering=False, num_devices=1,
                   dynamic_dma_scratch_size=1024)
    dram = {k: nc.dram_tensor(f"in_{k}", v.shape, F32, kind="ExternalInput").ap() for k, v in arrays.items()}
    out = nc.dram_tensor("out_dram", (P, C * REAL), F32, kind="ExternalOutput").ap()
    build(nc, dram["stream"], dram["small"], dram["keys"], dram["kiwi"], dram["tokens"], out)
    r = run_bass_kernel_spmd(nc, [{f"in_{k}": v for k, v in arrays.items()}], core_ids=[0])
    got = r.results[0]["out_dram"]
    return np.ascontiguousarray(got.reshape(P, C, REAL).transpose(2, 1, 0)).reshape(1, REAL, D)
```
